# Optimizing a Trainium2 kernel written in Bass

```python
import jax, jax.numpy as jnp
from jax import lax
import numpy as np

D_MODEL = 1024
BATCH = 1
SEQ = 512
DEPTH = 1
DEC_BATCH = 8
DEC_SEQ = 1
PAST_LEN = 4096
PAGE_SIZE = 128

N_META = 16
EPS = 1e-6
SSD_D_INNER = 2 * D_MODEL
SSD_HEAD_DIM = 64
SSD_HEADS = SSD_D_INNER // SSD_HEAD_DIM
SSD_GROUPS = 4
SSD_D_STATE = 128
SSD_CONV = 4
SSD_CHUNK = 128
SSD_CONV_DIM = SSD_D_INNER + 2 * SSD_GROUPS * SSD_D_STATE
GLA_HEADS = 4
GLA_KEY_DIM = D_MODEL // 2
GLA_VAL_DIM = D_MODEL
GLA_DK = GLA_KEY_DIM // GLA_HEADS
GLA_DV = GLA_VAL_DIM // GLA_HEADS
GLA_GATE_RANK = 16
GLA_GATE_NORMALIZER = 16.0
GLA_CHUNK = 64
PEER_HEADS = 8
PEER_N_KEYS = 128
PEER_N_EXPERTS = PEER_N_KEYS * PEER_N_KEYS
PEER_DQ = 256
PEER_TOPK = 16
PEER_BLOCK = 256
IN_SIZES = (SSD_D_INNER, SSD_CONV_DIM, SSD_HEADS, GLA_KEY_DIM, GLA_KEY_DIM, GLA_VAL_DIM, GLA_VAL_DIM, GLA_GATE_RANK, 2 * D_MODEL)
IN_DIM = sum(IN_SIZES)

kernel_name = 'hybrid_ssd_gla_peer_step'

def rms(x):
    x32 = x.astype(jnp.float32)
    return x32 * lax.rsqrt(jnp.mean(x32 * x32, axis=-1, keepdims=True) + EPS)

def rmsnorm(x, w):
    return rms(x).astype(x.dtype) * w

def pad_chunks(t, front, chunk):
    back = (-(front + t.shape[1])) % chunk
    widths = [(0, 0)] * t.ndim
    widths[1] = (front, back)
    return jnp.pad(t, widths)

def ssd_chunked(xh, dt, a, bm, cm, s0, front):
    b, l = xh.shape[:2]
    q = SSD_CHUNK
    hpg = SSD_HEADS // SSD_GROUPS
    xh, dt, bm, cm = [pad_chunks(t, front, q) for t in (xh, dt, bm, cm)]
    nc = xh.shape[1] // q
    x = xh.reshape(b, nc, q, SSD_GROUPS, hpg, SSD_HEAD_DIM)
    dt = dt.reshape(b, nc, q, SSD_GROUPS, hpg)
    bm = bm.reshape(b, nc, q, SSD_GROUPS, SSD_D_STATE)
    cm = cm.reshape(b, nc, q, SSD_GROUPS, SSD_D_STATE)
    acum = jnp.cumsum(dt * a.reshape(SSD_GROUPS, hpg), axis=2)
    causal = jnp.tril(jnp.ones((q, q), dtype=bool))[:, :, None, None]
    seg = jnp.exp(jnp.where(causal, acum[:, :, :, None] - acum[:, :, None], -jnp.inf))
    xdt = x * dt[..., None]
    cb = jnp.einsum('bctgn,bcsgn->bctsg', cm, bm)
    y_diag = jnp.einsum('bctsg,bctsgh,bcsghp->bctghp', cb, seg, xdt)
    decay_to_end = jnp.exp(acum[:, :, -1:] - acum)
    chunk_states = jnp.einsum('bcsgn,bcsgh,bcsghp->bcghpn', bm, decay_to_end, xdt)
    chunk_decay = jnp.exp(acum[:, :, -1])

    def step(s, inp):
        cs, cd = inp
        return cd[..., None, None] * s + cs, s

    s_fin, s_in = lax.scan(step, s0.reshape(b, SSD_GROUPS, hpg, SSD_HEAD_DIM, SSD_D_STATE),
                           (jnp.moveaxis(chunk_states, 1, 0), jnp.moveaxis(chunk_decay, 1, 0)))
    s_in = jnp.moveaxis(s_in, 0, 1)
    y_off = jnp.einsum('bctgn,bcghpn,bctgh->bctghp', cm, s_in, jnp.exp(acum))
    y = (y_diag + y_off).reshape(b, nc * q, SSD_HEADS, SSD_HEAD_DIM)[:, front:front + l]
    return y, s_fin.reshape(b, SSD_HEADS, SSD_HEAD_DIM, SSD_D_STATE)

def gla_chunked(qh, kh, vh, gk, s0, front):
    b, l = qh.shape[:2]
    q = GLA_CHUNK
    qh, kh, vh, gk = [pad_chunks(t, front, q) for t in (qh, kh, vh, gk)]
    nc = qh.shape[1] // q
    qh = qh.reshape(b, nc, q, GLA_HEADS, GLA_DK)
    kh = kh.reshape(b, nc, q, GLA_HEADS, GLA_DK)
    vh = vh.reshape(b, nc, q, GLA_HEADS, GLA_DV)
    bcum = jnp.cumsum(gk.reshape(b, nc, q, GLA_HEADS, GLA_DK), axis=2)
    qe = qh * jnp.exp(bcum) * (GLA_DK ** -0.5)
    ke = kh * jnp.exp(-bcum)
    kend = kh * jnp.exp(bcum[:, :, -1:] - bcum)
    causal = jnp.tril(jnp.ones((q, q), dtype=bool))
    att = jnp.where(causal, jnp.einsum('bcthk,bcshk->bchts', qe, ke), 0.0)
    o_intra = jnp.einsum('bchts,bcshv->bcthv', att, vh)
    chunk_states = jnp.einsum('bcshk,bcshv->bchkv', kend, vh)
    chunk_decay = jnp.exp(bcum[:, :, -1])

    def step(s, inp):
        cs, cd = inp
        return cd[..., None] * s + cs, s

    s_fin, s_in = lax.scan(step, s0, (jnp.moveaxis(chunk_states, 1, 0), jnp.moveaxis(chunk_decay, 1, 0)))
    s_in = jnp.moveaxis(s_in, 0, 1)
    o = o_intra + jnp.einsum('bcthk,bchkv->bcthv', qe, s_in)
    return o.reshape(b, nc * q, GLA_HEADS, GLA_DV)[:, front:front + l], s_fin

def peer(xn, w_q, sub_keys, expert_u, expert_v):
    t_all = xn.shape[0]
    pad = (-t_all) % PEER_BLOCK
    blocks = jnp.pad(xn, ((0, pad), (0, 0))).reshape(-1, PEER_BLOCK, D_MODEL)

    def block(xb):
        qh = (xb @ w_q).reshape(PEER_BLOCK, PEER_HEADS, 2, PEER_DQ // 2)
        scores = jnp.einsum('thcd,chkd->thck', qh, sub_keys).astype(jnp.float32)
        sv, si = lax.top_k(scores, PEER_TOPK)
        cand = (sv[:, :, 0, :, None] + sv[:, :, 1, None, :]).reshape(PEER_BLOCK, PEER_HEADS, -1)
        cidx = (si[:, :, 0, :, None] * PEER_N_KEYS + si[:, :, 1, None, :]).reshape(PEER_BLOCK, PEER_HEADS, -1)
        best, pos = lax.top_k(cand, PEER_TOPK)
        idx = jnp.take_along_axis(cidx, pos, axis=-1)
        gate = jax.nn.softmax(best, axis=-1).astype(xb.dtype)
        hid = jax.nn.gelu(jnp.einsum('thkd,td->thk', expert_u[idx], xb), approximate=False)
        return jnp.einsum('thk,thkd->td', gate * hid, expert_v[idx])

    return lax.map(block, blocks).reshape(-1, D_MODEL)[:t_all]

def hybrid_layer(x, ssd_s, conv_s, gla_s, start, norm1_w, w_in, conv_w, conv_b, dt_bias, a_log, d_skip,
                 ssd_norm_w, w_ssd_out, gla_gate_up, gla_gate_b, gla_norm_w, w_gla_out, w_out,
                 norm2_w, peer_w_q, peer_sub_keys, peer_u, peer_v):
    b, l, _ = x.shape
    xn = rmsnorm(x, norm1_w)
    splits = np.cumsum(IN_SIZES)[:-1].tolist()
    z, xbc, dt_raw, q, k, v, g, g_lr, merge = jnp.split(xn @ w_in, splits, axis=-1)
    hist = jnp.concatenate([conv_s.astype(xbc.dtype), xbc], axis=1)
    conv = conv_b
    for j in range(SSD_CONV):
        conv = conv + conv_w[j] * hist[:, j:j + l]
    xbc_c = jax.nn.silu(conv)
    xs, bs, cs = jnp.split(xbc_c, [SSD_D_INNER, SSD_D_INNER + SSD_GROUPS * SSD_D_STATE], axis=-1)
    dt = jax.nn.softplus((dt_raw + dt_bias).astype(jnp.float32))
    a = -jnp.exp(a_log.astype(jnp.float32))
    xh = xs.reshape(b, l, SSD_HEADS, SSD_HEAD_DIM).astype(jnp.float32)
    y, ssd_new = ssd_chunked(xh, dt, a,
                             bs.reshape(b, l, SSD_GROUPS, SSD_D_STATE).astype(jnp.float32),
                             cs.reshape(b, l, SSD_GROUPS, SSD_D_STATE).astype(jnp.float32),
                             ssd_s.astype(jnp.float32), start % SSD_CHUNK)
    y = (y + d_skip[:, None] * xh).reshape(b, l, SSD_D_INNER) * jax.nn.silu(z.astype(jnp.float32))
    y = rms(y.reshape(b, l, SSD_GROUPS, -1)).reshape(b, l, SSD_D_INNER) * ssd_norm_w
    y_ssd = y.astype(x.dtype) @ w_ssd_out
    gk = jax.nn.log_sigmoid((g_lr @ gla_gate_up + gla_gate_b).astype(jnp.float32)) / GLA_GATE_NORMALIZER
    o, gla_new = gla_chunked(q.reshape(b, l, GLA_HEADS, GLA_DK).astype(jnp.float32),
                             k.reshape(b, l, GLA_HEADS, GLA_DK).astype(jnp.float32),
                             v.reshape(b, l, GLA_HEADS, GLA_DV).astype(jnp.float32),
                             gk.reshape(b, l, GLA_HEADS, GLA_DK), gla_s.astype(jnp.float32), start % GLA_CHUNK)
    o = rms(o) * gla_norm_w * jax.nn.silu(g.reshape(b, l, GLA_HEADS, GLA_DV).astype(jnp.float32))
    y_gla = o.reshape(b, l, GLA_VAL_DIM).astype(x.dtype) @ w_gla_out
    gate_ssd, gate_gla = jnp.split(jax.nn.sigmoid(merge), 2, axis=-1)
    x = x + (gate_ssd * y_ssd + gate_gla * y_gla) @ w_out
    hn = rmsnorm(x, norm2_w).reshape(b * l, D_MODEL)
    x = x + peer(hn, peer_w_q, peer_sub_keys, peer_u, peer_v).reshape(b, l, D_MODEL)
    new_conv = hist[:, -(SSD_CONV - 1):]
    return x, ssd_new.astype(ssd_s.dtype), new_conv.astype(conv_s.dtype), gla_new.astype(gla_s.dtype)

def setup_inputs(seed: int = 0) -> dict:
    key = jax.random.key(seed)
    ks = jax.random.split(key, 32)

    def nrm(k, shape, scale):
        return jax.random.normal(k, shape, jnp.float32) * scale

    dt0 = jnp.exp(jax.random.uniform(ks[8], (DEPTH, SSD_HEADS), jnp.float32, np.log(1e-3), np.log(1e-1)))
    return {
        'x_prompt': nrm(ks[0], (BATCH, SEQ, D_MODEL), 1.0),
        'x_sample': nrm(ks[1], (DEC_BATCH, DEC_SEQ, D_MODEL), 1.0),
        'state_ssd': nrm(ks[2], (DEPTH, DEC_BATCH, SSD_HEADS, SSD_HEAD_DIM, SSD_D_STATE), 0.1),
        'state_conv': nrm(ks[3], (DEPTH, DEC_BATCH, SSD_CONV - 1, SSD_CONV_DIM), 1.0),
        'state_gla': nrm(ks[4], (DEPTH, DEC_BATCH, GLA_HEADS, GLA_DK, GLA_DV), 1.0),
        'meta_tokens': nrm(ks[5], (N_META, D_MODEL), 1.0),
        'norm1_w': 1.0 + nrm(ks[6], (DEPTH, D_MODEL), 0.02),
        'w_in': nrm(ks[7], (DEPTH, D_MODEL, IN_DIM), D_MODEL ** -0.5),
        'conv_w': nrm(ks[9], (DEPTH, SSD_CONV, SSD_CONV_DIM), SSD_CONV ** -0.5),
        'conv_b': nrm(ks[10], (DEPTH, SSD_CONV_DIM), 0.02),
        'dt_bias': dt0 + jnp.log(-jnp.expm1(-dt0)),
        'a_log': jnp.log(jax.random.uniform(ks[11], (DEPTH, SSD_HEADS), jnp.float32, 1.0, 16.0)),
        'd_skip': 1.0 + nrm(ks[12], (DEPTH, SSD_HEADS), 0.02),
        'ssd_norm_w': 1.0 + nrm(ks[13], (DEPTH, SSD_D_INNER), 0.02),
        'w_ssd_out': nrm(ks[14], (DEPTH, SSD_D_INNER, D_MODEL), SSD_D_INNER ** -0.5),
        'gla_gate_up': nrm(ks[15], (DEPTH, GLA_GATE_RANK, GLA_KEY_DIM), GLA_GATE_RANK ** -0.5),
        'gla_gate_b': nrm(ks[16], (DEPTH, GLA_KEY_DIM), 0.02),
        'gla_norm_w': 1.0 + nrm(ks[17], (DEPTH, GLA_DV), 0.02),
        'w_gla_out': nrm(ks[18], (DEPTH, GLA_VAL_DIM, D_MODEL), GLA_VAL_DIM ** -0.5),
        'w_out': nrm(ks[19], (DEPTH, D_MODEL, D_MODEL), D_MODEL ** -0.5),
        'norm2_w': 1.0 + nrm(ks[20], (DEPTH, D_MODEL), 0.02),
        'peer_w_q': nrm(ks[21], (DEPTH, D_MODEL, PEER_HEADS * PEER_DQ), D_MODEL ** -0.5),
        'peer_sub_keys': nrm(ks[22], (DEPTH, 2, PEER_HEADS, PEER_N_KEYS, PEER_DQ // 2), (PEER_DQ // 2) ** -0.5),
        'peer_u': nrm(ks[23], (DEPTH, PEER_N_EXPERTS, D_MODEL), D_MODEL ** -0.5),
        'peer_v': nrm(ks[24], (DEPTH, PEER_N_EXPERTS, D_MODEL), PEER_HEADS ** -0.5),
        'final_norm_w': 1.0 + nrm(ks[25], (D_MODEL,), 0.02),
    }

def reference(x_prompt, x_sample, state_ssd, state_conv, state_gla, meta_tokens, norm1_w, w_in, conv_w,
              conv_b, dt_bias, a_log, d_skip, ssd_norm_w, w_ssd_out, gla_gate_up, gla_gate_b, gla_norm_w,
              w_gla_out, w_out, norm2_w, peer_w_q, peer_sub_keys, peer_u, peer_v, final_norm_w):
    layer_w = (norm1_w, w_in, conv_w, conv_b, dt_bias, a_log, d_skip, ssd_norm_w, w_ssd_out, gla_gate_up,
               gla_gate_b, gla_norm_w, w_gla_out, w_out, norm2_w, peer_w_q, peer_sub_keys, peer_u, peer_v)

    def run(x, s_ssd, s_conv, s_gla, start):
        new_ssd, new_conv, new_gla = [], [], []
        for i in range(DEPTH):
            x, s1, s2, s3 = hybrid_layer(x, s_ssd[i], s_conv[i], s_gla[i], start, *[w[i] for w in layer_w])
            new_ssd.append(s1)
            new_conv.append(s2)
            new_gla.append(s3)
        return rmsnorm(x, final_norm_w), jnp.stack(new_ssd), jnp.stack(new_conv), jnp.stack(new_gla)

    b = x_prompt.shape[0]
    dt = x_prompt.dtype
    meta = jnp.broadcast_to(meta_tokens.astype(dt)[None], (b, N_META, D_MODEL))
    xp = jnp.concatenate([meta, x_prompt], axis=1)
    z_ssd = jnp.zeros((DEPTH, b, SSD_HEADS, SSD_HEAD_DIM, SSD_D_STATE), dt)
    z_conv = jnp.zeros((DEPTH, b, SSD_CONV - 1, SSD_CONV_DIM), dt)
    z_gla = jnp.zeros((DEPTH, b, GLA_HEADS, GLA_DK, GLA_DV), dt)
    yp, p_ssd, p_conv, p_gla = run(xp, z_ssd, z_conv, z_gla, -N_META)
    ys, s_ssd, s_conv, s_gla = run(x_sample, state_ssd, state_conv, state_gla, PAST_LEN)
    return (yp[:, N_META:], ys, p_ssd, p_conv, p_gla, s_ssd, s_conv, s_gla)


_drawn_inputs = setup_inputs


def setup_inputs(seed=0):
    import zlib

    import numpy as np

    out = dict(_drawn_inputs(seed))
    spreads = {}
    factors = {'d_skip': 82.123,
     'ssd_norm_w': 33.428,
     'gla_gate_b': 6.448,
     'gla_norm_w': 61.617,
     'final_norm_w': 21.024,
     'norm2_w': 18.92}
    for name, (base, spread) in spreads.items():
        noise = np.random.default_rng([zlib.crc32(name.encode()), seed]).standard_normal(out[name].shape)
        drawn = base * np.exp(spread * noise) if base else spread * noise
        out[name] = __import__('jax').numpy.asarray(drawn.astype(out[name].dtype))
    for name, factor in factors.items():
        out[name] = (out[name] * factor).astype(out[name].dtype)
    return out
```

```python
import concourse.bass as bass
from concourse import mybir
from concourse.alu_op_type import AluOpType as ALU
from contextlib import ExitStack
import numpy as np

ACT = mybir.ActivationFunctionType
AX = mybir.AxisListType
F32 = mybir.dt.float32
BF16 = mybir.dt.bfloat16
I32 = mybir.dt.int32
U32 = mybir.dt.uint32

P = 128
D = 1024
KD = D // P
SEQ, NMETA, NSAMP = 512, 16, 8
TILES = SEQ // P
META0 = 32
SM = META0 + NMETA
COLS = SM + SEQ
EPS = 1e-6
GROUPS, HPG, HEAD = 4, 8, 64
HEADS = GROUPS * HPG
GW = HPG * HEAD
CT = GW // P + 2
B_TILE, C_TILE = CT - 2, CT - 1
CONV = 4
HIST = CONV - 1
RAW = HIST + NMETA + SEQ
CONVD = NMETA + SEQ
GH, DK, DV = 4, 128, 256
GCH = 64
RANK = 16
EH, NKEYS, TOPK = 8, 128, 16
ROW = 2 * D


def tile_cols(c):
    return slice(SM + c * P, SM + (c + 1) * P)


BLOCKS = ([("ssd", g) for g in range(GROUPS)] + [("gla", h) for h in range(GH)]
          + [("z", g) for g in range(GROUPS)] + [("g", i) for i in range(2)]
          + [("merge", j) for j in range(KD)] + [("out", i) for i in range(2)]
          + [("query", i) for i in range(4)])
FIRST = {kind: next(i for i, x in enumerate(BLOCKS) if x[0] == kind)
         for kind in ("ssd", "gla", "z", "g", "merge", "out", "query")}


class Shared:

    def __init__(self, dram):
        self.dram = dram


class Link:

    def __init__(self, sem):
        self.sem, self.count = sem, 0

    def __call__(self, eng, ins):
        self.count += 1
        ins.then_inc(self.sem, 1)
        eng.wait_ge(self.sem, self.count)


def load_block(sp, k, b):
    if b >= len(BLOCKS):
        return
    kind, i = BLOCKS[b]
    if b >= 2:
        sp.wait_ge(*k.block_used[b - 2])
    src = k.dram["w"][kind][i]
    sp.dma_start(k.ring[b % 2][:, 0:src.shape[1]], src).then_inc(k.block_here[b % 2], 16)


def wait_block(pe, k, b):
    pe.wait_ge(k.block_here[b % 2], 16 * (b // 2 + 1))


def stage_norm(nc, k):
    NT = TILES + 1
    with ExitStack() as ctx:
        sb = lambda n, s, d=F32: ctx.enter_context(nc.sbuf_tensor(n, s, d, side="right"))
        sem = lambda n: k.sem("n_" + n)
        x = sb("n_x", [P, NT, D])
        xn = sb("n_xn", [P, NT, D])
        ss = sb("n_ss", [P, NT])
        rs = sb("n_rs", [P, NT])
        w1 = sb("n_w1", [P, KD])
        wdt = sb("n_wdt", [P, KD, HEADS])
        dtb = sb("n_dtb", [P, HEADS])
        ea = sb("n_ea", [P, HEADS])
        u = sb("n_u", [P, 6, HEADS])
        e = sb("n_e", [P, 6, HEADS])
        lu = sb("n_lu", [P, 6, HEADS])
        w = sb("n_w", [P, 6, HEADS])
        ac = sb("n_ac", [P, 5, HEADS])
        al = sb("n_al", [P, 5, HEADS])
        decd = sb("n_decd", [NSAMP, NSAMP, HEADS])
        x_here, sq_done, ms_done, rt_done, xn_done = map(sem, ("x_here", "sq_done", "ms_done", "rt_done", "xn_done"))
        tr_done, ev_done, dt_raw, dt_lin = map(sem, ("tr_done", "ev_done", "dt_raw", "dt_lin"))
        dt_e, dt_ln, da_done, cum_done, cum_copied = map(sem, ("dt_e", "dt_ln", "da_done", "cum_done", "cum_copied"))
        ex_done, decd_done, decb_done, small_here = map(sem, ("ex_done", "decd_done", "decb_done", "small_here"))
        rows = [P] * TILES + [SM]
        ps = k.ps
        block = ctx.enter_context(nc.Block())

        @block.sync
        def _(sp):
            for i in range(NT):
                lo = SM + i * P if i < TILES else 0
                sp.dma_start(x[0:rows[i], i, :], k.dram["x_all"][lo:lo + rows[i], :]).then_inc(x_here, 16)
            for dst, src in ((w1[:, :], k.dram["norm1"]), (wdt[:, :, :], k.dram["wdt"]), (dtb[:, :], k.dram["dt_bias"]), (ea[:, :], k.dram["a_log"])):
                sp.dma_start(dst, src).then_inc(small_here, 16)
            for dst, src in k.const_loads:
                sp.dma_start(dst, src).then_inc(k.consts_here, 16)
            load_block(sp, k, 0)
            load_block(sp, k, 1)

        @block.scalar
        def _(act):
            act.wait_ge(x_here, 16 * NT)
            for i in range(NT):
                last = nc.scalar.activation(xn[0:rows[i], i, :], x[0:rows[i], i, :], ACT.Square,
                                            accum_out=ss[0:rows[i], i:i + 1])
                last.then_inc(sq_done, 1)
            act.wait_ge(ms_done, 1)
            nc.scalar.activation(rs[:, 0:TILES], rs[:, 0:TILES], ACT.Sqrt)
            nc.scalar.activation(rs[0:SM, TILES:NT], rs[0:SM, TILES:NT], ACT.Sqrt).then_inc(rt_done, 1)
            act.wait_ge(small_here, 64)
            nc.scalar.activation(ea[:, :], ea[:, :], ACT.Exp).then_inc(dt_e, 1)
            act.wait_ge(dt_lin, 1)
            k.alink(act, nc.scalar.activation(e[:, :, :], u[:, :, :], ACT.Abs))
            k.alink(act, nc.scalar.activation(e[:, :, :], e[:, :, :], ACT.Exp, scale=-1.0))
            nc.scalar.activation(lu[:, :, :], e[:, :, :], ACT.Ln, bias=1.0).then_inc(dt_ln, 1)
            act.wait_ge(cum_copied, 1)
            nc.scalar.activation(k.eac[:, :, :], ac[:, 0:TILES, :], ACT.Exp)
            nc.scalar.activation(k.cdec[:, :, :], al[:, 0:TILES, :], ACT.Exp)
            nc.scalar.activation(k.decs[:, :], k.da[0:NSAMP, 5, :], ACT.Exp)
            nc.scalar.activation(k.dte[:, :, :], w[:, 0:5, :], ACT.Exp).then_inc(ex_done, 1)

        @block.vector
        def _(dve):
            dve.wait_ge(sq_done, NT)
            nc.vector.tensor_scalar(rs[:, 0:TILES], ss[:, 0:TILES], 1.0 / D, EPS, ALU.mult, ALU.add)
            nc.vector.tensor_scalar(rs[0:SM, TILES:NT], ss[0:SM, TILES:NT], 1.0 / D, EPS, ALU.mult, ALU.add).then_inc(ms_done, 1)
            dve.wait_ge(rt_done, 1)
            nc.vector.reciprocal(rs[:, 0:TILES], rs[:, 0:TILES])
            k.vlink(dve, nc.vector.reciprocal(rs[0:SM, TILES:NT], rs[0:SM, TILES:NT]))
            dve.wait_ge(x_here, 16 * NT)
            for i in range(NT):
                nc.vector.tensor_scalar(xn[0:rows[i], i, :], x[0:rows[i], i, :], rs[0:rows[i], i:i + 1], None, ALU.mult).then_inc(xn_done, 1)
            dve.wait_ge(small_here, 64)
            for i in range(NT):
                lo = SM + i * P if i < TILES else 0
                for half in range(2):
                    n = 2 * i + half
                    dve.wait_ge(tr_done, n + 1)
                    src = ps[n % 2][:, :].rearrange("p (a t) -> p a t", a=4)[:, :, 0:rows[i]]
                    nc.vector.tensor_tensor(k.xnT[:, 4 * half:4 * half + 4, lo:lo + rows[i]], src,
                                            w1[:, 4 * half:4 * half + 4].unsqueeze(2).to_broadcast([P, 4, rows[i]]),
                                            ALU.mult).then_inc(ev_done, 1)
            k.vlink(dve, nc.vector.memset(u[:, :, :], 0.0))
            dve.wait_ge(dt_raw, 1)
            raw = ps[2][:, 0:6 * HEADS].rearrange("p (a h) -> p a h", a=6)
            nc.vector.tensor_tensor(u[:, 0:TILES, :], raw[:, 0:TILES, :], dtb[:, :].unsqueeze(1).to_broadcast([P, TILES, HEADS]), ALU.add)
            nc.vector.tensor_tensor(u[0:NMETA, 4, :], raw[0:NMETA, 4, :], dtb[0:NMETA, :], ALU.add)
            nc.vector.tensor_tensor(u[0:NSAMP, 5, :], raw[0:NSAMP, 5, :], dtb[0:NSAMP, :], ALU.add).then_inc(dt_lin, 1)
            dve.wait_ge(dt_ln, 1)
            TINY = 1e-30
            k.vlink(dve, nc.vector.tensor_scalar(w[:, :, :], e[:, :, :], 1.0, None, ALU.add))
            k.vlink(dve, nc.vector.tensor_scalar(w[:, :, :], w[:, :, :], -1.0, TINY, ALU.add, ALU.add))
            k.vlink(dve, nc.vector.reciprocal(w[:, :, :], w[:, :, :]))
            k.vlink(dve, nc.vector.scalar_tensor_tensor(lu[:, :, :], lu[:, :, :], TINY, w[:, :, :], ALU.add, ALU.mult))
            k.vlink(dve, nc.vector.tensor_tensor(lu[:, :, :], lu[:, :, :], e[:, :, :], ALU.mult))
            k.vlink(dve, nc.vector.scalar_tensor_tensor(k.dt[:, :, :], u[:, :, :], 0.0, lu[:, :, :], ALU.max, ALU.add))
            dve.wait_ge(dt_e, 1)
            nc.vector.scalar_tensor_tensor(k.da[:, :, :], k.dt[:, :, :], -1.0, ea[:, :].unsqueeze(1).to_broadcast([P, 6, HEADS]), ALU.mult, ALU.mult).then_inc(da_done, 1)
            k.vlink(dve, nc.vector.memset(ac[:, :, :], 0.0))
            dve.wait_ge(cum_done, 1)
            cum = ps[3][:, 0:5 * HEADS].rearrange("p (a h) -> p a h", a=5)
            tot = ps[4][:, 0:5 * HEADS].rearrange("p (a h) -> p a h", a=5)
            nc.vector.tensor_copy(ac[:, 0:TILES, :], cum[:, 0:TILES, :])
            nc.vector.tensor_copy(al[:, :, :], tot)
            k.vlink(dve, nc.vector.tensor_copy(ac[0:NMETA, 4, :], cum[0:NMETA, 4, :]))
            nc.vector.tensor_scalar(k.nac[:, :, :], ac[:, 0:TILES, :], -1.0, None, ALU.mult)
            nc.vector.tensor_tensor(w[:, 0:5, :], al[:, :, :], ac[:, :, :], ALU.subtract).then_inc(cum_copied, 1)
            dve.wait_ge(ex_done, 1)
            dve.wait_ge(k.consts_here, 16 * len(k.const_loads))
            nc.vector.tensor_tensor(k.dte[:, :, :], k.dte[:, :, :], k.dt[:, 0:5, :], ALU.mult)
            nc.vector.tensor_tensor(decd[:, :, :], k.decs[:, :].unsqueeze(1).to_broadcast([NSAMP, NSAMP, HEADS]),
                                    k.diag8[:, :].unsqueeze(2).to_broadcast([NSAMP, NSAMP, HEADS]),
                                    ALU.mult).then_inc(decd_done, 1)
            dve.wait_ge(decb_done, 1)
            k.vlink(dve, nc.vector.tensor_copy(k.decb[:, :, :], ps[5][:, 0:NSAMP * HEADS].rearrange("p (b h) -> p b h", b=NSAMP)))

        @block.tensor
        def _(pe):
            pe.wait_ge(k.consts_here, 16 * len(k.const_loads))
            for i in range(NT):
                pe.wait_ge(xn_done, i + 1)
                for half in range(2):
                    n = 2 * i + half
                    if n >= 2:
                        pe.wait_ge(ev_done, n - 1)
                    for a in range(4):
                        kt = 4 * half + a
                        last = nc.tensor.transpose(ps[n % 2][:, a * P:a * P + rows[i]], xn[0:rows[i], i, kt * P:(kt + 1) * P],
                                                   k.ident[0:rows[i], 0:rows[i]])
                    last.then_inc(tr_done, 1)
            pe.wait_ge(ev_done, 2 * NT)
            pe.wait_ge(small_here, 64)
            spans = [(tile_cols(c), P) for c in range(TILES)] + [(slice(META0, SM), NMETA), (slice(0, NSAMP), NSAMP)]
            for a, (cols, m) in enumerate(spans):
                for kt in range(KD):
                    last = nc.tensor.matmul(ps[2][0:m, a * HEADS:(a + 1) * HEADS], k.xnT[:, kt, cols], wdt[:, kt, :],
                                            start=kt == 0, stop=kt == KD - 1)
            last.then_inc(dt_raw, 1)
            pe.wait_ge(da_done, 1)
            daf = k.da[:, :, :].rearrange("p a h -> p (a h)")
            m0 = TILES * HEADS
            nc.tensor.matmul(ps[3][:, 0:m0], k.tri[:, :], daf[:, 0:m0], start=True, stop=True)
            nc.tensor.matmul(ps[3][0:NMETA, m0:m0 + HEADS], k.tri[0:NMETA, 0:NMETA], daf[0:NMETA, m0:m0 + HEADS], start=True, stop=True)
            nc.tensor.matmul(ps[4][:, 0:m0], k.ones[:, :], daf[:, 0:m0], start=True, stop=True)
            nc.tensor.matmul(ps[4][:, m0:m0 + HEADS], k.ones[0:NMETA, :], daf[0:NMETA, m0:m0 + HEADS], start=True, stop=True).then_inc(cum_done, 1)
            pe.wait_ge(decd_done, 1)
            nc.tensor.matmul(ps[5][:, 0:NSAMP * HEADS], k.ones[0:NSAMP, :], decd[:, :, :].rearrange("p b h -> p (b h)"), start=True, stop=True).then_inc(decb_done, 1)


STEPS = 1 + TILES


def ssd_order():
    order = [("tile", 0, j) for j in range(CT)]
    for g in range(GROUPS):
        tiles = [("tile", g + 1, j) for j in range(CT)] if g + 1 < GROUPS else []
        order += [("front", g, 0)] + tiles[0:1]
        for i in range(1, STEPS):
            order += [("front", g, i), ("back", g, i - 1)] + tiles[i:i + (1 if i < STEPS - 1 else 2)]
        order += [("back", g, STEPS - 1), ("sample", g, 0)]
    return order


SSD_ORDER = ssd_order()


def stage_ssd(nc, k):
    with ExitStack() as ctx:
        sb = lambda n, s, d=F32: ctx.enter_context(nc.sbuf_tensor("s_" + n, s, d, side="right"))
        sem = lambda n: k.sem("s_" + n)
        raw = sb("raw", [P, 3, RAW])
        cv = sb("cv", [P, 3, CONVD])
        xc = sb("xc", [P, 2, CT, CONVD])
        hist = sb("hist", [P, GROUPS, CT, CONV, NSAMP])
        cw = sb("cw", [P, GROUPS, CT, CONV + 1])
        last3 = sb("last3", [P, GROUPS, CT, HIST])
        sconv = sb("sconv", [P, CT, NSAMP])
        sterm = sb("sterm", [P, CT, NSAMP])
        sxc = sb("sxc", [P, 2, CT, NSAMP])
        cmask = sb("cmask", [P, NSAMP, NSAMP])
        xdt = sb("xdt", [P, 2, GW])
        xdec = sb("xdec", [P, 2, GW])
        bcb = sb("bcb", [P, 2, 2, P])
        mix = sb("mix", [P, 2, 2, 4, P])
        yoff = sb("yoff", [P, GW])
        state = sb("state", [P, 2, GW])
        sxdt = sb("sxdt", [NSAMP, GW])
        sst = sb("sst", [P, NSAMP, GW])
        dsk = sb("dsk", [P, HEADS])
        ins_here, tile_ready, tile_evac, conv_first, conv_done, xc_ready = map(
            sem, ("ins_here", "tile_ready", "tile_evac", "conv_first", "conv_done", "xc_ready"))
        xt_ready, bc_ready, xt_used, bc_copied, yoff_done = map(sem, ("xt_ready", "bc_ready", "xt_used", "bc_copied", "yoff_done"))
        seg_ready, exp_done, mix_done, yd_ready, yo_ready = map(sem, ("seg_ready", "exp_done", "mix_done", "yd_ready", "yo_ready"))
        cs_ready, y_done, state_done, xdt_done, xdec_done, zeroed = map(
            sem, ("cs_ready", "y_done", "state_done", "xdt_done", "xdec_done", "zeroed"))
        sconv_done, sxc_ready, sxt_ready, sxdt_done, cmask_done = map(sem, ("sconv_done", "sxc_ready", "sxt_ready", "sxdt_done", "cmask_done"))
        sst_here, sdec_done, sx_ready, sst_done, sy_ready, sy_done = map(sem, ("sst_here", "sdec_done", "sx_ready", "sst_done", "sy_ready", "sy_done"))
        sst_out, pst_out, conv_out, pst_final = map(sem, ("sst_out", "pst_out", "conv_out", "pst_final"))
        k.block_used.update({FIRST["ssd"] + g: (tile_ready, CT * (g + 1)) for g in range(GROUPS)})
        ps = k.ps
        MAIN, SMALL, XT, BC, SEG, YD, YO = (0, 1), 2, 3, 4, 5, 6, 7
        CS = YO
        block = ctx.enter_context(nc.Block())

        def chunk_cols(i):
            return slice(0, NMETA) if i == 0 else slice(NMETA + (i - 1) * P, NMETA + i * P)

        def chunks_before(s):
            return s // STEPS * TILES + max(0, s % STEPS - 1)

        @block.sync
        def _(sp):
            for dst, src in ((hist[:, :, :, :, :], k.dram["state_conv"]), (cw[:, :, :, :], k.dram["conv_w"]), (dsk[:, :], k.dram["d_skip"])):
                sp.dma_start(dst, src).then_inc(ins_here, 16)
            for g in range(GROUPS):
                if g >= 1:
                    sp.wait_ge(sst_out, 16 * g)
                    sp.wait_ge(sy_ready, g)
                sp.dma_start(sst[:, :, :], k.dram["state_ssd"][g]).then_inc(sst_here, 16)
                load_block(sp, k, FIRST["ssd"] + g + 2)
                sp.wait_ge(sst_done, NSAMP * (g + 1))
                sp.dma_start(k.dram["o_sssd"][g], sst[:, :, :]).then_inc(sst_out, 16)
                sp.wait_ge(state_done, STEPS * (g + 1))
                sp.dma_start(k.dram["o_pssd"][g], state[:, g % 2, :]).then_inc(pst_out, 16)
            sp.wait_ge(tile_evac, GROUPS * CT)
            sp.dma_start(k.dram["o_sconv"], hist[:, :, :, 1:CONV, :]).then_inc(conv_out, 16)
            sp.dma_start(k.dram["o_pconv"], last3[:, :, :, :]).then_inc(conv_out, 16)
            sp.wait_ge(conv_out, 32)
            sp.wait_ge(sst_out, 16 * GROUPS)
            sp.wait_ge(pst_out, 16 * GROUPS)

        @block.tensor
        def _(pe):
            for kind, g, i in SSD_ORDER:
                if kind == "tile":
                    n, b = g * CT + i, FIRST["ssd"] + g
                    if i == 0:
                        wait_block(pe, k, b)
                    if n >= 2:
                        pe.wait_ge(tile_evac, n - 1)
                    w = k.ring[b % 2][:, 0:KD * CT * P].rearrange("p (k c) -> p k c", k=KD)
                    for kt in range(KD):
                        wt = w[:, kt, i * P:(i + 1) * P]
                        nc.tensor.matmul(ps[MAIN[n % 2]][:, :], wt, k.xnT[:, kt, SM:COLS], start=kt == 0, stop=kt == KD - 1)
                    if n >= 1:
                        pe.wait_ge(tile_evac, n)
                    for kt in range(KD):
                        wt = w[:, kt, i * P:(i + 1) * P]
                        last = nc.tensor.matmul(ps[SMALL][:, 0:SM], wt, k.xnT[:, kt, 0:SM], start=kt == 0, stop=kt == KD - 1)
                    last.then_inc(tile_ready, 1)
                elif kind == "front":
                    s = g * STEPS + i
                    d = g * TILES + i - 1
                    cols, m = chunk_cols(i), (NMETA if i == 0 else P)
                    x = xc[:, g % 2]

                    def decays(half):
                        q = 2 * d + half
                        if q >= 1:
                            pe.wait_ge(exp_done, q)
                        nc.tensor.matmul(ps[SEG][:, :], k.identb[:, :], k.future[:, :], start=True, stop=False)
                        for h in range(4):
                            hh = g * HPG + half * 4 + h
                            last = nc.tensor.matmul(ps[SEG][:, h * P:(h + 1) * P], k.da[:, i - 1, hh:hh + 1].to_broadcast([P, P]),
                                                    k.tri[:, :], start=False, stop=h == 3)
                        last.then_inc(seg_ready, 1)

                    if i > 0:
                        decays(0)
                    if i == 0:
                        pe.wait_ge(xc_ready, CT * (g + 1))
                        if g >= 1:
                            pe.wait_ge(sst_done, NSAMP * g)
                            pe.wait_ge(sy_done, g)
                    if i == 1:
                        pe.wait_ge(xdec_done, s)
                    elif s >= 1:
                        pe.wait_ge(xt_used, chunks_before(s))
                    for a in range(CT - 2):
                        last = nc.tensor.transpose(ps[XT][0:m, a * P:(a + 1) * P], x[:, a, cols], k.ident[:, :])
                    last.then_inc(xt_ready, 1)
                    if s >= 1:
                        pe.wait_ge(bc_copied, s)
                    last = nc.tensor.transpose(ps[BC][0:m, 0:P], x[:, B_TILE, cols], k.ident[:, :])
                    if i > 0:
                        last = nc.tensor.matmul(ps[BC][:, P:2 * P], x[:, B_TILE, cols], x[:, C_TILE, cols], start=True, stop=True)
                    last.then_inc(bc_ready, 1)
                    if i > 0:
                        decays(1)
                elif kind == "back":
                    s, d = g * STEPS + i, g * TILES + i - 1
                    cols, m, par = chunk_cols(i), (NMETA if i == 0 else P), s % 2
                    if s >= 1:
                        pe.wait_ge(state_done, s)
                    if i > 0:
                        nc.tensor.matmul(ps[YO][:, :], xc[:, g % 2, C_TILE, cols], state[:, g % 2, :], start=True, stop=True).then_inc(yo_ready, 1)
                        if d >= 1:
                            pe.wait_ge(y_done, d)
                        pe.wait_ge(xdt_done, d + 1)
                        pe.wait_ge(mix_done, 2 * d + 2)
                        for h in range(HPG):
                            last = nc.tensor.matmul(ps[YD][:, h * HEAD:(h + 1) * HEAD], mix[:, d % 2, h // 4, h % 4, :],
                                                    xdt[:, par, h * HEAD:(h + 1) * HEAD], start=True, stop=True)
                        last.then_inc(yd_ready, 1)
                        pe.wait_ge(yoff_done, d + 1)
                    pe.wait_ge(xdec_done, s + 1)
                    pe.wait_ge(bc_copied, s + 1)
                    nc.tensor.matmul(ps[CS][:, :], bcb[0:m, par, 0, :], xdec[0:m, par, :], start=True, stop=True).then_inc(cs_ready, 1)
                else:
                    pe.wait_ge(sxc_ready, g + 1)
                    pe.wait_ge(xt_used, TILES * (g + 1))
                    for a in range(CT - 2):
                        last = nc.tensor.transpose(ps[XT][0:NSAMP, a * P:(a + 1) * P], sxc[:, g % 2, a, :], k.ident[:, :])
                    last.then_inc(sxt_ready, 1)
                    pe.wait_ge(sxdt_done, g + 1)
                    pe.wait_ge(cmask_done, g + 1)
                    pe.wait_ge(state_done, STEPS * (g + 1))
                    pe.wait_ge(y_done, TILES * (g + 1))

                    def spread(b):
                        q = g * NSAMP + b
                        if q >= 2:
                            pe.wait_ge(sst_done, q - 1)
                        nc.tensor.matmul(ps[(XT, CS)[b % 2]][:, :], k.sel8[:, b, :], sxdt[:, :], start=True, stop=True).then_inc(sx_ready, 1)

                    spread(0)
                    for b in range(NSAMP):
                        if b + 1 < NSAMP:
                            spread(b + 1)
                        pe.wait_ge(sst_done, g * NSAMP + b + 1)
                        last = nc.tensor.matmul(ps[YD][0:NSAMP, :], cmask[:, b, :], sst[:, b, :], start=b == 0, stop=b == NSAMP - 1)
                    last.then_inc(sy_ready, 1)

        @block.scalar
        def _(act):
            act.wait_ge(ins_here, 48)
            act.wait_ge(zeroed, 1)

            def silu(n):
                g, j = divmod(n, CT)
                act.wait_ge(conv_done, n + 1)
                if j == 0 and g >= 2:
                    act.wait_ge(cs_ready, STEPS * (g - 1))
                nc.scalar.activation(xc[:, g % 2, j, :], cv[:, n % 3, :], ACT.Silu).then_inc(xc_ready, 1)

            for kind, g, i in SSD_ORDER:
                if kind == "tile":
                    n = g * CT + i
                    act.wait_ge(tile_ready, n + 1)
                    if n >= 3:
                        act.wait_ge(conv_done, n - 2)
                    small = ps[SMALL][:, 0:SM]
                    nc.scalar.copy(raw[:, n % 3, HIST + NMETA:RAW], ps[MAIN[n % 2]][:, :])
                    nc.scalar.copy(raw[:, n % 3, HIST:HIST + NMETA], small[:, META0:SM])
                    nc.scalar.copy(hist[:, g, i, CONV - 1, :], small[:, 0:NSAMP])
                    nc.scalar.copy(last3[:, g, i, :], ps[MAIN[n % 2]][:, SEQ - HIST:SEQ]).then_inc(tile_evac, 1)
                    act.wait_ge(tile_evac, n + 1)
                    if n >= 3:
                        act.wait_ge(xc_ready, n - 2)
                    nc.scalar.activation(cv[:, n % 3, :], raw[:, n % 3, 0:CONVD], ACT.Identity,
                                         bias=cw[:, g, i, CONV:CONV + 1], scale=cw[:, g, i, 0:1]).then_inc(conv_first, 1)
                    if n % CT >= 1:
                        silu(n - 1)
                    if n % CT == CT - 1:
                        silu(n)
                        act.wait_ge(sconv_done, g + 1)
                        if g >= 2:
                            act.wait_ge(sst_done, NSAMP * (g - 1))
                        nc.scalar.activation(sxc[:, g % 2, :, :], sconv[:, :, :], ACT.Silu).then_inc(sxc_ready, 1)
                elif kind == "front":
                    s, d = g * STEPS + i, g * TILES + i - 1
                    m, par = (NMETA if i == 0 else P), s % 2

                    def decays(half):
                        act.wait_ge(seg_ready, 2 * d + half + 1)
                        if d >= 2:
                            act.wait_ge(yd_ready, d - 1)
                        for h in range(4):
                            hh = g * HPG + half * 4 + h
                            last = nc.scalar.activation(mix[:, d % 2, half, h, :], ps[SEG][:, h * P:(h + 1) * P], ACT.Exp,
                                                        bias=k.nac[:, i - 1, hh:hh + 1])
                        last.then_inc(exp_done, 1)

                    if i > 0:
                        decays(0)
                    act.wait_ge(bc_ready, s + 1)
                    if s >= 2:
                        act.wait_ge(cs_ready, s - 1)
                        if chunks_before(s - 1):
                            act.wait_ge(mix_done, 2 * chunks_before(s - 1))
                    w = P if i == 0 else 2 * P
                    nc.scalar.copy(bcb[0:m, par, :, :].rearrange("p a b -> p (a b)")[:, 0:w], ps[BC][0:m, 0:w]).then_inc(bc_copied, 1)
                    if i > 0:
                        decays(1)

        @block.vector
        def _(dve):
            dve.wait_ge(ins_here, 48)
            nc.vector.memset(raw[:, :, 0:HIST], 0.0).then_inc(zeroed, 1)
            heads = lambda ap: ap.rearrange("p (h c) -> p h c", c=HEAD)
            for kind, g, i in SSD_ORDER:
                hs = slice(g * HPG, (g + 1) * HPG)
                gc = slice(g * GW, (g + 1) * GW)
                wide = lambda ap, m=P: ap.unsqueeze(2).to_broadcast([m, HPG, HEAD])
                if kind == "tile":
                    n = g * CT + i
                    dve.wait_ge(conv_first, n + 1)
                    for j in range(1, CONV):
                        ins = nc.vector.scalar_tensor_tensor(cv[:, n % 3, :], raw[:, n % 3, j:j + CONVD], cw[:, g, i, j:j + 1],
                                                             cv[:, n % 3, :], ALU.mult, ALU.add)
                        if j < CONV - 1:
                            k.vlink(dve, ins)
                    ins.then_inc(conv_done, 1)
                elif kind == "front":
                    s, d = g * STEPS + i, g * TILES + i - 1
                    m, par = (NMETA if i == 0 else P), s % 2
                    c = TILES if i == 0 else i - 1
                    dve.wait_ge(xt_ready, s + 1)
                    if s >= 2:
                        dve.wait_ge(cs_ready, s - 1)
                        if chunks_before(s - 1):
                            dve.wait_ge(yd_ready, chunks_before(s - 1))
                    xt = heads(ps[XT][0:m, :])
                    nc.vector.tensor_tensor(heads(xdec[0:m, par, :]), xt, wide(k.dte[0:m, c, hs], m), ALU.mult).then_inc(xdec_done, 1)
                    if i > 0:
                        nc.vector.tensor_tensor(heads(xdt[:, par, :]), xt, wide(k.dt[:, c, hs]), ALU.mult).then_inc(xdt_done, 1)
                        nc.vector.tensor_tensor(heads(k.y[:, c, gc]), xt, wide(dsk[:, hs]), ALU.mult).then_inc(xt_used, 1)
                        for half in range(2):
                            dve.wait_ge(bc_copied, s + 1)
                            dve.wait_ge(exp_done, 2 * d + half + 1)
                            nc.vector.tensor_tensor(mix[:, d % 2, half, :, :], mix[:, d % 2, half, :, :],
                                                    bcb[:, par, 1, :].unsqueeze(1).to_broadcast([P, 4, P]), ALU.mult).then_inc(mix_done, 1)
                elif kind == "back":
                    s, d, c = g * STEPS + i, g * TILES + i - 1, i - 1
                    if i > 0:
                        dve.wait_ge(yo_ready, d + 1)
                        nc.vector.tensor_tensor(heads(yoff[:, :]), heads(ps[YO][:, :]), wide(k.eac[:, c, hs]), ALU.mult).then_inc(yoff_done, 1)
                        k.vlink(dve, nc.vector.tensor_tensor(heads(state[:, g % 2, :]), heads(state[:, g % 2, :]), wide(k.cdec[:, c, hs]), ALU.mult))
                        dve.wait_ge(xt_used, d + 1)
                        nc.vector.tensor_tensor(k.y[:, c, gc], k.y[:, c, gc], yoff[:, :], ALU.add)
                        dve.wait_ge(cs_ready, s + 1)
                        nc.vector.tensor_tensor(state[:, g % 2, :], state[:, g % 2, :], ps[CS][:, :], ALU.add).then_inc(state_done, 1)
                        dve.wait_ge(yd_ready, d + 1)
                        dve.wait_ge(state_done, s + 1)
                        nc.vector.tensor_tensor(k.y[:, c, gc], k.y[:, c, gc], ps[YD][:, :], ALU.add).then_inc(y_done, 1)
                    else:
                        if g >= 2:
                            dve.wait_ge(pst_out, 16 * (g - 1))
                        dve.wait_ge(cs_ready, s + 1)
                        nc.vector.tensor_copy(state[:, g % 2, :], ps[CS][:, :]).then_inc(state_done, 1)
                else:
                    dve.wait_ge(sxc_ready, g + 1)
                    if g >= 1:
                        dve.wait_ge(sy_ready, g)
                    nc.vector.tensor_tensor(cmask[:, :, :], k.eye8[:, :, :], sxc[:, g % 2, C_TILE, :].unsqueeze(1).to_broadcast([P, NSAMP, NSAMP]),
                                            ALU.mult).then_inc(cmask_done, 1)
                    dve.wait_ge(sxt_ready, g + 1)
                    xt = heads(ps[XT][0:NSAMP, :])
                    nc.vector.tensor_tensor(heads(sxdt[:, :]), xt, wide(k.dt[0:NSAMP, 5, hs], NSAMP), ALU.mult)
                    nc.vector.tensor_tensor(heads(k.ys[:, gc]), xt, wide(dsk[0:NSAMP, hs], NSAMP), ALU.mult).then_inc(sxdt_done, 1)
                    for b in range(NSAMP):
                        q = g * NSAMP + b
                        dve.wait_ge(sdec_done, q + 1)
                        dve.wait_ge(sx_ready, q + 1)
                        nc.vector.scalar_tensor_tensor(sst[:, b, :], ps[(XT, CS)[b % 2]][:, :], sxc[:, g % 2, B_TILE, b:b + 1],
                                                       sst[:, b, :], ALU.mult, ALU.add).then_inc(sst_done, 1)
                    dve.wait_ge(sy_ready, g + 1)
                    dve.wait_ge(sxdt_done, g + 1)
                    nc.vector.tensor_tensor(k.ys[:, gc], k.ys[:, gc], ps[YD][0:NSAMP, :], ALU.add).then_inc(sy_done, 1)

        @block.gpsimd
        def _(pool):
            pool.wait_ge(ins_here, 48)
            for kind, g, i in SSD_ORDER:
                if kind == "tile" and i == CT - 1:
                    pool.wait_ge(tile_evac, CT * (g + 1))
                    if g >= 1:
                        pool.wait_ge(sxc_ready, g)
                    tap = lambda j: cw[:, g, :, j:j + 1].to_broadcast([P, CT, NSAMP])
                    k.plink(pool, nc.gpsimd.tensor_tensor(sconv[:, :, :], hist[:, g, :, 0, :], tap(0), ALU.mult))
                    for j in range(1, CONV):
                        k.plink(pool, nc.gpsimd.tensor_tensor(sterm[:, :, :], hist[:, g, :, j, :], tap(j), ALU.mult))
                        k.plink(pool, nc.gpsimd.tensor_tensor(sconv[:, :, :], sconv[:, :, :], sterm[:, :, :], ALU.add))
                    nc.gpsimd.tensor_tensor(sconv[:, :, :], sconv[:, :, :], tap(CONV), ALU.add).then_inc(sconv_done, 1)
                elif kind == "front" and i == 1:
                    pool.wait_ge(sst_here, 16 * (g + 1))
                    for b in range(NSAMP):
                        v = sst[:, b, :].rearrange("p (h c) -> p h c", c=HEAD)
                        nc.gpsimd.tensor_tensor(v, v, k.decb[:, b, g * HPG:(g + 1) * HPG].unsqueeze(2).to_broadcast([P, HPG, HEAD]),
                                                ALU.mult).then_inc(sdec_done, 1)


def gla_order():
    proj = lambda h: [("q", h, 0), ("k", h, 0)] + [("v", h, c) for c in range(TILES)] + [("vsmall", h, 0)]
    order = proj(0)
    for h in range(GH):
        steps = [("prep", h, 0), ("fold", h, 0)] + [("chunk", h, c) for c in range(TILES)] + [("sample", h, 0)]
        nxt = proj(h + 1) if h + 1 < GH else [None] * len(steps)
        for a, b in zip(steps, nxt):
            order += [a] + ([b] if b else [])
    return order


def stage_gla(nc, k):
    order = gla_order()
    NCH = SEQ // GCH
    NP = 2 + TILES
    QSCALE = DK ** -0.5
    with ExitStack() as ctx:
        sb = lambda n, s, d=F32: ctx.enter_context(nc.sbuf_tensor("g_" + n, s, d, side="right"))
        sem = lambda n: k.sem("g_" + n)
        wglr = sb("wglr", [P, KD, RANK])
        up = sb("up", [RANK + 1, GH * DK])
        glrT = sb("glrT", [RANK + 1, COLS])
        gk = sb("gk", [P, TILES, GH * DK])
        gkm = sb("gkm", [NMETA, GH * DK])
        gks = sb("gks", [P, GH, NSAMP])
        qT = sb("qT", [P, 2, SEQ])
        qs = sb("qs", [P, 2, NSAMP])
        kT = sb("kT", [P, 2, NMETA + SEQ])
        ks = sb("ks", [P, 2, NSAMP])
        vt = sb("vt", [P, 2, TILES, DV])
        vm = sb("vm", [NMETA, 2, DV])
        vs = sb("vs", [NSAMP, 2, DV])
        bend = sb("bend", [P, NCH + 1])
        cdg = sb("cdg", [P, 2, NCH])
        ep = sb("ep", [P, SEQ])
        qa = sb("qa", [P, 2, TILES, 4, GCH])
        ke = sb("ke", [P, SEQ])
        kd = sb("kd", [P, NMETA + SEQ])
        kt_ = sb("kt", [P, TILES, DK])
        ktm = sb("ktm", [NMETA, DK])
        att = sb("att", [P, TILES, P])
        st = sb("st", [P, 2, 2, DV])
        gs = sb("gs", [P, NSAMP, DV])
        qmask = sb("qmask", [P, NSAMP, NSAMP])
        ins_here, ones_set, glr_ready, glr_copied, gk_ready, gk_ln, gk_done, gs_exp = map(
            sem, ("ins_here", "ones_set", "glr_ready", "glr_copied", "gk_ready", "gk_ln", "gk_done", "gs_exp"))
        proj_ready, proj_evac, vs_ready, vs_evac = map(sem, ("proj_ready", "proj_evac", "vs_ready", "vs_evac"))
        cum_ready, bend_done, exp_done, qa_done, ke_done, kd_done = map(sem, ("cum_ready", "bend_done", "exp_done", "qa_done", "ke_done", "kd_done"))
        kt_ready, kt_copied, att_ready, att_done = map(sem, ("kt_ready", "kt_copied", "att_ready", "att_done"))
        cs_ready, st_done, o_ready, o_copied, st_out = map(sem, ("cs_ready", "st_done", "o_ready", "o_copied", "st_out"))
        gs_here, sdec_done, sv_ready, gs_done, os_ready, os_done, gs_out, qm_done = map(
            sem, ("gs_here", "sdec_done", "sv_ready", "gs_done", "os_ready", "os_done", "gs_out", "qm_done"))
        k.block_used.update({FIRST["gla"] + h: (vs_ready, h + 1) for h in range(GH)})
        ps = k.ps
        SMALL, CUM, ATT, O, CS, MISC = 2, 3, 4, 5, 6, 7
        block = ctx.enter_context(nc.Block())

        @block.sync
        def _(sp):
            for dst, src in ((wglr[:, :, :], k.dram["wglr"]), (up[:, :], k.dram["gate_up"])):
                sp.dma_start(dst, src).then_inc(ins_here, 16)
            for h in range(GH):
                if h >= 1:
                    sp.wait_ge(gs_out, 16 * h)
                    sp.wait_ge(os_ready, h)
                sp.dma_start(gs[:, :, :], k.dram["state_gla"][h]).then_inc(gs_here, 16)
                load_block(sp, k, FIRST["gla"] + h + 2)
                sp.wait_ge(st_done, (NCH + 1) * (h + 1))
                sp.dma_start(k.dram["o_pgla"][h], st[:, h % 2, 0, :]).then_inc(st_out, 16)
                sp.wait_ge(gs_done, NSAMP * (h + 1))
                sp.dma_start(k.dram["o_sgla"][h], gs[:, :, :]).then_inc(gs_out, 16)
            sp.wait_ge(st_out, 16 * GH)
            sp.wait_ge(gs_out, 16 * GH)

        @block.tensor
        def _(pe):
            pe.wait_ge(ins_here, 32)
            for kt in range(KD):
                nc.tensor.matmul(ps[0][0:RANK, :], wglr[:, kt, :], k.xnT[:, kt, SM:COLS], start=kt == 0, stop=kt == KD - 1)
            for kt in range(KD):
                last = nc.tensor.matmul(ps[SMALL][0:RANK, 0:SM], wglr[:, kt, :], k.xnT[:, kt, 0:SM], start=kt == 0, stop=kt == KD - 1)
            last.then_inc(glr_ready, 1)
            pe.wait_ge(glr_copied, 1)
            for c in range(TILES):
                nc.tensor.matmul(ps[CUM + c][:, :], glrT[:, tile_cols(c)], up[:, :], start=True, stop=True)
            nc.tensor.matmul(ps[MISC][0:NMETA, :], glrT[:, META0:SM], up[:, :], start=True, stop=True)
            for h in range(GH):
                last = nc.tensor.matmul(ps[SMALL][:, h * NSAMP:(h + 1) * NSAMP], up[:, h * DK:(h + 1) * DK], glrT[:, 0:NSAMP], start=True, stop=True)
            last.then_inc(gk_ready, 1)
            pe.wait_ge(gk_done, 1)
            for kind, h, c in order:
                par, b = h % 2, FIRST["gla"] + h
                w = k.ring[b % 2][:, 0:KD * (2 * DK + DV)].rearrange("p (k c) -> p k c", k=KD)
                if kind in ("q", "k"):
                    n = h * NP + (kind == "k")
                    if kind == "q":
                        wait_block(pe, k, b)
                    if n >= 2:
                        pe.wait_ge(proj_evac, n - 1)
                    off = DK * (kind == "k")
                    for kt in range(KD):
                        nc.tensor.matmul(ps[n % 2][:, :], w[:, kt, off:off + DK], k.xnT[:, kt, SM:COLS], start=kt == 0, stop=kt == KD - 1)
                    if kind == "k":
                        pe.wait_ge(proj_evac, n)
                    elif h >= 1:
                        pe.wait_ge(vs_evac, h)
                    for kt in range(KD):
                        last = nc.tensor.matmul(ps[SMALL][:, 0:SM], w[:, kt, off:off + DK], k.xnT[:, kt, 0:SM], start=kt == 0, stop=kt == KD - 1)
                    last.then_inc(proj_ready, 1)
                elif kind == "v":
                    n = h * NP + 2 + c
                    pe.wait_ge(proj_evac, n - 1)
                    for kt in range(KD):
                        last = nc.tensor.matmul(ps[n % 2][:, 0:DV], k.xnT[:, kt, tile_cols(c)], w[:, kt, 2 * DK:2 * DK + DV],
                                                start=kt == 0, stop=kt == KD - 1)
                    last.then_inc(proj_ready, 1)
                elif kind == "vsmall":
                    pe.wait_ge(proj_evac, h * NP + 2)
                    for kt in range(KD):
                        nc.tensor.matmul(ps[SMALL][0:NMETA, 0:DV], k.xnT[:, kt, META0:SM], w[:, kt, 2 * DK:2 * DK + DV], start=kt == 0, stop=kt == KD - 1)
                    for kt in range(KD):
                        last = nc.tensor.matmul(ps[SMALL][0:NSAMP, DV:2 * DV], k.xnT[:, kt, 0:NSAMP], w[:, kt, 2 * DK:2 * DK + DV],
                                                start=kt == 0, stop=kt == KD - 1)
                    last.then_inc(vs_ready, 1)
                elif kind == "prep":
                    if h >= 1:
                        pe.wait_ge(gs_done, NSAMP * h)
                        pe.wait_ge(os_done, h)
                    for c_ in range(TILES):
                        nc.tensor.matmul(ps[CUM][:, c_ * P:(c_ + 1) * P], gk[:, c_, h * DK:(h + 1) * DK], k.tri64[:, :], start=True, stop=True)
                    nc.tensor.matmul(ps[MISC][:, 0:NMETA], gkm[:, h * DK:(h + 1) * DK], k.tri64[0:NMETA, 0:NMETA], start=True, stop=True).then_inc(cum_ready, 1)
                elif kind == "fold":
                    pe.wait_ge(kd_done, h + 1)
                    pe.wait_ge(exp_done, h + 1)
                    for c_ in range(TILES):
                        nc.tensor.transpose(ps[CUM][:, c_ * P:(c_ + 1) * P], kd[:, NMETA + c_ * P:NMETA + (c_ + 1) * P], k.ident[:, :])
                    nc.tensor.transpose(ps[MISC][0:NMETA, 0:DK], kd[:, 0:NMETA], k.ident[:, :]).then_inc(kt_ready, 1)
                    pe.wait_ge(ke_done, h + 1)
                    pe.wait_ge(qa_done, h + 1)
                    for c_ in range(TILES):
                        last = nc.tensor.matmul(ps[ATT][:, c_ * P:(c_ + 1) * P], ke[:, c_ * P:(c_ + 1) * P], qa[:, par, c_, 0:4:3, :], start=True, stop=True)
                    last.then_inc(att_ready, 1)
                    pe.wait_ge(kt_copied, h + 1)
                    pe.wait_ge(vs_evac, h + 1)
                    if h >= 1:
                        pe.wait_ge(st_done, (NCH + 1) * h)
                    nc.tensor.matmul(ps[CS][:, 0:DV], ktm[:, :], vm[:, par, :], start=True, stop=True).then_inc(cs_ready, 1)
                elif kind == "chunk":
                    t = h * TILES + c
                    if c == 0:
                        pe.wait_ge(att_done, h + 1)
                    if t >= 1:
                        pe.wait_ge(o_copied, t)
                    nc.tensor.matmul(ps[O][:, 0:DV], att[:, c, :], vt[:, par, c, :], start=True, stop=False)
                    for half in range(2):
                        j = 2 * c + half
                        pe.wait_ge(st_done, (NCH + 1) * h + j + 1)
                        rows = slice(half * GCH, (half + 1) * GCH)
                        last = nc.tensor.matmul(ps[O][:, 0:DV], qa[:, par, c, 2 * half:2 * half + 2, :], st[:, par, j % 2, :], start=False, stop=half == 1)
                        if half == 1:
                            last.then_inc(o_ready, 1)
                        nc.tensor.matmul(ps[CS][:, 0:DV], kt_[rows, c, :], vt[rows, par, c, :], start=True, stop=True).then_inc(cs_ready, 1)
                else:
                    pe.wait_ge(qm_done, h + 1)
                    pe.wait_ge(kt_copied, h + 1)
                    pe.wait_ge(att_done, h + 1)

                    def spread(b_):
                        q = h * NSAMP + b_
                        if q >= 2:
                            pe.wait_ge(gs_done, q - 1)
                        nc.tensor.matmul(ps[(CUM, ATT)[b_ % 2]][:, 0:DV], k.sel8[:, b_, :], vs[:, par, :], start=True, stop=True).then_inc(sv_ready, 1)

                    spread(0)
                    for b_ in range(NSAMP):
                        if b_ + 1 < NSAMP:
                            spread(b_ + 1)
                        pe.wait_ge(gs_done, h * NSAMP + b_ + 1)
                        last = nc.tensor.matmul(ps[MISC][0:NSAMP, 0:DV], qmask[:, b_, :], gs[:, b_, :], start=b_ == 0, stop=b_ == NSAMP - 1)
                    last.then_inc(os_ready, 1)

        @block.scalar
        def _(act):
            act.wait_ge(ones_set, 1)
            act.wait_ge(glr_ready, 1)
            nc.scalar.copy(glrT[0:RANK, SM:COLS], ps[0][0:RANK, :])
            nc.scalar.copy(glrT[0:RANK, 0:SM], ps[SMALL][0:RANK, 0:SM]).then_inc(glr_copied, 1)
            act.wait_ge(gk_ready, 1)
            parts = [(gk[:, c, :], ps[CUM + c][:, :]) for c in range(TILES)]
            parts += [(gkm[:, :], ps[MISC][0:NMETA, :]), (gks[:, :, :].rearrange("p h b -> p (h b)"), ps[SMALL][:, 0:GH * NSAMP])]
            for dst, src in parts:
                last = nc.scalar.activation(dst, src, ACT.Abs)
            k.alink(act, last)
            for dst, src in parts:
                last = nc.scalar.activation(dst, dst, ACT.Exp, scale=-1.0)
            k.alink(act, last)
            for dst, src in parts:
                last = nc.scalar.activation(dst, dst, ACT.Ln, bias=1.0)
            last.then_inc(gk_ln, 1)
            act.wait_ge(gk_done, 1)
            nc.scalar.activation(gks[:, :, :], gks[:, :, :], ACT.Exp, scale=1.0 / 16.0).then_inc(gs_exp, 1)
            for kind, h, c in order:
                par = h % 2
                if kind in ("q", "k"):
                    n = h * NP + (kind == "k")
                    act.wait_ge(proj_ready, n + 1)
                    if kind == "q" and h >= 2:
                        act.wait_ge(os_done, h - 1)
                    if kind == "q":
                        nc.scalar.mul(qT[:, par, :], ps[n % 2][:, :], QSCALE)
                        nc.scalar.mul(qs[:, par, :], ps[SMALL][:, 0:NSAMP], QSCALE).then_inc(proj_evac, 1)
                    else:
                        nc.scalar.copy(kT[:, par, NMETA:NMETA + SEQ], ps[n % 2][:, :])
                        nc.scalar.copy(kT[:, par, 0:NMETA], ps[SMALL][:, META0:SM])
                        nc.scalar.copy(ks[:, par, :], ps[SMALL][:, 0:NSAMP]).then_inc(proj_evac, 1)
                elif kind == "v":
                    n = h * NP + 2 + c
                    act.wait_ge(proj_ready, n + 1)
                    nc.scalar.copy(vt[:, par, c, :], ps[n % 2][:, 0:DV]).then_inc(proj_evac, 1)
                elif kind == "vsmall":
                    act.wait_ge(vs_ready, h + 1)
                    nc.scalar.copy(vm[:, par, :], ps[SMALL][0:NMETA, 0:DV])
                    nc.scalar.copy(vs[:, par, :], ps[SMALL][0:NSAMP, DV:2 * DV]).then_inc(vs_evac, 1)
                elif kind == "prep":
                    act.wait_ge(bend_done, h + 1)
                    if h >= 1:
                        act.wait_ge(qa_done, h)
                        act.wait_ge(att_ready, h)
                        act.wait_ge(kt_ready, h)
                    nc.scalar.activation(ep[:, :], ps[CUM][:, :], ACT.Exp)
                    nc.scalar.activation(ke[:, :], ps[CUM][:, :], ACT.Exp, scale=-1.0)
                    for j in range(NCH):
                        nc.scalar.activation(kd[:, NMETA + j * GCH:NMETA + (j + 1) * GCH], ps[CUM][:, j * GCH:(j + 1) * GCH], ACT.Exp,
                                             scale=-1.0, bias=bend[:, j:j + 1])
                    nc.scalar.activation(kd[:, 0:NMETA], ps[MISC][:, 0:NMETA], ACT.Exp, scale=-1.0, bias=bend[:, NCH:NCH + 1])
                    nc.scalar.activation(cdg[:, par, :], bend[:, 0:NCH], ACT.Exp).then_inc(exp_done, 1)
                elif kind == "fold":
                    act.wait_ge(kt_ready, h + 1)
                    if h >= 1:
                        act.wait_ge(cs_ready, (NCH + 1) * h)
                    nc.scalar.copy(kt_[:, :, :].rearrange("p c d -> p (c d)"), ps[CUM][:, :])
                    nc.scalar.copy(ktm[:, :], ps[MISC][0:NMETA, 0:DK]).then_inc(kt_copied, 1)
                elif kind == "chunk":
                    t = h * TILES + c
                    act.wait_ge(o_ready, t + 1)
                    nc.scalar.copy(k.o[:, c, h * DV:(h + 1) * DV], ps[O][:, 0:DV]).then_inc(o_copied, 1)

        @block.vector
        def _(dve):
            nc.vector.memset(glrT[:, :], 1.0).then_inc(ones_set, 1)
            nc.vector.memset(att[:, :, :], 0.0)
            k.vlink(dve, nc.vector.memset(qa[:, :, :, :, :], 0.0))
            dve.wait_ge(gk_ln, 1)
            parts = [(gk[:, c, :], ps[CUM + c][:, :]) for c in range(TILES)]
            parts += [(gkm[:, :], ps[MISC][0:NMETA, :]), (gks[:, :, :].rearrange("p h b -> p (h b)"), ps[SMALL][:, 0:GH * NSAMP])]
            for dst, src in parts:
                last = nc.vector.scalar_tensor_tensor(dst, src, 0.0, dst, ALU.min, ALU.subtract)
            last.then_inc(gk_done, 1)
            for kind, h, c in order:
                par = h % 2
                if kind == "prep":
                    dve.wait_ge(cum_ready, h + 1)
                    if h >= 1:
                        dve.wait_ge(exp_done, h)
                    nc.vector.tensor_copy(bend[:, 0:NCH], ps[CUM][:, GCH - 1:SEQ:GCH])
                    nc.vector.tensor_copy(bend[:, NCH:NCH + 1], ps[MISC][:, NMETA - 1:NMETA]).then_inc(bend_done, 1)
                    dve.wait_ge(exp_done, h + 1)
                    dve.wait_ge(proj_evac, h * NP + 2)
                    nc.vector.tensor_tensor(ke[:, :], kT[:, par, NMETA:NMETA + SEQ], ke[:, :], ALU.mult).then_inc(ke_done, 1)
                elif kind == "fold":
                    dve.wait_ge(att_ready, h + 1)
                    if h >= 1:
                        dve.wait_ge(o_ready, TILES * h)
                    nc.vector.copy_predicated(att[:, :, :], k.att_mask[:, :].unsqueeze(1).to_broadcast([P, TILES, P]),
                                              ps[ATT][:, :].rearrange("p (c t) -> p c t", c=TILES)).then_inc(att_done, 1)
                    dve.wait_ge(cs_ready, (NCH + 1) * h + 1)
                    if h >= 2:
                        dve.wait_ge(st_out, 16 * (h - 1))
                    nc.vector.tensor_copy(st[:, par, 0, :], ps[CS][:, 0:DV]).then_inc(st_done, 1)
                elif kind == "chunk":
                    for half in range(2):
                        j = 2 * c + half
                        dve.wait_ge(cs_ready, (NCH + 1) * h + j + 2)
                        dve.wait_ge(st_done, (NCH + 1) * h + j + 1)
                        nc.vector.scalar_tensor_tensor(st[:, par, (j + 1) % 2, :], st[:, par, j % 2, :], cdg[:, par, j:j + 1],
                                                       ps[CS][:, 0:DV], ALU.mult, ALU.add).then_inc(st_done, 1)
                elif kind == "sample":
                    dve.wait_ge(proj_evac, h * NP + 2)
                    if h >= 1:
                        dve.wait_ge(os_ready, h)
                    nc.vector.tensor_tensor(qmask[:, :, :], k.eye8[:, :, :], qs[:, par, :].unsqueeze(1).to_broadcast([P, NSAMP, NSAMP]),
                                            ALU.mult).then_inc(qm_done, 1)
                    for b in range(NSAMP):
                        q = h * NSAMP + b
                        dve.wait_ge(sdec_done, q + 1)
                        dve.wait_ge(sv_ready, q + 1)
                        nc.vector.scalar_tensor_tensor(gs[:, b, :], ps[(CUM, ATT)[b % 2]][:, 0:DV], ks[:, par, b:b + 1],
                                                       gs[:, b, :], ALU.mult, ALU.add).then_inc(gs_done, 1)
                    dve.wait_ge(os_ready, h + 1)
                    nc.vector.tensor_copy(k.os[:, h * DV:(h + 1) * DV], ps[MISC][0:NSAMP, 0:DV]).then_inc(os_done, 1)

        @block.gpsimd
        def _(pool):
            pool.wait_ge(gs_exp, 1)
            for kind, h, c in order:
                par = h % 2
                if kind == "prep":
                    pool.wait_ge(exp_done, h + 1)
                    pool.wait_ge(proj_evac, h * NP + 2)
                    if h >= 2:
                        pool.wait_ge(os_done, h - 1)
                    nc.gpsimd.tensor_tensor(qa[:, par, :, 0:4:3, :], qT[:, par, :].rearrange("p (c a t) -> p c a t", c=TILES, a=2),
                                            ep[:, :].rearrange("p (c a t) -> p c a t", c=TILES, a=2), ALU.mult).then_inc(qa_done, 1)
                    nc.gpsimd.tensor_tensor(kd[:, :], kT[:, par, :], kd[:, :], ALU.mult).then_inc(kd_done, 1)
                elif kind == "fold":
                    pool.wait_ge(gs_here, 16 * (h + 1))
                    for b in range(NSAMP):
                        nc.gpsimd.tensor_scalar(gs[:, b, :], gs[:, b, :], gks[:, h, b:b + 1], None, ALU.mult).then_inc(sdec_done, 1)


def stage_gate(nc, k):
    TOKENS = TILES + 1
    z_items = [("z", g, c) for g in range(GROUPS) for c in range(TOKENS)]
    g_items = [("g", i, c) for i in range(2) for c in range(TOKENS)]
    y_turns = [(c, g) for c in range(TOKENS) for g in range(GROUPS)]
    o_turns = [(c, i) for c in range(TOKENS) for i in range(2)]
    NZ, NG = len(z_items), len(g_items)
    rows = [P] * TILES + [NSAMP]
    cols = lambda c: tile_cols(c) if c < TILES else slice(0, NSAMP)
    out_cols = lambda c: slice(c * P, c * P + rows[c])
    BANKS, BUFS = 4, 3
    with ExitStack() as ctx:
        sb = lambda n, s, d=F32: ctx.enter_context(nc.sbuf_tensor("t_" + n, s, d, side="right"))
        sem = lambda n: k.sem("t_" + n)
        gate = sb("gate", [P, BUFS, 512])
        ssy = sb("ssy", [P, TOKENS, GROUPS])
        sso = sb("sso", [P, TOKENS, GH])
        wy = sb("wy", [P, GROUPS * 4])
        wo = sb("wo", [P, KD])
        ins_here, item_ready, item_gated, mul_done, sq_done, zero_done = map(sem, ("ins_here", "item_ready", "item_gated", "mul_done", "sq_done", "zero_done"))
        osq_done, mean_done, root_done, ynorm_done, turn_ready, turn_done = map(
            sem, ("osq_done", "mean_done", "root_done", "ynorm_done", "turn_ready", "turn_done"))
        k.block_used.update({FIRST["z"] + g: (item_ready, TOKENS * (g + 1)) for g in range(GROUPS)})
        k.block_used.update({FIRST["g"] + i: (item_ready, NZ + TOKENS * (i + 1)) for i in range(2)})
        ps = k.ps
        y_of = lambda c, g: (k.y[:, c, g * GW:(g + 1) * GW] if c < TILES else k.ys[:, g * GW:(g + 1) * GW])
        o_of = lambda c, h: (k.o[:, c, h * DV:(h + 1) * DV] if c < TILES else k.os[:, h * DV:(h + 1) * DV])
        turns = [("y", c, g) for c, g in y_turns] + [("o", c, i) for c, i in o_turns]
        block = ctx.enter_context(nc.Block())

        @block.sync
        def _(sp):
            for dst, src in ((wy[:, :], k.dram["ssd_norm"]), (wo[:, :], k.dram["gla_norm"])):
                sp.dma_start(dst, src).then_inc(ins_here, 16)
            for b in range(FIRST["z"], FIRST["merge"]):
                load_block(sp, k, b + 2)

        @block.tensor
        def _(pe):
            def project(n, kind, i, c):
                b = FIRST[kind] + i
                if c == 0:
                    wait_block(pe, k, b)
                if n >= BANKS:
                    pe.wait_ge(item_gated, n - BANKS + 1)
                w = k.ring[b % 2][:, 0:KD * 512].rearrange("p (k c) -> p k c", k=KD)
                for kt in range(KD):
                    last = nc.tensor.matmul(ps[n % BANKS][0:rows[c], :], k.xnT[:, kt, cols(c)], w[:, kt, :], start=kt == 0, stop=kt == KD - 1)
                last.then_inc(item_ready, 1)

            def turn(m):
                kind, c, i = turns[m]
                if kind == "y":
                    pe.wait_ge(ynorm_done, m + 1)
                elif i == 0 and c == 0:
                    pe.wait_ge(mul_done, NZ + NG)
                if m >= 2:
                    pe.wait_ge(turn_done, m - 1)
                for a in range(4):
                    src = y_of(c, i)[:, a * P:(a + 1) * P] if kind == "y" else o_of(c, 2 * i + a // 2)[:, (a % 2) * P:(a % 2 + 1) * P]
                    last = nc.tensor.transpose(ps[BANKS + m % 2][:, a * P:a * P + rows[c]], src, k.ident[0:rows[c], 0:rows[c]])
                last.then_inc(turn_ready, 1)

            for n, item in enumerate(z_items):
                project(n, *item)
            for j, item in enumerate(g_items):
                project(NZ + j, *item)
                turn(2 * j)
                turn(2 * j + 1)
            for m in range(2 * NG, len(turns)):
                turn(m)

        @block.scalar
        def _(act):
            act.wait_ge(zero_done, 1)
            for c in range(TOKENS):
                for h in range(GH):
                    at = (c * GH + h) * DV
                    last = nc.scalar.activation(k.yT[0:rows[c], :, :].rearrange("p a b -> p (a b)")[:, at:at + DV], o_of(c, h),
                                                ACT.Square, accum_out=sso[0:rows[c], c, h:h + 1])
            last.then_inc(osq_done, 1)

            def square(n):
                _, g, c = z_items[n]
                act.wait_ge(mul_done, n + 1)
                nc.scalar.activation(gate[0:rows[c], n % BUFS, :], y_of(c, g), ACT.Square, accum_out=ssy[0:rows[c], c, g:g + 1]).then_inc(sq_done, 1)

            for n, (kind, g, c) in enumerate(z_items + g_items):
                act.wait_ge(item_ready, n + 1)
                if n >= BUFS:
                    act.wait_ge(mul_done, n - BUFS + 1)
                    act.wait_ge(sq_done, min(n - BUFS + 1, NZ))
                nc.scalar.activation(gate[0:rows[c], n % BUFS, :], ps[n % BANKS][0:rows[c], :], ACT.Silu).then_inc(item_gated, 1)
                if 1 <= n < NZ:
                    square(n - 1)
                if n == NZ - 1:
                    square(n)
                    act.wait_ge(mean_done, 1)
                    nc.scalar.activation(ssy[:, :, :], ssy[:, :, :], ACT.Sqrt)
                    nc.scalar.activation(sso[:, :, :], sso[:, :, :], ACT.Sqrt).then_inc(root_done, 1)

        @block.vector
        def _(dve):
            nc.vector.memset(ssy[:, :, :], 1.0)
            nc.vector.memset(sso[:, :, :], 1.0).then_inc(zero_done, 1)
            dve.wait_ge(ins_here, 32)
            for n, (_, g, c) in enumerate(z_items):
                dve.wait_ge(item_gated, n + 1)
                nc.vector.tensor_tensor(y_of(c, g), y_of(c, g), gate[0:rows[c], n % BUFS, :], ALU.mult).then_inc(mul_done, 1)
            dve.wait_ge(sq_done, NZ)
            dve.wait_ge(osq_done, 1)
            nc.vector.tensor_scalar(ssy[:, :, :], ssy[:, :, :], 1.0 / GW, EPS, ALU.mult, ALU.add)
            nc.vector.tensor_scalar(sso[:, :, :], sso[:, :, :], 1.0 / DV, EPS, ALU.mult, ALU.add).then_inc(mean_done, 1)
            dve.wait_ge(root_done, 1)
            nc.vector.reciprocal(ssy[:, :, :], ssy[:, :, :])
            k.vlink(dve, nc.vector.reciprocal(sso[:, :, :], sso[:, :, :]))
            for c, g in y_turns:
                nc.vector.tensor_scalar(y_of(c, g), y_of(c, g), ssy[0:rows[c], c, g:g + 1], None, ALU.mult).then_inc(ynorm_done, 1)

            def turn(m):
                kind, c, i = turns[m]
                dve.wait_ge(turn_ready, m + 1)
                w, dst = (wy, k.yT) if kind == "y" else (wo, k.oT)
                nc.vector.tensor_tensor(dst[:, 4 * i:4 * i + 4, out_cols(c)],
                                        ps[BANKS + m % 2][:, :].rearrange("p (a t) -> p a t", a=4)[:, :, 0:rows[c]],
                                        w[:, 4 * i:4 * i + 4].unsqueeze(2).to_broadcast([P, 4, rows[c]]), ALU.mult).then_inc(turn_done, 1)

            for j, (_, i, c) in enumerate(g_items):
                n = NZ + j
                dve.wait_ge(item_gated, n + 1)
                for a in range(2):
                    h = 2 * i + a
                    last = nc.vector.scalar_tensor_tensor(o_of(c, h), o_of(c, h), sso[0:rows[c], c, h:h + 1],
                                                          gate[0:rows[c], n % BUFS, a * DV:(a + 1) * DV], ALU.mult, ALU.mult)
                last.then_inc(mul_done, 1)
                turn(2 * j)
                turn(2 * j + 1)
            for m in range(2 * NG, len(turns)):
                turn(m)


TOK = SEQ + NSAMP


def stage_merge(nc, k):
    KY = GROUPS * GW // P
    MAINS = 6
    with ExitStack() as ctx:
        sb = lambda n, s, d=F32: ctx.enter_context(nc.sbuf_tensor("m_" + n, s, d, side="right"))
        sem = lambda n: k.sem("m_" + n)
        sig = sb("sig", [P, 2, 2, TOK])
        term = sb("term", [P, 2, TOK])
        main_ready, small_ready, sig_done, ssig_done, out_done, sout_done = map(
            sem, ("main_ready", "small_ready", "sig_done", "ssig_done", "out_done", "sout_done"))
        k.block_used.update({FIRST["merge"] + j: (small_ready, j + 1) for j in range(KD)})
        ps = k.ps
        block = ctx.enter_context(nc.Block())

        @block.sync
        def _(sp):
            for b in range(FIRST["merge"], FIRST["out"]):
                load_block(sp, k, b + 2)

        @block.tensor
        def _(pe):
            for j in range(KD):
                b = FIRST["merge"] + j
                wait_block(pe, k, b)
                w = k.ring[b % 2][:, 0:(3 * KD + KY) * P].rearrange("p (k c) -> p k c", c=P)
                parts = [(0, KD, k.xnT, SM, 0), (KD, KD, k.xnT, SM, 0), (2 * KD, KY, k.yT, 0, SEQ), (2 * KD + KY, KD, k.oT, 0, SEQ)]
                for i, (k0, n_k, src, at, _) in enumerate(parts):
                    n = 4 * j + i
                    if n >= MAINS:
                        if i < 2:
                            pe.wait_ge(out_done, 2 * (j - 2) + i + 1)
                        else:
                            pe.wait_ge(sig_done, 2 * (j - 1) + i - 1)
                    for kt in range(n_k):
                        last = nc.tensor.matmul(ps[n % MAINS][:, :], w[:, k0 + kt, :], src[:, kt, at:at + SEQ], start=kt == 0, stop=kt == n_k - 1)
                    last.then_inc(main_ready, 1)
                if j >= 2:
                    pe.wait_ge(sout_done, j - 1)
                for i, (k0, n_k, src, _, at) in enumerate(parts):
                    for kt in range(n_k):
                        last = nc.tensor.matmul(ps[MAINS + j % 2][:, i * NSAMP:(i + 1) * NSAMP], w[:, k0 + kt, :], src[:, kt, at:at + NSAMP],
                                                start=kt == 0, stop=kt == n_k - 1)
                last.then_inc(small_ready, 1)

        @block.scalar
        def _(act):
            for j in range(KD):
                for i in range(2):
                    n = 4 * j + i
                    act.wait_ge(main_ready, n + 1)
                    if j >= 2:
                        act.wait_ge(sout_done, j - 1)
                    nc.scalar.activation(sig[:, j % 2, i, 0:SEQ], ps[n % MAINS][:, :], ACT.Sigmoid).then_inc(sig_done, 1)
                act.wait_ge(small_ready, j + 1)
                nc.scalar.activation(sig[:, j % 2, :, SEQ:TOK], ps[MAINS + j % 2][:, 0:2 * NSAMP].rearrange("p (i b) -> p i b", i=2),
                                     ACT.Sigmoid).then_inc(ssig_done, 1)

        @block.vector
        def _(dve):
            for j in range(KD):
                for i in range(2):
                    n = 4 * j + 2 + i
                    dve.wait_ge(main_ready, n + 1)
                    dve.wait_ge(sig_done, 2 * j + i + 1)
                    dst = k.mixT[:, j, 0:SEQ] if i == 0 else term[:, j % 2, 0:SEQ]
                    nc.vector.tensor_tensor(dst, ps[n % MAINS][:, :], sig[:, j % 2, i, 0:SEQ], ALU.mult).then_inc(out_done, 1)
                dve.wait_ge(ssig_done, j + 1)
                small = ps[MAINS + j % 2]
                nc.vector.tensor_tensor(k.mixT[:, j, SEQ:TOK], small[:, 2 * NSAMP:3 * NSAMP], sig[:, j % 2, 0, SEQ:TOK], ALU.mult)
                k.vlink(dve, nc.vector.tensor_tensor(term[:, j % 2, SEQ:TOK], small[:, 3 * NSAMP:4 * NSAMP], sig[:, j % 2, 1, SEQ:TOK], ALU.mult))
                dve.wait_ge(out_done, 2 * j + 2)
                nc.vector.tensor_tensor(k.mixT[:, j, :], k.mixT[:, j, :], term[:, j % 2, :], ALU.add).then_inc(sout_done, 1)


def stage_query(nc, k):
    TOKENS = TILES + 1
    NQ = 2 * EH
    rows = [P] * TILES + [NSAMP]
    mix_cols = lambda c: slice(c * P, c * P + rows[c])
    BANKS = 4
    with ExitStack() as ctx:
        sb = lambda n, s, d=F32: ctx.enter_context(nc.sbuf_tensor("q_" + n, s, d, side="right"))
        sem = lambda n: k.sem("q_" + n)
        qT = sb("qT", [P, KD, TOK])
        ss = sb("ss", [P, TOKENS])
        hnT = k.xnT
        keys = k.ring[0][:, KD * 512:KD * 512 + NQ * NKEYS].rearrange("p (q n) -> p q n", q=NQ)
        w2 = k.ring[1][:, KD * 512:KD * 512 + D]
        x_here, ins_here, out_ready, x1_done, sq_done, mean_done, root_done = map(
            sem, ("x_here", "ins_here", "out_ready", "x1_done", "sq_done", "mean_done", "root_done"))
        hn_done, turn_ready, turn_done, q_ready, q_done, sc_ready, sc_done = map(
            sem, ("hn_done", "turn_ready", "turn_done", "q_ready", "q_done", "sc_ready", "sc_done"))
        k.block_used.update({FIRST["out"] + i: (out_ready, TOKENS * (i + 1)) for i in range(2)})
        k.block_used.update({FIRST["query"] + i: (q_ready, 4 * (i + 1)) for i in range(4)})
        ps = k.ps
        q_of = lambda m: (qT if m < KD else k.mixT)[:, m % KD, :]
        block = ctx.enter_context(nc.Block())

        @block.sync
        def _(sp):
            for c in range(TOKENS):
                lo = SM + c * P if c < TILES else 0
                sp.dma_start(k.x1[0:rows[c], c, :], k.dram["x_all"][lo:lo + rows[c], :]).then_inc(x_here, 16)
            for dst, src in ((keys, k.dram["keys"]), (w2, k.dram["norm2"])):
                sp.dma_start(dst, src).then_inc(ins_here, 16)
            for b in range(FIRST["out"], len(BLOCKS)):
                load_block(sp, k, b + 2)

        @block.tensor
        def _(pe):
            for i in range(2):
                b = FIRST["out"] + i
                wait_block(pe, k, b)
                w = k.ring[b % 2][:, 0:KD * 512].rearrange("p (k c) -> p k c", k=KD)
                for c in range(TOKENS):
                    n = i * TOKENS + c
                    if n >= BANKS:
                        pe.wait_ge(x1_done, n - BANKS + 1)
                    for kt in range(KD):
                        last = nc.tensor.matmul(ps[n % BANKS][0:rows[c], :], k.mixT[:, kt, mix_cols(c)], w[:, kt, :], start=kt == 0, stop=kt == KD - 1)
                    last.then_inc(out_ready, 1)
            for c in range(TOKENS):
                pe.wait_ge(hn_done, c + 1)
                for half in range(2):
                    m = 2 * c + half
                    if m >= 2:
                        pe.wait_ge(turn_done, m - 1)
                    for a in range(4):
                        kt = 4 * half + a
                        last = nc.tensor.transpose(ps[4 + m % 2][:, a * P:a * P + rows[c]], k.hn[0:rows[c], c, kt * P:(kt + 1) * P],
                                                   k.ident[0:rows[c], 0:rows[c]])
                    last.then_inc(turn_ready, 1)
            pe.wait_ge(turn_done, 2 * TOKENS)
            for m in range(NQ):
                b = FIRST["query"] + m // 4
                if m % 4 == 0:
                    wait_block(pe, k, b)
                w = k.ring[b % 2][:, 0:KD * 512].rearrange("p (k c) -> p k c", k=KD)
                if m >= 2:
                    pe.wait_ge(q_done, m - 1)
                for part, bank, cols in ((0, m % 2, slice(SM, COLS)), (1, 2 + m % 2, slice(0, NSAMP))):
                    for kt in range(KD):
                        last = nc.tensor.matmul(ps[bank][:, 0:cols.stop - cols.start], w[:, kt, (m % 4) * P:(m % 4 + 1) * P], hnT[:, kt, cols],
                                                start=kt == 0, stop=kt == KD - 1)
                last.then_inc(q_ready, 1)
            pe.wait_ge(q_done, NQ)
            pe.wait_ge(ins_here, 32)
            for c in range(TOKENS):
                for quad in range(4):
                    n = 4 * c + quad
                    if n >= 4:
                        pe.wait_ge(sc_done, n - 3)
                    for a in range(4):
                        m = 4 * quad + a
                        last = nc.tensor.matmul(ps[4 + n % 4][0:rows[c], a * NKEYS:(a + 1) * NKEYS], q_of(m)[:, mix_cols(c)], keys[:, m, :], start=True, stop=True)
                    last.then_inc(sc_ready, 1)

        @block.vector
        def _(dve):
            dve.wait_ge(x_here, 16 * TOKENS)
            for i in range(2):
                for c in range(TOKENS):
                    n = i * TOKENS + c
                    dve.wait_ge(out_ready, n + 1)
                    v = k.x1[0:rows[c], c, i * 512:(i + 1) * 512]
                    nc.vector.tensor_tensor(v, v, ps[n % BANKS][0:rows[c], :], ALU.add).then_inc(x1_done, 1)
            dve.wait_ge(ins_here, 32)
            dve.wait_ge(sq_done, 1)
            for c in range(TOKENS):
                last = nc.vector.tensor_scalar(ss[0:rows[c], c:c + 1], ss[0:rows[c], c:c + 1], 1.0 / D, EPS, ALU.mult, ALU.add)
            last.then_inc(mean_done, 1)
            dve.wait_ge(root_done, 1)
            for c in range(TOKENS):
                last = nc.vector.reciprocal(ss[0:rows[c], c:c + 1], ss[0:rows[c], c:c + 1])
            k.vlink(dve, last)
            for c in range(TOKENS):
                nc.vector.scalar_tensor_tensor(k.hn[0:rows[c], c, :], k.x1[0:rows[c], c, :], ss[0:rows[c], c:c + 1], w2[0:rows[c], :],
                                               ALU.mult, ALU.mult).then_inc(hn_done, 1)

        @block.scalar
        def _(act):
            for c in range(TOKENS):
                act.wait_ge(x1_done, TOKENS + c + 1)
                last = nc.scalar.activation(k.hn[0:rows[c], c, :], k.x1[0:rows[c], c, :], ACT.Square, accum_out=ss[0:rows[c], c:c + 1])
            last.then_inc(sq_done, 1)
            act.wait_ge(mean_done, 1)
            for c in range(TOKENS):
                last = nc.scalar.activation(ss[0:rows[c], c:c + 1], ss[0:rows[c], c:c + 1], ACT.Sqrt)
            last.then_inc(root_done, 1)
            for m in range(2 * TOKENS):
                c, half = divmod(m, 2)
                lo = SM + c * P if c < TILES else 0
                act.wait_ge(turn_ready, m + 1)
                nc.scalar.copy(hnT[:, 4 * half:4 * half + 4, lo:lo + rows[c]],
                               ps[4 + m % 2][:, :].rearrange("p (a t) -> p a t", a=4)[:, :, 0:rows[c]]).then_inc(turn_done, 1)
            for m in range(NQ):
                act.wait_ge(q_ready, m + 1)
                nc.scalar.copy(q_of(m)[:, 0:SEQ], ps[m % 2][:, :])
                nc.scalar.copy(q_of(m)[:, SEQ:TOK], ps[2 + m % 2][:, 0:NSAMP]).then_inc(q_done, 1)
            for n in range(4 * TOKENS):
                c, quad = divmod(n, 4)
                act.wait_ge(sc_ready, n + 1)
                dst = k.sc[:, c * EH + 2 * quad:c * EH + 2 * quad + 2, :] if c < TILES else k.ssc[:, 2 * quad:2 * quad + 2, :]
                nc.scalar.copy(dst.rearrange("p h n -> p (h n)"), ps[4 + n % 4][0:rows[c], :]).then_inc(sc_done, 1)


def stage_peer(nc, k):
    UNITS = TILES * EH
    RING = 8
    LOT = 8
    PAIR = 2
    DIAGS = 4
    PARTS_AFTER = (1, 3, 5, 6)
    SROWS = NSAMP * EH
    SLOTS = TOPK
    LOW = -3.4e38
    with ExitStack() as ctx:
        sb = lambda n, s, d=F32, side="left": ctx.enter_context(nc.sbuf_tensor("p_" + n, s, d, side=side))
        sem = lambda n: k.sem("p_" + n)
        rows = sb("rows", [P, RING, ROW])
        wf = sb("wf", [P, D])
        hn_cur = sb("hn_cur", [P, D])
        idx = sb("idx", [P, (UNITS + 2) * SLOTS], U32)
        gates = sb("gates", [P, (UNITS + 2) * SLOTS])
        sidx = sb("sidx", [SROWS, SLOTS], U32)
        sgates = sb("sgates", [SROWS, SLOTS])
        ssc = sb("ssc", [SROWS, 1, 2 * NKEYS])
        shn = sb("shn", [NSAMP, D])
        ssel = sb("ssel", [SROWS, NSAMP])
        ssel_t = sb("ssel_t", [NSAMP, SROWS])
        lot = sb("lot", [P, 2, LOT], U32)
        hid = sb("hid", [P, SLOTS])
        gel = sb("gel", [P, SLOTS])
        diag = sb("diag", [P, DIAGS, P])
        zeros = sb("zeros", [P, 512])
        fin = sb("fin", [P, D])
        sfin = sb("sfin", [NSAMP, D])
        squares = sb("squares", [P, D])
        fss = sb("fss", [P, 2])
        tv = sb("tv", [P, 2, TOPK])
        ti = sb("ti", [P, 2, TOPK], U32)
        tif = sb("tif", [P, 2, TOPK])
        rest = sb("rest", [P, 2, NKEYS])
        cand = sb("cand", [P, TOPK, TOPK])
        crest = sb("crest", [P, TOPK, TOPK])
        bv = sb("bv", [P, TOPK])
        bp = sb("bp", [P, TOPK], U32)
        ab = sb("ab", [P, 2, TOPK], U32)
        abf = sb("abf", [P, 2, TOPK])
        hot = sb("hot", [P, 2, TOPK, TOPK])
        pick = sb("pick", [P, 2, TOPK])
        pickf = sb("pickf", [P, TOPK])
        iota = sb("iota", [P, TOPK])
        scu = sb("scu", [P, 2 * NKEYS])
        nmax = sb("nmax", [P, 1])
        ex = sb("ex", [P, TOPK])
        esum = sb("esum", [P, 1])
        ins_here, ready, lot_here, dot_done, gelu_done, diag_done, used = map(
            sem, ("ins_here", "ready", "lot_here", "dot_done", "gelu_done", "diag_done", "used"))
        row_here = [sem(f"row_here{j}") for j in range(RING)]
        choice, best_done, exp_done, cleared, hn_rep, hn_cur_done = map(
            sem, ("choice", "best_done", "exp_done", "cleared", "hn_rep", "hn_cur_done"))
        acc_closed, fin_done, fsq_done, fmean, froot, out_ready, out_done, turn = map(
            sem, ("acc_closed", "fin_done", "fsq_done", "fmean", "froot", "out_ready", "out_done", "turn"))
        ps = k.ps
        ACC, SACC, REP = (0, 1), (2, 3), (4, 5)
        CHOICE_STEPS = 21
        block = ctx.enter_context(nc.Block())

        @block.sync
        def _(sp):
            for dst, src in ((ssc[:, 0, :], k.ssc[:, :, :]), (shn[:, :], k.hn[0:NSAMP, TILES, :]), (wf[:, :], k.dram["norm_f"]),
                             (iota[:, :], k.dram["c_iota"]), (ssel[:, :], k.dram["c_ssel"]), (ssel_t[:, :], k.dram["c_ssel_t"])):
                sp.dma_start(dst, src).then_inc(ins_here, 16)
            sp.wait_ge(out_ready, 1)
            sp.dma_start(k.dram["o_sample"], sfin[:, :]).then_inc(out_done, 16)
            with sp.Fori(0, TILES) as c:
                sp.wait_ge(out_ready, c + 2)
                sp.sem_inc(turn, 1)
                sp.dma_start(k.dram["o_prompt"][bass.ds(c * P, P), :], fin[:, :]).then_inc(out_done, 16)
                sp.wait_ge(out_done, c * 16 + 32)
                sp.sem_inc(turn, 1)
            sp.wait_ge(out_done, 16 * (TILES + 1))

        @block.gpsimd
        def _(pool):
            def gathers(m, unit):
                for s in range(SLOTS):
                    if s % LOT == 0:
                        pool.wait_ge(lot_here, unit * 2 + s // LOT + 1)
                        pool.sem_inc(turn, 1)
                    pool.wait_ge(used, unit * SLOTS + s + 1)
                    pool.sem_inc(turn, 1)
                    nc.gpsimd.indirect_dma_start(rows[0:m, s % RING, :], None, k.dram["experts"],
                                                 bass.IndirectOffsetOnAxis(lot[0:m, s // LOT, s % LOT:s % LOT + 1], 0)).then_inc(row_here[s % RING], 16)

            gathers(SROWS, 0)
            with pool.Fori(0, UNITS) as i:
                gathers(P, i + 1)

        @block.vector
        def _(dve):
            def choice_parts(m, sc, idx_out, gates_out, turn_no):
                count = [0]

                def link(ins):
                    count[0] += 1
                    ins.then_inc(choice, 1)
                    dve.wait_ge(choice, turn_no * CHOICE_STEPS + count[0])
                    dve.sem_inc(turn, 1)

                def best16(values, rest_, top, where):
                    link(nc.vector.max(top[:, 0:8], values))
                    nc.vector.max_index(where[:, 0:8], top[:, 0:8], values)
                    link(nc.vector.match_replace(rest_, top[:, 0:8], values, LOW))
                    link(nc.vector.max(top[:, 8:16], rest_))
                    nc.vector.max_index(where[:, 8:16], top[:, 8:16], rest_)

                flat = lambda t: t[0:m, :, :].rearrange("p a b -> p (a b)")
                grid = [m, TOPK, TOPK]

                def keys(s):
                    best16(scu[0:m, s * NKEYS:(s + 1) * NKEYS], rest[0:m, s, :], tv[0:m, s, :], ti[0:m, s, :])

                def part0():
                    link(nc.vector.tensor_copy(scu[0:m, :], sc))
                    keys(0)

                def part1():
                    keys(1)

                def part2():
                    link(nc.vector.tensor_tensor(cand[0:m], tv[0:m, 0, :].unsqueeze(2).to_broadcast(grid), tv[0:m, 1, :].unsqueeze(1).to_broadcast(grid), ALU.add))
                    nc.vector.tensor_copy(tif[0:m], ti[0:m])
                    link(nc.vector.max(bv[0:m, 0:8], flat(cand)))
                    nc.vector.max_index(bp[0:m, 0:8], bv[0:m, 0:8], flat(cand))
                    link(nc.vector.match_replace(flat(crest), bv[0:m, 0:8], flat(cand), LOW))
                    link(nc.vector.max(bv[0:m, 8:16], flat(crest)))
                    nc.vector.tensor_scalar(nmax[0:m], bv[0:m, 0:1], -1.0, None, ALU.mult).then_inc(best_done, 1)
                    link(nc.vector.max_index(bp[0:m, 8:16], bv[0:m, 8:16], flat(crest)))

                def part3():
                    nc.vector.tensor_scalar(ab[0:m, 0, :], bp[0:m], 4, None, ALU.logical_shift_right)
                    link(nc.vector.tensor_scalar(ab[0:m, 1, :], bp[0:m], 15, None, ALU.bitwise_and))
                    link(nc.vector.tensor_copy(abf[0:m], ab[0:m]))
                    for s in range(2):
                        last = nc.vector.tensor_tensor(hot[0:m, s], abf[0:m, s, :].unsqueeze(2).to_broadcast(grid),
                                                       iota[0:m, :].unsqueeze(1).to_broadcast(grid), ALU.is_equal)
                    link(last)
                    for s in range(2):
                        last = nc.vector.tensor_tensor(hot[0:m, s], hot[0:m, s], tif[0:m, s, :].unsqueeze(1).to_broadcast(grid), ALU.mult)
                    link(last)
                    link(nc.vector.tensor_reduce(pick[0:m], hot[0:m], AX.X, ALU.add))
                    link(nc.vector.scalar_tensor_tensor(pickf[0:m], pick[0:m, 0, :], float(NKEYS), pick[0:m, 1, :], ALU.mult, ALU.add))
                    link(nc.vector.tensor_copy(idx_out, pickf[0:m]))
                    dve.wait_ge(exp_done, turn_no + 1)
                    link(nc.vector.reciprocal(esum[0:m], esum[0:m]))
                    link(nc.vector.tensor_scalar(gates_out, ex[0:m], esum[0:m], None, ALU.mult))
                    assert count[0] == CHOICE_STEPS, count[0]

                return part0, part1, part2, part3

            def choose(*of):
                for part in choice_parts(*of):
                    part()

            def stage_lot(m, src, half):
                nc.vector.tensor_copy(lot[0:m, half, :], src).then_inc(lot_here, 1)

            def diags(m, width, ident, unit, pair, gate):
                dve.wait_ge(gelu_done, unit * (SLOTS // PAIR) + pair + 1)
                for s in range(PAIR * pair, PAIR * pair + PAIR):
                    dve.wait_ge(used, RING + unit * SLOTS + s - DIAGS + 1)
                    nc.vector.tensor_scalar(diag[0:m, s % DIAGS, 0:width], ident, gel[0:m, s:s + 1], gate(s), ALU.mult, ALU.mult).then_inc(diag_done, 1)

            def unit_slots(m, width, ident, hn, unit, gate, next_lots, parts):
                for pair in range(SLOTS // PAIR):
                    for s in range(PAIR * pair, PAIR * pair + PAIR):
                        dve.wait_ge(row_here[s % RING], unit * 16 * (SLOTS // RING) + 16 * (s // RING + 1))
                        u = rows[0:m, s % RING, 0:D]
                        nc.vector.tensor_tensor_reduce(out=u, in0=u, in1=hn, scale=1.0, scalar=0.0, op0=ALU.mult, op1=ALU.add,
                                                       accum_out=hid[0:m, s:s + 1]).then_inc(dot_done, 1)
                    if (pair * PAIR + PAIR) % LOT == 0:
                        half = pair * PAIR // LOT
                        stage_lot(P, next_lots(half), half)
                    if pair >= 1:
                        diags(m, width, ident, unit, pair - 1, gate)
                    if pair in PARTS_AFTER:
                        parts[PARTS_AFTER.index(pair)]()
                diags(m, width, ident, unit, SLOTS // PAIR - 1, gate)

            def last_norm(m, x1, bank, out, j, n):
                dve.wait_ge(acc_closed, n + 1)
                for half in range(2):
                    cs = slice(half * 512, half * 512 + 512)
                    last = nc.vector.tensor_tensor(out[:, cs], x1[:, cs], ps[bank[half]][0:m, :], ALU.add)
                last.then_inc(fin_done, 1)
                dve.wait_ge(fsq_done, n + 1)
                nc.vector.tensor_scalar(fss[0:m, j:j + 1], fss[0:m, j:j + 1], 1.0 / D, EPS, ALU.mult, ALU.add).then_inc(fmean, 1)
                dve.wait_ge(froot, n + 1)
                nc.vector.reciprocal(fss[0:m, j:j + 1], fss[0:m, j:j + 1]).then_inc(cleared, 1)
                dve.wait_ge(cleared, n + 1)
                nc.vector.scalar_tensor_tensor(out, out, fss[0:m, j:j + 1], wf[0:m, :], ALU.mult, ALU.mult).then_inc(out_ready, 1)

            nc.vector.memset(zeros[:, :], 0.0)
            nc.vector.memset(k.sc[:, UNITS:UNITS + 2, :], 0.0).then_inc(ready, 1)
            dve.wait_ge(ready, 1)
            dve.wait_ge(ins_here, 16 * 6)
            unit_of = lambda t, i: t[:, bass.ds(i * SLOTS, SLOTS)]
            choose(SROWS, ssc[:, 0, :], sidx[:, :], sgates[:, :], 0)
            for half in range(2):
                stage_lot(SROWS, sidx[:, half * LOT:(half + 1) * LOT], half)
            choose(P, k.sc[:, 0, :], idx[:, 0:SLOTS], gates[:, 0:SLOTS], 1)
            dve.wait_ge(hn_rep, 1)
            for half in range(2):
                last = nc.vector.tensor_copy(hn_cur[0:SROWS, half * 512:half * 512 + 512], ps[REP[half]][0:SROWS, :])
            last.then_inc(hn_cur_done, 1)
            dve.wait_ge(hn_cur_done, 1)
            unit_slots(SROWS, NSAMP, ssel[:, :], hn_cur[0:SROWS, :], 0, lambda s: sgates[:, s:s + 1],
                       lambda half: idx[:, half * LOT:(half + 1) * LOT],
                       choice_parts(P, k.sc[:, 1, :], idx[:, SLOTS:2 * SLOTS], gates[:, SLOTS:2 * SLOTS], 2))
            last_norm(NSAMP, k.x1[0:NSAMP, TILES, :], SACC, sfin[:, :], 0, 0)
            hn_flat = k.hn[:, :, :].rearrange("p c d -> p (c d)")
            x1_flat = k.x1[:, :, :].rearrange("p c d -> p (c d)")
            sc_flat = k.sc[:, :, :].rearrange("p u n -> p (u n)")
            with dve.Fori(0, TILES) as c:
                dve.wait_ge(dot_done, (c * EH + 1) * SLOTS)
                nc.vector.tensor_copy(hn_cur[:, :], hn_flat[:, bass.ds(c * D, D)]).then_inc(hn_cur_done, 1)
                dve.wait_ge(hn_cur_done, c + 2)
                dve.sem_inc(turn, 1)
                with dve.Fori(0, EH) as h:
                    i = c * EH + h
                    unit_slots(P, P, k.ident[:, :], hn_cur[:, :], i + 1, lambda s: gates[:, bass.ds(i * SLOTS + s, 1)],
                               lambda half: idx[:, bass.ds((i + 1) * SLOTS + half * LOT, LOT)],
                               choice_parts(P, sc_flat[:, bass.ds((i + 2) * 2 * NKEYS, 2 * NKEYS)],
                                              unit_of(idx, i + 2), unit_of(gates, i + 2), i + 3))
                dve.wait_ge(out_done, c * 16 + 16)
                last_norm(P, x1_flat[:, bass.ds(c * D, D)], ACC, fin[:, :], 1, c + 1)

        @block.scalar
        def _(act):
            def softmax(m, turn_no):
                act.wait_ge(best_done, turn_no + 1)
                nc.scalar.activation(ex[0:m], bv[0:m], ACT.Exp, bias=nmax[0:m], accum_out=esum[0:m]).then_inc(exp_done, 1)

            def unit_gelus(m, unit, middle):
                for pair in range(SLOTS // PAIR):
                    act.wait_ge(dot_done, unit * SLOTS + PAIR * pair + PAIR)
                    s = slice(PAIR * pair, PAIR * pair + PAIR)
                    nc.scalar.activation(gel[0:m, s], hid[0:m, s], ACT.Gelu).then_inc(gelu_done, 1)
                    if pair == PARTS_AFTER[2]:
                        middle()

            def last_norm(m, out, j, n):
                act.wait_ge(fin_done, n + 1)
                if j == 1:
                    act.wait_ge(froot, n)
                nc.scalar.activation(squares[0:m, :], out, ACT.Square, accum_out=fss[0:m, j:j + 1]).then_inc(fsq_done, 1)
                act.wait_ge(fmean, n + 1)
                nc.scalar.activation(fss[0:m, j:j + 1], fss[0:m, j:j + 1], ACT.Sqrt).then_inc(froot, 1)

            softmax(SROWS, 0)
            softmax(P, 1)
            unit_gelus(SROWS, 0, lambda: softmax(P, 2))
            last_norm(NSAMP, sfin[:, :], 0, 0)
            with act.Fori(0, TILES) as c:
                with act.Fori(0, EH) as h:
                    i = c * EH + h
                    unit_gelus(P, i + 1, lambda: softmax(P, i + 3))
                last_norm(P, fin[:, :], 1, c + 1)

        @block.tensor
        def _(pe):
            def open_sum(banks, m):
                for b in banks:
                    last = nc.tensor.matmul(ps[b][0:m, :], k.ident[:, 0:m], zeros[:, :], start=True, stop=False)
                return last

            def close_sum(banks, m):
                for b in banks:
                    last = nc.tensor.matmul(ps[b][0:m, :], k.ident[:, 0:m], zeros[:, :], start=False, stop=True)
                last.then_inc(acc_closed, 1)

            def unit_sums(m, width, banks, unit):
                for s in range(SLOTS):
                    pe.wait_ge(diag_done, unit * SLOTS + s + 1)
                    for half, b in enumerate(banks):
                        last = nc.tensor.matmul(ps[b][0:width, :], diag[0:m, s % DIAGS, 0:width],
                                                rows[0:m, s % RING, D + half * 512:D + half * 512 + 512], start=False, stop=False)
                    last.then_inc(used, 1)

            pe.wait_ge(ready, 1)
            open_sum(SACC, NSAMP).then_inc(used, RING)
            pe.wait_ge(ins_here, 16 * 6)
            for half, b in enumerate(REP):
                last = nc.tensor.matmul(ps[b][0:SROWS, :], ssel_t[:, :], shn[:, half * 512:half * 512 + 512], start=True, stop=True)
            last.then_inc(hn_rep, 1)
            unit_sums(SROWS, NSAMP, SACC, 0)
            close_sum(SACC, NSAMP)
            with pe.Fori(0, TILES) as c:
                pe.wait_ge(fin_done, c + 1)
                open_sum(ACC, P)
                with pe.Fori(0, EH) as h:
                    unit_sums(P, P, ACC, c * EH + h + 1)
                close_sum(ACC, P)


def build(nc, ins, outs):
    with ExitStack() as ctx:
        k = Shared({**ins, **outs})
        k.sem = lambda n: ctx.enter_context(nc.semaphore(n))
        sb = lambda n, s, d=F32, side="left": ctx.enter_context(nc.sbuf_tensor(n, s, d, side=side))
        k.ps = [ctx.enter_context(nc.psum_tensor(f"bank{i}", [P, 512], F32)) for i in range(8)]
        k.vlink, k.alink, k.plink = Link(k.sem("vector_step")), Link(k.sem("scalar_step")), Link(k.sem("pool_step"))
        k.consts_here, k.block_used = k.sem("consts_here"), {}
        k.block_here = [k.sem("block_here0"), k.sem("block_here1")]
        k.ident = sb("ident", [P, P])
        k.tri = sb("tri", [P, P])
        k.tri64 = sb("tri64", [P, P])
        k.ones = sb("ones", [P, P])
        k.identb = sb("identb", [P, P], BF16)
        k.future = sb("future", [P, 4 * P], BF16)
        k.att_mask = sb("att_mask", [P, P], I32)
        k.sel8 = sb("sel8", [NSAMP, NSAMP, P])
        k.diag8 = sb("diag8", [NSAMP, NSAMP])
        k.eye8 = sb("eye8", [P, NSAMP, NSAMP])
        k.const_loads = [(k.ident[:, :], k.dram["c_ident"]), (k.tri[:, :], k.dram["c_tri"]), (k.tri64[:, :], k.dram["c_tri64"]), (k.ones[:, :], k.dram["c_ones"]),
                         (k.identb[:, :], k.dram["c_identb"]), (k.future[:, :], k.dram["c_future"]), (k.att_mask[:, :], k.dram["c_att_mask"]),
                         (k.sel8[:, :, :], k.dram["c_sel8"]), (k.diag8[:, :], k.dram["c_diag8"]), (k.eye8[:, :, :], k.dram["c_eye8"])]
        k.dt = sb("dt", [P, 6, HEADS])
        k.da = sb("da", [P, 6, HEADS])
        k.dte = sb("dte", [P, 5, HEADS])
        k.eac = sb("eac", [P, TILES, HEADS])
        k.cdec = sb("cdec", [P, TILES, HEADS])
        k.nac = sb("nac", [P, TILES, HEADS])
        k.decs = sb("decs", [NSAMP, HEADS])
        k.decb = sb("decb", [P, NSAMP, HEADS])
        base = ExitStack()
        ring = [base.enter_context(nc.sbuf_tensor(f"ring{i}", [P, KD * CT * P], F32, side="left")) for i in range(2)]
        k.ring = ring
        k.xnT = base.enter_context(nc.sbuf_tensor("xnT", [P, KD, COLS], F32, side="left"))
        stage_norm(nc, k)
        top = ExitStack()
        k.y = top.enter_context(nc.sbuf_tensor("y", [P, TILES, GROUPS * GW], F32, side="left"))
        k.ys = top.enter_context(nc.sbuf_tensor("ys", [NSAMP, GROUPS * GW], F32, side="left"))
        stage_ssd(nc, k)
        top2 = ExitStack()
        k.o = top2.enter_context(nc.sbuf_tensor("o", [P, TILES, GH * DV], F32, side="left"))
        k.os = top2.enter_context(nc.sbuf_tensor("os", [NSAMP, GH * DV], F32, side="left"))
        stage_gla(nc, k)
        mid = ExitStack()
        k.yT = mid.enter_context(nc.sbuf_tensor("yT", [P, GROUPS * GW // P, TOK], F32, side="right"))
        k.oT = mid.enter_context(nc.sbuf_tensor("oT", [P, KD, TOK], F32, side="right"))
        stage_gate(nc, k)
        top2.close()
        top.close()
        k.mixT = base.enter_context(nc.sbuf_tensor("mixT", [P, KD, TOK], F32, side="left"))
        stage_merge(nc, k)
        mid.close()
        late = ExitStack()
        k.x1 = late.enter_context(nc.sbuf_tensor("x1", [P, TILES + 1, D], F32, side="right"))
        k.hn = late.enter_context(nc.sbuf_tensor("hn", [P, TILES + 1, D], F32, side="right"))
        k.sc = late.enter_context(nc.sbuf_tensor("sc", [P, TILES * EH + 2, 2 * NKEYS], F32, side="right"))
        k.ssc = late.enter_context(nc.sbuf_tensor("ssc", [NSAMP, EH, 2 * NKEYS], F32, side="right"))
        stage_query(nc, k)
        base.close()
        stage_peer(nc, k)
        late.close()



def _weight_tiles(w, width):
    n_k = w.shape[0] // P
    return np.ascontiguousarray(w.reshape(n_k, P, -1, width).transpose(2, 1, 0, 3).reshape(-1, P, n_k * width))


def _every_partition(row):
    return np.ascontiguousarray(np.broadcast_to(row, (P, row.shape[-1])))


def _channels():
    x, b = np.arange(GW), np.arange(P)
    return np.concatenate([np.concatenate([g * GW + x, GROUPS * GW + g * P + b, GROUPS * (GW + P) + g * P + b]) for g in range(GROUPS)])


def _constants():
    i = np.arange(P)
    upto = (i[:, None] <= i[None, :]).astype(np.float32)
    chunk = i[:, None] // GCH == i[None, :] // GCH
    b = np.arange(NSAMP)
    sel8 = np.zeros((NSAMP, NSAMP, P), np.float32)
    sel8[b, b, :] = 1
    ssel = (np.arange(NSAMP * EH)[:, None] // EH == b[None, :]).astype(np.float32)
    low = np.dtype("bfloat16")
    return dict(
        c_ident=np.eye(P, dtype=np.float32), c_tri=upto, c_tri64=(upto * chunk / 16).astype(np.float32), c_ones=np.ones((P, P), np.float32),
        c_identb=np.eye(P).astype(low), c_future=np.ascontiguousarray(np.tile(np.where(upto > 0, 0.0, -1e30).astype(low), (1, 4))),
        c_att_mask=(upto * chunk).astype(np.int32), c_sel8=sel8, c_diag8=np.eye(NSAMP, dtype=np.float32),
        c_eye8=np.ascontiguousarray(np.broadcast_to(np.eye(NSAMP, dtype=np.float32), (P, NSAMP, NSAMP))),
        c_iota=_every_partition(np.arange(TOPK, dtype=np.float32)), c_ssel=ssel, c_ssel_t=np.ascontiguousarray(ssel.T))


def _inputs(a):
    d_inner, gn = GROUPS * GW, GROUPS * P
    sizes = (d_inner, d_inner + 2 * gn, HEADS, GH * DK, GH * DK, GH * DV, GH * DV, RANK, 2 * D)
    z, xbc, dt, q, key, v, g, glr, merge = np.split(a["w_in"][0], np.cumsum(sizes)[:-1], axis=1)
    ch = _channels()
    conv = np.concatenate([a["conv_w"][0], a["conv_b"]], 0)[:, ch]
    hist = np.zeros((P, GROUPS, CT, CONV, NSAMP), np.float32)
    hist[:, :, :, :HIST] = a["state_conv"][0][:, :, ch].reshape(NSAMP, HIST, GROUPS, CT, P).transpose(4, 2, 3, 1, 0)
    w_gla = [np.concatenate([q[:, h * DK:(h + 1) * DK], key[:, h * DK:(h + 1) * DK], v[:, h * DV:(h + 1) * DV]], 1) for h in range(GH)]
    w = dict(
        ssd=_weight_tiles(xbc[:, ch], CT * P), gla=np.concatenate([_weight_tiles(x, 2 * DK + DV) for x in w_gla]),
        z=_weight_tiles(z, 512), g=_weight_tiles(g, 512), out=_weight_tiles(a["w_out"][0], 512), query=_weight_tiles(a["peer_w_q"][0], 512),
        merge=np.concatenate([_weight_tiles(x, P) for x in (merge[:, :D], merge[:, D:], a["w_ssd_out"][0], a["w_gla_out"][0])], 2))
    x = dict(
        x_all=np.concatenate([a["x_sample"][:, 0], np.zeros((META0 - NSAMP, D), np.float32), a["meta_tokens"], a["x_prompt"][0]]),
        norm1=np.ascontiguousarray(a["norm1_w"][0].reshape(KD, P).T), wdt=_weight_tiles(dt, HEADS)[0].reshape(P, KD, HEADS),
        dt_bias=_every_partition(a["dt_bias"][0]), a_log=_every_partition(a["a_log"][0]), d_skip=_every_partition(a["d_skip"][0]),
        conv_w=np.ascontiguousarray(conv.reshape(CONV + 1, GROUPS, CT, P).transpose(3, 1, 2, 0)), state_conv=hist,
        state_ssd=np.ascontiguousarray(a["state_ssd"][0].reshape(NSAMP, GROUPS, GW, P).transpose(1, 3, 0, 2)),
        wglr=_weight_tiles(glr, RANK)[0].reshape(P, KD, RANK), gate_up=np.concatenate([a["gla_gate_up"][0], a["gla_gate_b"]], 0),
        state_gla=np.ascontiguousarray(a["state_gla"][0].transpose(1, 2, 0, 3)),
        ssd_norm=np.ascontiguousarray(a["ssd_norm_w"][0].reshape(-1, P).T),
        gla_norm=np.ascontiguousarray(np.tile(a["gla_norm_w"][0].reshape(DV // P, P), (GH, 1)).T),
        norm2=_every_partition(a["norm2_w"][0]), norm_f=_every_partition(a["final_norm_w"]),
        keys=np.ascontiguousarray(a["peer_sub_keys"][0].transpose(3, 1, 0, 2).reshape(P, 2 * EH, NKEYS)),
        experts=np.concatenate([a["peer_u"][0], a["peer_v"][0]], 1))
    return {**x, **{"w_" + n: t for n, t in w.items()}, **_constants()}


_OUTS = dict(o_prompt=(SEQ, D), o_sample=(NSAMP, D), o_pssd=(GROUPS, P, GW), o_pconv=(P, GROUPS, CT, HIST), o_pgla=(GH, DK, DV),
             o_sssd=(GROUPS, P, NSAMP, GW), o_sconv=(P, GROUPS, CT, HIST, NSAMP), o_sgla=(GH, DK, NSAMP, DV))


def kernel(**inputs):
    import concourse.bacc as _bacc
    from concourse.bass_utils import run_bass_kernel_spmd as _run

    nc = _bacc.Bacc("TRN2", target_bir_lowering=False, num_devices=1)
    arrays = {f"in_{n}": x for n, x in _inputs({n: np.asarray(x) for n, x in inputs.items()}).items()}
    ins = {n[3:]: nc.dram_tensor(n, x.shape, mybir.dt.from_np(x.dtype), kind="ExternalInput").ap() for n, x in arrays.items()}
    ins["w"] = {n[2:]: ins.pop(n) for n in [n for n in ins if n.startswith("w_")]}
    outs = {n: nc.dram_tensor(n, shape, F32, kind="ExternalOutput").ap() for n, shape in _OUTS.items()}
    build(nc, ins, outs)
    got = _run(nc, [arrays], core_ids=[0]).results[0]
    back = np.argsort(_channels())
    return (
        got["o_prompt"][None], got["o_sample"][:, None],
        got["o_pssd"].transpose(0, 2, 1).reshape(1, 1, HEADS, HEAD, P),
        got["o_pconv"].transpose(3, 1, 2, 0).reshape(HIST, -1)[:, back][None, None],
        got["o_pgla"][None, None],
        got["o_sssd"].transpose(2, 0, 3, 1).reshape(1, NSAMP, HEADS, HEAD, P),
        got["o_sconv"].transpose(4, 3, 1, 2, 0).reshape(NSAMP, HIST, -1)[:, :, back][None],
        got["o_sgla"].transpose(2, 0, 1, 3)[None])
```

```python
import concourse.bass as bass
from concourse import mybir
from concourse.alu_op_type import AluOpType as ALU
from contextlib import ExitStack
import numpy as np

ACT = mybir.ActivationFunctionType
AX = mybir.AxisListType
F32 = mybir.dt.float32
BF16 = mybir.dt.bfloat16
I32 = mybir.dt.int32
U32 = mybir.dt.uint32

P = 128
D = 1024
KD = D // P
SEQ, NMETA, NSAMP = 512, 16, 8
TILES = SEQ // P
META0 = 32
SM = META0 + NMETA
COLS = SM + SEQ
EPS = 1e-6
GROUPS, HPG, HEAD = 4, 8, 64
HEADS = GROUPS * HPG
GW = HPG * HEAD
CT = GW // P + 2
B_TILE, C_TILE = CT - 2, CT - 1
CONV = 4
HIST = CONV - 1
RAW = HIST + NMETA + SEQ
CONVD = NMETA + SEQ
GH, DK, DV = 4, 128, 256
GCH = 64
RANK = 16
EH, NKEYS, TOPK = 8, 128, 16
ROW = 2 * D


def tile_cols(c):
    return slice(SM + c * P, SM + (c + 1) * P)


BLOCKS = ([("ssd", g) for g in range(GROUPS)] + [("gla", h) for h in range(GH)]
          + [("z", g) for g in range(GROUPS)] + [("g", i) for i in range(2)]
          + [("merge", j) for j in range(KD)] + [("out", i) for i in range(2)])
FIRST = {kind: next(i for i, x in enumerate(BLOCKS) if x[0] == kind)
         for kind in ("ssd", "gla", "z", "g", "merge", "out")}


class Shared:

    def __init__(self, dram):
        self.dram = dram


class Link:

    def __init__(self, sem):
        self.sem, self.count = sem, 0

    def __call__(self, eng, ins):
        self.count += 1
        ins.then_inc(self.sem, 1)
        eng.wait_ge(self.sem, self.count)


def load_block(sp, k, b):
    if b >= len(BLOCKS):
        return
    kind, i = BLOCKS[b]
    if b >= 2:
        sp.wait_ge(*k.block_used[b - 2])
    src = k.dram["w"][kind][i]
    sp.dma_start(k.ring[b % 2][:, 0:src.shape[1]], src).then_inc(k.block_here[b % 2], 16)


def wait_block(pe, k, b):
    pe.wait_ge(k.block_here[b % 2], 16 * (b // 2 + 1))


def stage_norm(nc, k):
    NT = TILES + 1
    with ExitStack() as ctx:
        sb = lambda n, s, d=F32: ctx.enter_context(nc.sbuf_tensor(n, s, d, side="right"))
        sem = lambda n: k.sem("n_" + n)
        x = sb("n_x", [P, NT, D])
        xn = sb("n_xn", [P, NT, D])
        ss = sb("n_ss", [P, NT])
        rs = sb("n_rs", [P, NT])
        w1 = sb("n_w1", [P, KD])
        wdt = sb("n_wdt", [P, KD, HEADS])
        dtb = sb("n_dtb", [P, HEADS])
        ea = sb("n_ea", [P, HEADS])
        u = sb("n_u", [P, 6, HEADS])
        e = sb("n_e", [P, 6, HEADS])
        lu = sb("n_lu", [P, 6, HEADS])
        w = sb("n_w", [P, 6, HEADS])
        ac = sb("n_ac", [P, 5, HEADS])
        al = sb("n_al", [P, 5, HEADS])
        decd = sb("n_decd", [NSAMP, NSAMP, HEADS])
        x_here, sq_done, ms_done, rt_done, xn_done = map(sem, ("x_here", "sq_done", "ms_done", "rt_done", "xn_done"))
        tr_done, ev_done, dt_raw, dt_lin = map(sem, ("tr_done", "ev_done", "dt_raw", "dt_lin"))
        exps_done, da_done, cum_done, cum_copied = map(sem, ("exps_done", "da_done", "cum_done", "cum_copied"))
        decd_done, decb_done, small_here = map(sem, ("decd_done", "decb_done", "small_here"))
        rows = [P] * TILES + [SM]
        ps = k.ps
        block = ctx.enter_context(nc.Block())

        @block.sync
        def _(sp):
            for i in range(NT):
                lo = SM + i * P if i < TILES else 0
                sp.dma_start(x[0:rows[i], i, :], k.dram["x_all"][lo:lo + rows[i], :]).then_inc(x_here, 16)
            for dst, src in ((w1[:, :], k.dram["norm1"]), (wdt[:, :, :], k.dram["wdt"]), (dtb[:, :], k.dram["dt_bias"]), (ea[:, :], k.dram["a_log"])):
                sp.dma_start(dst, src).then_inc(small_here, 16)
            for dst, src in k.const_loads:
                sp.dma_start(dst, src).then_inc(k.consts_here, 16)
            load_block(sp, k, 0)
            load_block(sp, k, 1)

        @block.scalar
        def _(act):
            act.wait_ge(x_here, 16 * NT)
            for i in range(NT):
                last = nc.scalar.activation(xn[0:rows[i], i, :], x[0:rows[i], i, :], ACT.Square,
                                            accum_out=ss[0:rows[i], i:i + 1])
                last.then_inc(sq_done, 1)
            act.wait_ge(ms_done, 1)
            nc.scalar.activation(rs[:, 0:TILES], rs[:, 0:TILES], ACT.Sqrt)
            nc.scalar.activation(rs[0:SM, TILES:NT], rs[0:SM, TILES:NT], ACT.Sqrt).then_inc(rt_done, 1)
            act.wait_ge(small_here, 64)
            nc.scalar.activation(ea[:, :], ea[:, :], ACT.Exp).then_inc(exps_done, 1)
            act.wait_ge(dt_lin, 1)
            k.alink(act, nc.scalar.activation(e[:, :, :], u[:, :, :], ACT.Abs))
            k.alink(act, nc.scalar.activation(e[:, :, :], e[:, :, :], ACT.Exp, scale=-1.0))
            nc.scalar.activation(lu[:, :, :], e[:, :, :], ACT.Ln, bias=1.0).then_inc(exps_done, 1)
            act.wait_ge(cum_copied, 1)
            nc.scalar.activation(k.eac[:, :, :], ac[:, 0:TILES, :], ACT.Exp)
            nc.scalar.activation(k.cdec[:, :, :], al[:, 0:TILES, :], ACT.Exp)
            nc.scalar.activation(k.decs[:, :], k.da[0:NSAMP, 5, :], ACT.Exp)
            nc.scalar.activation(k.dte[:, :, :], w[:, 0:5, :], ACT.Exp).then_inc(exps_done, 1)

        @block.vector
        def _(dve):
            dve.wait_ge(sq_done, NT)
            nc.vector.tensor_scalar(rs[:, 0:TILES], ss[:, 0:TILES], 1.0 / D, EPS, ALU.mult, ALU.add)
            nc.vector.tensor_scalar(rs[0:SM, TILES:NT], ss[0:SM, TILES:NT], 1.0 / D, EPS, ALU.mult, ALU.add).then_inc(ms_done, 1)
            dve.wait_ge(rt_done, 1)
            nc.vector.reciprocal(rs[:, 0:TILES], rs[:, 0:TILES])
            k.vlink(dve, nc.vector.reciprocal(rs[0:SM, TILES:NT], rs[0:SM, TILES:NT]))
            dve.wait_ge(x_here, 16 * NT)
            for i in range(NT):
                nc.vector.tensor_scalar(xn[0:rows[i], i, :], x[0:rows[i], i, :], rs[0:rows[i], i:i + 1], None, ALU.mult).then_inc(xn_done, 1)
            dve.wait_ge(small_here, 64)
            for i in range(NT):
                lo = SM + i * P if i < TILES else 0
                for half in range(2):
                    n = 2 * i + half
                    dve.wait_ge(tr_done, n + 1)
                    src = ps[n % 2][:, :].rearrange("p (a t) -> p a t", a=4)[:, :, 0:rows[i]]
                    nc.vector.tensor_tensor(k.xnT[:, 4 * half:4 * half + 4, lo:lo + rows[i]], src,
                                            w1[:, 4 * half:4 * half + 4].unsqueeze(2).to_broadcast([P, 4, rows[i]]),
                                            ALU.mult).then_inc(ev_done, 1)
            k.vlink(dve, nc.vector.memset(u[:, :, :], 0.0))
            dve.wait_ge(dt_raw, 1)
            raw = ps[2][:, 0:6 * HEADS].rearrange("p (a h) -> p a h", a=6)
            nc.vector.tensor_tensor(u[:, 0:TILES, :], raw[:, 0:TILES, :], dtb[:, :].unsqueeze(1).to_broadcast([P, TILES, HEADS]), ALU.add)
            nc.vector.tensor_tensor(u[0:NMETA, 4, :], raw[0:NMETA, 4, :], dtb[0:NMETA, :], ALU.add)
            nc.vector.tensor_tensor(u[0:NSAMP, 5, :], raw[0:NSAMP, 5, :], dtb[0:NSAMP, :], ALU.add).then_inc(dt_lin, 1)
            dve.wait_ge(exps_done, 2)
            TINY = 1e-30
            k.vlink(dve, nc.vector.tensor_scalar(w[:, :, :], e[:, :, :], 1.0, None, ALU.add))
            k.vlink(dve, nc.vector.tensor_scalar(w[:, :, :], w[:, :, :], -1.0, TINY, ALU.add, ALU.add))
            k.vlink(dve, nc.vector.reciprocal(w[:, :, :], w[:, :, :]))
            k.vlink(dve, nc.vector.scalar_tensor_tensor(lu[:, :, :], lu[:, :, :], TINY, w[:, :, :], ALU.add, ALU.mult))
            k.vlink(dve, nc.vector.tensor_tensor(lu[:, :, :], lu[:, :, :], e[:, :, :], ALU.mult))
            k.vlink(dve, nc.vector.scalar_tensor_tensor(k.dt[:, :, :], u[:, :, :], 0.0, lu[:, :, :], ALU.max, ALU.add))
            dve.wait_ge(exps_done, 1)
            nc.vector.scalar_tensor_tensor(k.da[:, :, :], k.dt[:, :, :], -1.0, ea[:, :].unsqueeze(1).to_broadcast([P, 6, HEADS]), ALU.mult, ALU.mult).then_inc(da_done, 1)
            k.vlink(dve, nc.vector.memset(ac[:, :, :], 0.0))
            dve.wait_ge(cum_done, 1)
            cum = ps[3][:, 0:5 * HEADS].rearrange("p (a h) -> p a h", a=5)
            tot = ps[4][:, 0:5 * HEADS].rearrange("p (a h) -> p a h", a=5)
            nc.vector.tensor_copy(ac[:, 0:TILES, :], cum[:, 0:TILES, :])
            nc.vector.tensor_copy(al[:, :, :], tot)
            k.vlink(dve, nc.vector.tensor_copy(ac[0:NMETA, 4, :], cum[0:NMETA, 4, :]))
            nc.vector.tensor_scalar(k.nac[:, :, :], ac[:, 0:TILES, :], -1.0, None, ALU.mult)
            nc.vector.tensor_tensor(w[:, 0:5, :], al[:, :, :], ac[:, :, :], ALU.subtract).then_inc(cum_copied, 1)
            dve.wait_ge(exps_done, 3)
            dve.wait_ge(k.consts_here, 16 * len(k.const_loads))
            nc.vector.tensor_tensor(k.dte[:, :, :], k.dte[:, :, :], k.dt[:, 0:5, :], ALU.mult)
            nc.vector.tensor_tensor(decd[:, :, :], k.decs[:, :].unsqueeze(1).to_broadcast([NSAMP, NSAMP, HEADS]),
                                    k.diag8[:, :].unsqueeze(2).to_broadcast([NSAMP, NSAMP, HEADS]),
                                    ALU.mult).then_inc(decd_done, 1)
            dve.wait_ge(decb_done, 1)
            k.vlink(dve, nc.vector.tensor_copy(k.decb[:, :, :], ps[5][:, 0:NSAMP * HEADS].rearrange("p (b h) -> p b h", b=NSAMP)))

        @block.tensor
        def _(pe):
            pe.wait_ge(k.consts_here, 16 * len(k.const_loads))
            for i in range(NT):
                pe.wait_ge(xn_done, i + 1)
                for half in range(2):
                    n = 2 * i + half
                    if n >= 2:
                        pe.wait_ge(ev_done, n - 1)
                    for a in range(4):
                        kt = 4 * half + a
                        last = nc.tensor.transpose(ps[n % 2][:, a * P:a * P + rows[i]], xn[0:rows[i], i, kt * P:(kt + 1) * P],
                                                   k.ident[0:rows[i], 0:rows[i]])
                    last.then_inc(tr_done, 1)
            pe.wait_ge(ev_done, 2 * NT)
            pe.wait_ge(small_here, 64)
            spans = [(tile_cols(c), P) for c in range(TILES)] + [(slice(META0, SM), NMETA), (slice(0, NSAMP), NSAMP)]
            for a, (cols, m) in enumerate(spans):
                for kt in range(KD):
                    last = nc.tensor.matmul(ps[2][0:m, a * HEADS:(a + 1) * HEADS], k.xnT[:, kt, cols], wdt[:, kt, :],
                                            start=kt == 0, stop=kt == KD - 1)
            last.then_inc(dt_raw, 1)
            pe.wait_ge(da_done, 1)
            daf = k.da[:, :, :].rearrange("p a h -> p (a h)")
            m0 = TILES * HEADS
            nc.tensor.matmul(ps[3][:, 0:m0], k.tri[:, :], daf[:, 0:m0], start=True, stop=True)
            nc.tensor.matmul(ps[3][0:NMETA, m0:m0 + HEADS], k.tri[0:NMETA, 0:NMETA], daf[0:NMETA, m0:m0 + HEADS], start=True, stop=True)
            nc.tensor.matmul(ps[4][:, 0:m0], k.ones[:, :], daf[:, 0:m0], start=True, stop=True)
            nc.tensor.matmul(ps[4][:, m0:m0 + HEADS], k.ones[0:NMETA, :], daf[0:NMETA, m0:m0 + HEADS], start=True, stop=True).then_inc(cum_done, 1)
            pe.wait_ge(decd_done, 1)
            nc.tensor.matmul(ps[5][:, 0:NSAMP * HEADS], k.ones[0:NSAMP, :], decd[:, :, :].rearrange("p b h -> p (b h)"), start=True, stop=True).then_inc(decb_done, 1)


STEPS = 1 + TILES


def ssd_order():
    order = [("tile", 0, j) for j in range(CT)]
    for g in range(GROUPS):
        tiles = [("tile", g + 1, j) for j in range(CT)] if g + 1 < GROUPS else []
        order += [("front", g, 0)] + tiles[0:1]
        for i in range(1, STEPS):
            order += [("front", g, i), ("back", g, i - 1)] + tiles[i:i + (1 if i < STEPS - 1 else 2)]
        order += [("back", g, STEPS - 1), ("sample", g, 0)]
    return order


SSD_ORDER = ssd_order()


def stage_ssd(nc, k):
    with ExitStack() as ctx:
        sb = lambda n, s, d=F32: ctx.enter_context(nc.sbuf_tensor("s_" + n, s, d, side="right"))
        sem = lambda n: k.sem("s_" + n)
        raw = sb("raw", [P, 3, RAW])
        cv = sb("cv", [P, 3, CONVD])
        xc = sb("xc", [P, 2, CT, CONVD])
        hist = sb("hist", [P, GROUPS, CT, CONV, NSAMP])
        cw = sb("cw", [P, GROUPS, CT, CONV + 1])
        last3 = sb("last3", [P, GROUPS, CT, HIST])
        sconv = sb("sconv", [P, CT, NSAMP])
        sterm = sb("sterm", [P, CT, NSAMP])
        sxc = sb("sxc", [P, 2, CT, NSAMP])
        cmask = sb("cmask", [P, NSAMP, NSAMP])
        xdt = sb("xdt", [P, 2, GW])
        xdec = sb("xdec", [P, 2, GW])
        bcb = sb("bcb", [P, 2, 2, P])
        mix = sb("mix", [P, 2, 2, 4, P])
        yoff = sb("yoff", [P, GW])
        state = sb("state", [P, 2, GW])
        sxdt = sb("sxdt", [NSAMP, GW])
        sst = sb("sst", [P, NSAMP, GW])
        dsk = sb("dsk", [P, HEADS])
        ins_here, tile_ready, tile_evac, conv_first, conv_done, xc_ready = map(
            sem, ("ins_here", "tile_ready", "tile_evac", "conv_first", "conv_done", "xc_ready"))
        xt_ready, bc_ready, xt_used, bc_copied, yoff_done = map(sem, ("xt_ready", "bc_ready", "xt_used", "bc_copied", "yoff_done"))
        seg_ready, exp_done, mix_done, yd_ready, yo_ready = map(sem, ("seg_ready", "exp_done", "mix_done", "yd_ready", "yo_ready"))
        cs_ready, y_done, state_done, xdt_done, xdec_done, zeroed = map(
            sem, ("cs_ready", "y_done", "state_done", "xdt_done", "xdec_done", "zeroed"))
        sconv_done, sxc_ready, sxt_ready, sxdt_done, cmask_done = map(sem, ("sconv_done", "sxc_ready", "sxt_ready", "sxdt_done", "cmask_done"))
        sst_here, sdec_done, sx_ready, sst_done, sy_ready, sy_done = map(sem, ("sst_here", "sdec_done", "sx_ready", "sst_done", "sy_ready", "sy_done"))
        sst_out, pst_out, conv_out, pst_final = map(sem, ("sst_out", "pst_out", "conv_out", "pst_final"))
        k.block_used.update({FIRST["ssd"] + g: (tile_ready, CT * (g + 1)) for g in range(GROUPS)})
        ps = k.ps
        MAIN, SMALL, XT, BC, SEG, YD, YO = (0, 1), 2, 3, 4, 5, 6, 7
        CS = YO
        block = ctx.enter_context(nc.Block())

        def chunk_cols(i):
            return slice(0, NMETA) if i == 0 else slice(NMETA + (i - 1) * P, NMETA + i * P)

        def chunks_before(s):
            return s // STEPS * TILES + max(0, s % STEPS - 1)

        @block.sync
        def _(sp):
            for dst, src in ((hist[:, :, :, :, :], k.dram["state_conv"]), (cw[:, :, :, :], k.dram["conv_w"]), (dsk[:, :], k.dram["d_skip"])):
                sp.dma_start(dst, src).then_inc(ins_here, 16)
            for g in range(GROUPS):
                if g >= 1:
                    sp.wait_ge(sst_out, 16 * g)
                    sp.wait_ge(sy_ready, g)
                sp.dma_start(sst[:, :, :], k.dram["state_ssd"][g]).then_inc(sst_here, 16)
                load_block(sp, k, FIRST["ssd"] + g + 2)
                sp.wait_ge(sst_done, NSAMP * (g + 1))
                sp.dma_start(k.dram["o_sssd"][g], sst[:, :, :]).then_inc(sst_out, 16)
                sp.wait_ge(state_done, STEPS * (g + 1))
                sp.dma_start(k.dram["o_pssd"][g], state[:, g % 2, :]).then_inc(pst_out, 16)
            sp.wait_ge(tile_evac, GROUPS * CT)
            sp.dma_start(k.dram["o_sconv"], hist[:, :, :, 1:CONV, :]).then_inc(conv_out, 16)
            sp.dma_start(k.dram["o_pconv"], last3[:, :, :, :]).then_inc(conv_out, 16)
            sp.wait_ge(conv_out, 32)
            sp.wait_ge(sst_out, 16 * GROUPS)
            sp.wait_ge(pst_out, 16 * GROUPS)

        @block.tensor
        def _(pe):
            for kind, g, i in SSD_ORDER:
                if kind == "tile":
                    n, b = g * CT + i, FIRST["ssd"] + g
                    if i == 0:
                        wait_block(pe, k, b)
                    if n >= 2:
                        pe.wait_ge(tile_evac, n - 1)
                    w = k.ring[b % 2][:, 0:KD * CT * P].rearrange("p (k c) -> p k c", k=KD)
                    for kt in range(KD):
                        wt = w[:, kt, i * P:(i + 1) * P]
                        nc.tensor.matmul(ps[MAIN[n % 2]][:, :], wt, k.xnT[:, kt, SM:COLS], start=kt == 0, stop=kt == KD - 1)
                    if n >= 1:
                        pe.wait_ge(tile_evac, n)
                    for kt in range(KD):
                        wt = w[:, kt, i * P:(i + 1) * P]
                        last = nc.tensor.matmul(ps[SMALL][:, 0:SM], wt, k.xnT[:, kt, 0:SM], start=kt == 0, stop=kt == KD - 1)
                    last.then_inc(tile_ready, 1)
                elif kind == "front":
                    s = g * STEPS + i
                    d = g * TILES + i - 1
                    cols, m = chunk_cols(i), (NMETA if i == 0 else P)
                    x = xc[:, g % 2]

                    def decays(half):
                        q = 2 * d + half
                        if q >= 1:
                            pe.wait_ge(exp_done, q)
                        nc.tensor.matmul(ps[SEG][:, :], k.identb[:, :], k.future[:, :], start=True, stop=False)
                        for h in range(4):
                            hh = g * HPG + half * 4 + h
                            last = nc.tensor.matmul(ps[SEG][:, h * P:(h + 1) * P], k.da[:, i - 1, hh:hh + 1].to_broadcast([P, P]),
                                                    k.tri[:, :], start=False, stop=h == 3)
                        last.then_inc(seg_ready, 1)

                    if i > 0:
                        decays(0)
                    if i == 0:
                        pe.wait_ge(xc_ready, CT * (g + 1))
                        if g >= 1:
                            pe.wait_ge(sst_done, NSAMP * g)
                            pe.wait_ge(sy_done, g)
                    if i == 1:
                        pe.wait_ge(xdec_done, s)
                    elif s >= 1:
                        pe.wait_ge(xt_used, chunks_before(s))
                    for a in range(CT - 2):
                        last = nc.tensor.transpose(ps[XT][0:m, a * P:(a + 1) * P], x[:, a, cols], k.ident[:, :])
                    last.then_inc(xt_ready, 1)
                    if s >= 1:
                        pe.wait_ge(bc_copied, s)
                    last = nc.tensor.transpose(ps[BC][0:m, 0:P], x[:, B_TILE, cols], k.ident[:, :])
                    if i > 0:
                        last = nc.tensor.matmul(ps[BC][:, P:2 * P], x[:, B_TILE, cols], x[:, C_TILE, cols], start=True, stop=True)
                    last.then_inc(bc_ready, 1)
                    if i > 0:
                        decays(1)
                elif kind == "back":
                    s, d = g * STEPS + i, g * TILES + i - 1
                    cols, m, par = chunk_cols(i), (NMETA if i == 0 else P), s % 2
                    if s >= 1:
                        pe.wait_ge(state_done, s)
                    if i > 0:
                        nc.tensor.matmul(ps[YO][:, :], xc[:, g % 2, C_TILE, cols], state[:, g % 2, :], start=True, stop=True).then_inc(yo_ready, 1)
                        if d >= 1:
                            pe.wait_ge(y_done, d)
                        pe.wait_ge(xdt_done, d + 1)
                        pe.wait_ge(mix_done, 2 * d + 2)
                        for h in range(HPG):
                            last = nc.tensor.matmul(ps[YD][:, h * HEAD:(h + 1) * HEAD], mix[:, d % 2, h // 4, h % 4, :],
                                                    xdt[:, par, h * HEAD:(h + 1) * HEAD], start=True, stop=True)
                        last.then_inc(yd_ready, 1)
                        pe.wait_ge(yoff_done, d + 1)
                    pe.wait_ge(xdec_done, s + 1)
                    pe.wait_ge(bc_copied, s + 1)
                    nc.tensor.matmul(ps[CS][:, :], bcb[0:m, par, 0, :], xdec[0:m, par, :], start=True, stop=True).then_inc(cs_ready, 1)
                else:
                    pe.wait_ge(sxc_ready, g + 1)
                    pe.wait_ge(xt_used, TILES * (g + 1))
                    for a in range(CT - 2):
                        last = nc.tensor.transpose(ps[XT][0:NSAMP, a * P:(a + 1) * P], sxc[:, g % 2, a, :], k.ident[:, :])
                    last.then_inc(sxt_ready, 1)
                    pe.wait_ge(sxdt_done, g + 1)
                    pe.wait_ge(cmask_done, g + 1)
                    pe.wait_ge(state_done, STEPS * (g + 1))
                    pe.wait_ge(y_done, TILES * (g + 1))

                    def spread(b):
                        q = g * NSAMP + b
                        if q >= 2:
                            pe.wait_ge(sst_done, q - 1)
                        nc.tensor.matmul(ps[(XT, CS)[b % 2]][:, :], k.sel8[:, b, :], sxdt[:, :], start=True, stop=True).then_inc(sx_ready, 1)

                    spread(0)
                    for b in range(NSAMP):
                        if b + 1 < NSAMP:
                            spread(b + 1)
                        pe.wait_ge(sst_done, g * NSAMP + b + 1)
                        last = nc.tensor.matmul(ps[YD][0:NSAMP, :], cmask[:, b, :], sst[:, b, :], start=b == 0, stop=b == NSAMP - 1)
                    last.then_inc(sy_ready, 1)

        @block.scalar
        def _(act):
            act.wait_ge(ins_here, 48)
            act.wait_ge(zeroed, 1)

            def silu(n):
                g, j = divmod(n, CT)
                act.wait_ge(conv_done, n + 1)
                if j == 0 and g >= 2:
                    act.wait_ge(cs_ready, STEPS * (g - 1))
                nc.scalar.activation(xc[:, g % 2, j, :], cv[:, n % 3, :], ACT.Silu).then_inc(xc_ready, 1)

            for kind, g, i in SSD_ORDER:
                if kind == "tile":
                    n = g * CT + i
                    act.wait_ge(tile_ready, n + 1)
                    if n >= 3:
                        act.wait_ge(conv_done, n - 2)
                    small = ps[SMALL][:, 0:SM]
                    nc.scalar.copy(raw[:, n % 3, HIST + NMETA:RAW], ps[MAIN[n % 2]][:, :])
                    nc.scalar.copy(raw[:, n % 3, HIST:HIST + NMETA], small[:, META0:SM])
                    nc.scalar.copy(hist[:, g, i, CONV - 1, :], small[:, 0:NSAMP])
                    nc.scalar.copy(last3[:, g, i, :], ps[MAIN[n % 2]][:, SEQ - HIST:SEQ]).then_inc(tile_evac, 1)
                    act.wait_ge(tile_evac, n + 1)
                    if n >= 3:
                        act.wait_ge(xc_ready, n - 2)
                    nc.scalar.activation(cv[:, n % 3, :], raw[:, n % 3, 0:CONVD], ACT.Identity,
                                         bias=cw[:, g, i, CONV:CONV + 1], scale=cw[:, g, i, 0:1]).then_inc(conv_first, 1)
                    if n % CT >= 1:
                        silu(n - 1)
                    if n % CT == CT - 1:
                        silu(n)
                        act.wait_ge(sconv_done, g + 1)
                        if g >= 2:
                            act.wait_ge(sst_done, NSAMP * (g - 1))
                        nc.scalar.activation(sxc[:, g % 2, :, :], sconv[:, :, :], ACT.Silu).then_inc(sxc_ready, 1)
                elif kind == "front":
                    s, d = g * STEPS + i, g * TILES + i - 1
                    m, par = (NMETA if i == 0 else P), s % 2

                    def decays(half):
                        act.wait_ge(seg_ready, 2 * d + half + 1)
                        if d >= 2:
                            act.wait_ge(yd_ready, d - 1)
                        for h in range(4):
                            hh = g * HPG + half * 4 + h
                            last = nc.scalar.activation(mix[:, d % 2, half, h, :], ps[SEG][:, h * P:(h + 1) * P], ACT.Exp,
                                                        bias=k.nac[:, i - 1, hh:hh + 1])
                        last.then_inc(exp_done, 1)

                    if i > 0:
                        decays(0)
                    act.wait_ge(bc_ready, s + 1)
                    if s >= 2:
                        act.wait_ge(cs_ready, s - 1)
                        if chunks_before(s - 1):
                            act.wait_ge(mix_done, 2 * chunks_before(s - 1))
                    w = P if i == 0 else 2 * P
                    nc.scalar.copy(bcb[0:m, par, :, :].rearrange("p a b -> p (a b)")[:, 0:w], ps[BC][0:m, 0:w]).then_inc(bc_copied, 1)
                    if i > 0:
                        decays(1)

        @block.vector
        def _(dve):
            dve.wait_ge(ins_here, 48)
            nc.vector.memset(raw[:, :, 0:HIST], 0.0).then_inc(zeroed, 1)
            heads = lambda ap: ap.rearrange("p (h c) -> p h c", c=HEAD)
            for kind, g, i in SSD_ORDER:
                hs = slice(g * HPG, (g + 1) * HPG)
                gc = slice(g * GW, (g + 1) * GW)
                wide = lambda ap, m=P: ap.unsqueeze(2).to_broadcast([m, HPG, HEAD])
                if kind == "tile":
                    n = g * CT + i
                    dve.wait_ge(conv_first, n + 1)
                    for j in range(1, CONV):
                        ins = nc.vector.scalar_tensor_tensor(cv[:, n % 3, :], raw[:, n % 3, j:j + CONVD], cw[:, g, i, j:j + 1],
                                                             cv[:, n % 3, :], ALU.mult, ALU.add)
                        if j < CONV - 1:
                            k.vlink(dve, ins)
                    ins.then_inc(conv_done, 1)
                elif kind == "front":
                    s, d = g * STEPS + i, g * TILES + i - 1
                    m, par = (NMETA if i == 0 else P), s % 2
                    c = TILES if i == 0 else i - 1
                    dve.wait_ge(xt_ready, s + 1)
                    if s >= 2:
                        dve.wait_ge(cs_ready, s - 1)
                        if chunks_before(s - 1):
                            dve.wait_ge(yd_ready, chunks_before(s - 1))
                    xt = heads(ps[XT][0:m, :])
                    nc.vector.tensor_tensor(heads(xdec[0:m, par, :]), xt, wide(k.dte[0:m, c, hs], m), ALU.mult).then_inc(xdec_done, 1)
                    if i > 0:
                        nc.vector.tensor_tensor(heads(xdt[:, par, :]), xt, wide(k.dt[:, c, hs]), ALU.mult).then_inc(xdt_done, 1)
                        nc.vector.tensor_tensor(heads(k.y[:, c, gc]), xt, wide(dsk[:, hs]), ALU.mult).then_inc(xt_used, 1)
                        for half in range(2):
                            dve.wait_ge(bc_copied, s + 1)
                            dve.wait_ge(exp_done, 2 * d + half + 1)
                            nc.vector.tensor_tensor(mix[:, d % 2, half, :, :], mix[:, d % 2, half, :, :],
                                                    bcb[:, par, 1, :].unsqueeze(1).to_broadcast([P, 4, P]), ALU.mult).then_inc(mix_done, 1)
                elif kind == "back":
                    s, d, c = g * STEPS + i, g * TILES + i - 1, i - 1
                    if i > 0:
                        dve.wait_ge(yo_ready, d + 1)
                        nc.vector.tensor_tensor(heads(yoff[:, :]), heads(ps[YO][:, :]), wide(k.eac[:, c, hs]), ALU.mult).then_inc(yoff_done, 1)
                        k.vlink(dve, nc.vector.tensor_tensor(heads(state[:, g % 2, :]), heads(state[:, g % 2, :]), wide(k.cdec[:, c, hs]), ALU.mult))
                        dve.wait_ge(xt_used, d + 1)
                        nc.vector.tensor_tensor(k.y[:, c, gc], k.y[:, c, gc], yoff[:, :], ALU.add)
                        dve.wait_ge(cs_ready, s + 1)
                        nc.vector.tensor_tensor(state[:, g % 2, :], state[:, g % 2, :], ps[CS][:, :], ALU.add).then_inc(state_done, 1)
                        dve.wait_ge(yd_ready, d + 1)
                        dve.wait_ge(state_done, s + 1)
                        nc.vector.tensor_tensor(k.y[:, c, gc], k.y[:, c, gc], ps[YD][:, :], ALU.add).then_inc(y_done, 1)
                    else:
                        if g >= 2:
                            dve.wait_ge(pst_out, 16 * (g - 1))
                        dve.wait_ge(cs_ready, s + 1)
                        nc.vector.tensor_copy(state[:, g % 2, :], ps[CS][:, :]).then_inc(state_done, 1)
                else:
                    dve.wait_ge(sxc_ready, g + 1)
                    if g >= 1:
                        dve.wait_ge(sy_ready, g)
                    nc.vector.tensor_tensor(cmask[:, :, :], k.eye8[:, :, :], sxc[:, g % 2, C_TILE, :].unsqueeze(1).to_broadcast([P, NSAMP, NSAMP]),
                                            ALU.mult).then_inc(cmask_done, 1)
                    dve.wait_ge(sxt_ready, g + 1)
                    xt = heads(ps[XT][0:NSAMP, :])
                    nc.vector.tensor_tensor(heads(sxdt[:, :]), xt, wide(k.dt[0:NSAMP, 5, hs], NSAMP), ALU.mult)
                    nc.vector.tensor_tensor(heads(k.ys[:, gc]), xt, wide(dsk[0:NSAMP, hs], NSAMP), ALU.mult).then_inc(sxdt_done, 1)
                    for b in range(NSAMP):
                        q = g * NSAMP + b
                        dve.wait_ge(sdec_done, q + 1)
                        dve.wait_ge(sx_ready, q + 1)
                        nc.vector.scalar_tensor_tensor(sst[:, b, :], ps[(XT, CS)[b % 2]][:, :], sxc[:, g % 2, B_TILE, b:b + 1],
                                                       sst[:, b, :], ALU.mult, ALU.add).then_inc(sst_done, 1)
                    dve.wait_ge(sy_ready, g + 1)
                    dve.wait_ge(sxdt_done, g + 1)
                    nc.vector.tensor_tensor(k.ys[:, gc], k.ys[:, gc], ps[YD][0:NSAMP, :], ALU.add).then_inc(sy_done, 1)

        @block.gpsimd
        def _(pool):
            pool.wait_ge(ins_here, 48)
            for kind, g, i in SSD_ORDER:
                if kind == "tile" and i == CT - 1:
                    pool.wait_ge(tile_evac, CT * (g + 1))
                    if g >= 1:
                        pool.wait_ge(sxc_ready, g)
                    tap = lambda j: cw[:, g, :, j:j + 1].to_broadcast([P, CT, NSAMP])
                    k.plink(pool, nc.gpsimd.tensor_tensor(sconv[:, :, :], hist[:, g, :, 0, :], tap(0), ALU.mult))
                    for j in range(1, CONV):
                        k.plink(pool, nc.gpsimd.tensor_tensor(sterm[:, :, :], hist[:, g, :, j, :], tap(j), ALU.mult))
                        k.plink(pool, nc.gpsimd.tensor_tensor(sconv[:, :, :], sconv[:, :, :], sterm[:, :, :], ALU.add))
                    nc.gpsimd.tensor_tensor(sconv[:, :, :], sconv[:, :, :], tap(CONV), ALU.add).then_inc(sconv_done, 1)
                elif kind == "front" and i == 1:
                    pool.wait_ge(sst_here, 16 * (g + 1))
                    for b in range(NSAMP):
                        v = sst[:, b, :].rearrange("p (h c) -> p h c", c=HEAD)
                        nc.gpsimd.tensor_tensor(v, v, k.decb[:, b, g * HPG:(g + 1) * HPG].unsqueeze(2).to_broadcast([P, HPG, HEAD]),
                                                ALU.mult).then_inc(sdec_done, 1)


def gla_order():
    proj = lambda h: [("q", h, 0), ("k", h, 0)] + [("v", h, c) for c in range(TILES)] + [("vsmall", h, 0)]
    order = proj(0)
    for h in range(GH):
        steps = [("prep", h, 0), ("fold", h, 0)] + [("chunk", h, c) for c in range(TILES)] + [("sample", h, 0)]
        nxt = proj(h + 1) if h + 1 < GH else [None] * len(steps)
        for a, b in zip(steps, nxt):
            order += [a] + ([b] if b else [])
    return order


def stage_gla(nc, k):
    order = gla_order()
    NCH = SEQ // GCH
    NP = 2 + TILES
    QSCALE = DK ** -0.5
    with ExitStack() as ctx:
        sb = lambda n, s, d=F32: ctx.enter_context(nc.sbuf_tensor("g_" + n, s, d, side="right"))
        sem = lambda n: k.sem("g_" + n)
        wglr = sb("wglr", [P, KD, RANK])
        up = sb("up", [RANK + 1, GH * DK])
        glrT = sb("glrT", [RANK + 1, COLS])
        gk = sb("gk", [P, TILES, GH * DK])
        gkm = sb("gkm", [NMETA, GH * DK])
        gks = sb("gks", [P, GH, NSAMP])
        qT = sb("qT", [P, 2, SEQ])
        qs = sb("qs", [P, 2, NSAMP])
        kT = sb("kT", [P, 2, NMETA + SEQ])
        ks = sb("ks", [P, 2, NSAMP])
        vt = sb("vt", [P, 2, TILES, DV])
        vm = sb("vm", [NMETA, 2, DV])
        vs = sb("vs", [NSAMP, 2, DV])
        bend = sb("bend", [P, NCH + 1])
        cdg = sb("cdg", [P, 2, NCH])
        ep = sb("ep", [P, SEQ])
        qa = sb("qa", [P, 2, TILES, 4, GCH])
        ke = sb("ke", [P, SEQ])
        kd = sb("kd", [P, NMETA + SEQ])
        kt_ = sb("kt", [P, TILES, DK])
        ktm = sb("ktm", [NMETA, DK])
        att = sb("att", [P, TILES, P])
        st = sb("st", [P, 2, 2, DV])
        gs = sb("gs", [P, NSAMP, DV])
        qmask = sb("qmask", [P, NSAMP, NSAMP])
        ins_here, ones_set, glr_ready, glr_copied, gk_ready, gk_ln, gk_done, gs_exp = map(
            sem, ("ins_here", "ones_set", "glr_ready", "glr_copied", "gk_ready", "gk_ln", "gk_done", "gs_exp"))
        proj_ready, proj_evac, vs_ready, vs_evac = map(sem, ("proj_ready", "proj_evac", "vs_ready", "vs_evac"))
        cum_ready, bend_done, exp_done, qa_done, ke_done, kd_done = map(sem, ("cum_ready", "bend_done", "exp_done", "qa_done", "ke_done", "kd_done"))
        kt_ready, kt_copied, att_ready, att_done = map(sem, ("kt_ready", "kt_copied", "att_ready", "att_done"))
        cs_ready, st_done, o_ready, o_copied, st_out = map(sem, ("cs_ready", "st_done", "o_ready", "o_copied", "st_out"))
        gs_here, sdec_done, sv_ready, gs_done, os_ready, os_done, gs_out, qm_done = map(
            sem, ("gs_here", "sdec_done", "sv_ready", "gs_done", "os_ready", "os_done", "gs_out", "qm_done"))
        k.block_used.update({FIRST["gla"] + h: (vs_ready, h + 1) for h in range(GH)})
        ps = k.ps
        SMALL, CUM, ATT, O, CS, MISC = 2, 3, 4, 5, 6, 7
        block = ctx.enter_context(nc.Block())

        @block.sync
        def _(sp):
            for dst, src in ((wglr[:, :, :], k.dram["wglr"]), (up[:, :], k.dram["gate_up"])):
                sp.dma_start(dst, src).then_inc(ins_here, 16)
            for h in range(GH):
                if h >= 1:
                    sp.wait_ge(gs_out, 16 * h)
                    sp.wait_ge(os_ready, h)
                sp.dma_start(gs[:, :, :], k.dram["state_gla"][h]).then_inc(gs_here, 16)
                load_block(sp, k, FIRST["gla"] + h + 2)
                sp.wait_ge(st_done, (NCH + 1) * (h + 1))
                sp.dma_start(k.dram["o_pgla"][h], st[:, h % 2, 0, :]).then_inc(st_out, 16)
                sp.wait_ge(gs_done, NSAMP * (h + 1))
                sp.dma_start(k.dram["o_sgla"][h], gs[:, :, :]).then_inc(gs_out, 16)
            sp.wait_ge(st_out, 16 * GH)
            sp.wait_ge(gs_out, 16 * GH)

        @block.tensor
        def _(pe):
            pe.wait_ge(ins_here, 32)
            for kt in range(KD):
                nc.tensor.matmul(ps[0][0:RANK, :], wglr[:, kt, :], k.xnT[:, kt, SM:COLS], start=kt == 0, stop=kt == KD - 1)
            for kt in range(KD):
                last = nc.tensor.matmul(ps[SMALL][0:RANK, 0:SM], wglr[:, kt, :], k.xnT[:, kt, 0:SM], start=kt == 0, stop=kt == KD - 1)
            last.then_inc(glr_ready, 1)
            pe.wait_ge(glr_copied, 1)
            for c in range(TILES):
                nc.tensor.matmul(ps[CUM + c][:, :], glrT[:, tile_cols(c)], up[:, :], start=True, stop=True)
            nc.tensor.matmul(ps[MISC][0:NMETA, :], glrT[:, META0:SM], up[:, :], start=True, stop=True)
            for h in range(GH):
                last = nc.tensor.matmul(ps[SMALL][:, h * NSAMP:(h + 1) * NSAMP], up[:, h * DK:(h + 1) * DK], glrT[:, 0:NSAMP], start=True, stop=True)
            last.then_inc(gk_ready, 1)
            pe.wait_ge(gk_done, 1)
            for kind, h, c in order:
                par, b = h % 2, FIRST["gla"] + h
                w = k.ring[b % 2][:, 0:KD * (2 * DK + DV)].rearrange("p (k c) -> p k c", k=KD)
                if kind in ("q", "k"):
                    n = h * NP + (kind == "k")
                    if kind == "q":
                        wait_block(pe, k, b)
                    if n >= 2:
                        pe.wait_ge(proj_evac, n - 1)
                    off = DK * (kind == "k")
                    for kt in range(KD):
                        nc.tensor.matmul(ps[n % 2][:, :], w[:, kt, off:off + DK], k.xnT[:, kt, SM:COLS], start=kt == 0, stop=kt == KD - 1)
                    if kind == "k":
                        pe.wait_ge(proj_evac, n)
                    elif h >= 1:
                        pe.wait_ge(vs_evac, h)
                    for kt in range(KD):
                        last = nc.tensor.matmul(ps[SMALL][:, 0:SM], w[:, kt, off:off + DK], k.xnT[:, kt, 0:SM], start=kt == 0, stop=kt == KD - 1)
                    last.then_inc(proj_ready, 1)
                elif kind == "v":
                    n = h * NP + 2 + c
                    pe.wait_ge(proj_evac, n - 1)
                    for kt in range(KD):
                        last = nc.tensor.matmul(ps[n % 2][:, 0:DV], k.xnT[:, kt, tile_cols(c)], w[:, kt, 2 * DK:2 * DK + DV],
                                                start=kt == 0, stop=kt == KD - 1)
                    last.then_inc(proj_ready, 1)
                elif kind == "vsmall":
                    pe.wait_ge(proj_evac, h * NP + 2)
                    for kt in range(KD):
                        nc.tensor.matmul(ps[SMALL][0:NMETA, 0:DV], k.xnT[:, kt, META0:SM], w[:, kt, 2 * DK:2 * DK + DV], start=kt == 0, stop=kt == KD - 1)
                    for kt in range(KD):
                        last = nc.tensor.matmul(ps[SMALL][0:NSAMP, DV:2 * DV], k.xnT[:, kt, 0:NSAMP], w[:, kt, 2 * DK:2 * DK + DV],
                                                start=kt == 0, stop=kt == KD - 1)
                    last.then_inc(vs_ready, 1)
                elif kind == "prep":
                    if h >= 1:
                        pe.wait_ge(gs_done, NSAMP * h)
                        pe.wait_ge(os_done, h)
                    for c_ in range(TILES):
                        nc.tensor.matmul(ps[CUM][:, c_ * P:(c_ + 1) * P], gk[:, c_, h * DK:(h + 1) * DK], k.tri64[:, :], start=True, stop=True)
                    nc.tensor.matmul(ps[MISC][:, 0:NMETA], gkm[:, h * DK:(h + 1) * DK], k.tri64[0:NMETA, 0:NMETA], start=True, stop=True).then_inc(cum_ready, 1)
                elif kind == "fold":
                    pe.wait_ge(kd_done, h + 1)
                    pe.wait_ge(exp_done, h + 1)
                    for c_ in range(TILES):
                        nc.tensor.transpose(ps[CUM][:, c_ * P:(c_ + 1) * P], kd[:, NMETA + c_ * P:NMETA + (c_ + 1) * P], k.ident[:, :])
                    nc.tensor.transpose(ps[MISC][0:NMETA, 0:DK], kd[:, 0:NMETA], k.ident[:, :]).then_inc(kt_ready, 1)
                    pe.wait_ge(ke_done, h + 1)
                    pe.wait_ge(qa_done, h + 1)
                    for c_ in range(TILES):
                        last = nc.tensor.matmul(ps[ATT][:, c_ * P:(c_ + 1) * P], ke[:, c_ * P:(c_ + 1) * P], qa[:, par, c_, 0:4:3, :], start=True, stop=True)
                    last.then_inc(att_ready, 1)
                    pe.wait_ge(kt_copied, h + 1)
                    pe.wait_ge(vs_evac, h + 1)
                    if h >= 1:
                        pe.wait_ge(st_done, (NCH + 1) * h)
                    nc.tensor.matmul(ps[CS][:, 0:DV], ktm[:, :], vm[:, par, :], start=True, stop=True).then_inc(cs_ready, 1)
                elif kind == "chunk":
                    t = h * TILES + c
                    if c == 0:
                        pe.wait_ge(att_done, h + 1)
                    if t >= 1:
                        pe.wait_ge(o_copied, t)
                    nc.tensor.matmul(ps[O][:, 0:DV], att[:, c, :], vt[:, par, c, :], start=True, stop=False)
                    for half in range(2):
                        j = 2 * c + half
                        pe.wait_ge(st_done, (NCH + 1) * h + j + 1)
                        rows = slice(half * GCH, (half + 1) * GCH)
                        last = nc.tensor.matmul(ps[O][:, 0:DV], qa[:, par, c, 2 * half:2 * half + 2, :], st[:, par, j % 2, :], start=False, stop=half == 1)
                        if half == 1:
                            last.then_inc(o_ready, 1)
                        nc.tensor.matmul(ps[CS][:, 0:DV], kt_[rows, c, :], vt[rows, par, c, :], start=True, stop=True).then_inc(cs_ready, 1)
                else:
                    pe.wait_ge(qm_done, h + 1)
                    pe.wait_ge(kt_copied, h + 1)
                    pe.wait_ge(att_done, h + 1)

                    def spread(b_):
                        q = h * NSAMP + b_
                        if q >= 2:
                            pe.wait_ge(gs_done, q - 1)
                        nc.tensor.matmul(ps[(CUM, ATT)[b_ % 2]][:, 0:DV], k.sel8[:, b_, :], vs[:, par, :], start=True, stop=True).then_inc(sv_ready, 1)

                    spread(0)
                    for b_ in range(NSAMP):
                        if b_ + 1 < NSAMP:
                            spread(b_ + 1)
                        pe.wait_ge(gs_done, h * NSAMP + b_ + 1)
                        last = nc.tensor.matmul(ps[MISC][0:NSAMP, 0:DV], qmask[:, b_, :], gs[:, b_, :], start=b_ == 0, stop=b_ == NSAMP - 1)
                    last.then_inc(os_ready, 1)

        @block.scalar
        def _(act):
            act.wait_ge(ones_set, 1)
            act.wait_ge(glr_ready, 1)
            nc.scalar.copy(glrT[0:RANK, SM:COLS], ps[0][0:RANK, :])
            nc.scalar.copy(glrT[0:RANK, 0:SM], ps[SMALL][0:RANK, 0:SM]).then_inc(glr_copied, 1)
            act.wait_ge(gk_ready, 1)
            parts = [(gk[:, c, :], ps[CUM + c][:, :]) for c in range(TILES)]
            parts += [(gkm[:, :], ps[MISC][0:NMETA, :]), (gks[:, :, :].rearrange("p h b -> p (h b)"), ps[SMALL][:, 0:GH * NSAMP])]
            for dst, src in parts:
                last = nc.scalar.activation(dst, src, ACT.Abs)
            k.alink(act, last)
            for dst, src in parts:
                last = nc.scalar.activation(dst, dst, ACT.Exp, scale=-1.0)
            k.alink(act, last)
            for dst, src in parts:
                last = nc.scalar.activation(dst, dst, ACT.Ln, bias=1.0)
            last.then_inc(gk_ln, 1)
            act.wait_ge(gk_done, 1)
            nc.scalar.activation(gks[:, :, :], gks[:, :, :], ACT.Exp, scale=1.0 / 16.0).then_inc(gs_exp, 1)
            for kind, h, c in order:
                par = h % 2
                if kind in ("q", "k"):
                    n = h * NP + (kind == "k")
                    act.wait_ge(proj_ready, n + 1)
                    if kind == "q" and h >= 2:
                        act.wait_ge(os_done, h - 1)
                    if kind == "q":
                        nc.scalar.mul(qT[:, par, :], ps[n % 2][:, :], QSCALE)
                        nc.scalar.mul(qs[:, par, :], ps[SMALL][:, 0:NSAMP], QSCALE).then_inc(proj_evac, 1)
                    else:
                        nc.scalar.copy(kT[:, par, NMETA:NMETA + SEQ], ps[n % 2][:, :])
                        nc.scalar.copy(kT[:, par, 0:NMETA], ps[SMALL][:, META0:SM])
                        nc.scalar.copy(ks[:, par, :], ps[SMALL][:, 0:NSAMP]).then_inc(proj_evac, 1)
                elif kind == "v":
                    n = h * NP + 2 + c
                    act.wait_ge(proj_ready, n + 1)
                    nc.scalar.copy(vt[:, par, c, :], ps[n % 2][:, 0:DV]).then_inc(proj_evac, 1)
                elif kind == "vsmall":
                    act.wait_ge(vs_ready, h + 1)
                    nc.scalar.copy(vm[:, par, :], ps[SMALL][0:NMETA, 0:DV])
                    nc.scalar.copy(vs[:, par, :], ps[SMALL][0:NSAMP, DV:2 * DV]).then_inc(vs_evac, 1)
                elif kind == "prep":
                    act.wait_ge(bend_done, h + 1)
                    if h >= 1:
                        act.wait_ge(qa_done, h)
                        act.wait_ge(att_ready, h)
                        act.wait_ge(kt_ready, h)
                    nc.scalar.activation(ep[:, :], ps[CUM][:, :], ACT.Exp)
                    nc.scalar.activation(ke[:, :], ps[CUM][:, :], ACT.Exp, scale=-1.0)
                    for j in range(NCH):
                        nc.scalar.activation(kd[:, NMETA + j * GCH:NMETA + (j + 1) * GCH], ps[CUM][:, j * GCH:(j + 1) * GCH], ACT.Exp,
                                             scale=-1.0, bias=bend[:, j:j + 1])
                    nc.scalar.activation(kd[:, 0:NMETA], ps[MISC][:, 0:NMETA], ACT.Exp, scale=-1.0, bias=bend[:, NCH:NCH + 1])
                    nc.scalar.activation(cdg[:, par, :], bend[:, 0:NCH], ACT.Exp).then_inc(exp_done, 1)
                elif kind == "fold":
                    act.wait_ge(kt_ready, h + 1)
                    if h >= 1:
                        act.wait_ge(cs_ready, (NCH + 1) * h)
                    nc.scalar.copy(kt_[:, :, :].rearrange("p c d -> p (c d)"), ps[CUM][:, :])
                    nc.scalar.copy(ktm[:, :], ps[MISC][0:NMETA, 0:DK]).then_inc(kt_copied, 1)
                elif kind == "chunk":
                    t = h * TILES + c
                    act.wait_ge(o_ready, t + 1)
                    nc.scalar.copy(k.o[:, c, h * DV:(h + 1) * DV], ps[O][:, 0:DV]).then_inc(o_copied, 1)

        @block.vector
        def _(dve):
            nc.vector.memset(glrT[:, :], 1.0).then_inc(ones_set, 1)
            nc.vector.memset(att[:, :, :], 0.0)
            k.vlink(dve, nc.vector.memset(qa[:, :, :, :, :], 0.0))
            dve.wait_ge(gk_ln, 1)
            parts = [(gk[:, c, :], ps[CUM + c][:, :]) for c in range(TILES)]
            parts += [(gkm[:, :], ps[MISC][0:NMETA, :]), (gks[:, :, :].rearrange("p h b -> p (h b)"), ps[SMALL][:, 0:GH * NSAMP])]
            for dst, src in parts:
                last = nc.vector.scalar_tensor_tensor(dst, src, 0.0, dst, ALU.min, ALU.subtract)
            last.then_inc(gk_done, 1)
            for kind, h, c in order:
                par = h % 2
                if kind == "prep":
                    dve.wait_ge(cum_ready, h + 1)
                    if h >= 1:
                        dve.wait_ge(exp_done, h)
                    nc.vector.tensor_copy(bend[:, 0:NCH], ps[CUM][:, GCH - 1:SEQ:GCH])
                    nc.vector.tensor_copy(bend[:, NCH:NCH + 1], ps[MISC][:, NMETA - 1:NMETA]).then_inc(bend_done, 1)
                    dve.wait_ge(exp_done, h + 1)
                    dve.wait_ge(proj_evac, h * NP + 2)
                    nc.vector.tensor_tensor(ke[:, :], kT[:, par, NMETA:NMETA + SEQ], ke[:, :], ALU.mult).then_inc(ke_done, 1)
                elif kind == "fold":
                    dve.wait_ge(att_ready, h + 1)
                    if h >= 1:
                        dve.wait_ge(o_ready, TILES * h)
                    nc.vector.copy_predicated(att[:, :, :], k.att_mask[:, :].unsqueeze(1).to_broadcast([P, TILES, P]),
                                              ps[ATT][:, :].rearrange("p (c t) -> p c t", c=TILES)).then_inc(att_done, 1)
                    dve.wait_ge(cs_ready, (NCH + 1) * h + 1)
                    if h >= 2:
                        dve.wait_ge(st_out, 16 * (h - 1))
                    nc.vector.tensor_copy(st[:, par, 0, :], ps[CS][:, 0:DV]).then_inc(st_done, 1)
                elif kind == "chunk":
                    for half in range(2):
                        j = 2 * c + half
                        dve.wait_ge(cs_ready, (NCH + 1) * h + j + 2)
                        dve.wait_ge(st_done, (NCH + 1) * h + j + 1)
                        nc.vector.scalar_tensor_tensor(st[:, par, (j + 1) % 2, :], st[:, par, j % 2, :], cdg[:, par, j:j + 1],
                                                       ps[CS][:, 0:DV], ALU.mult, ALU.add).then_inc(st_done, 1)
                elif kind == "sample":
                    dve.wait_ge(proj_evac, h * NP + 2)
                    if h >= 1:
                        dve.wait_ge(os_ready, h)
                    nc.vector.tensor_tensor(qmask[:, :, :], k.eye8[:, :, :], qs[:, par, :].unsqueeze(1).to_broadcast([P, NSAMP, NSAMP]),
                                            ALU.mult).then_inc(qm_done, 1)
                    for b in range(NSAMP):
                        q = h * NSAMP + b
                        dve.wait_ge(sdec_done, q + 1)
                        dve.wait_ge(sv_ready, q + 1)
                        nc.vector.scalar_tensor_tensor(gs[:, b, :], ps[(CUM, ATT)[b % 2]][:, 0:DV], ks[:, par, b:b + 1],
                                                       gs[:, b, :], ALU.mult, ALU.add).then_inc(gs_done, 1)
                    dve.wait_ge(os_ready, h + 1)
                    nc.vector.tensor_copy(k.os[:, h * DV:(h + 1) * DV], ps[MISC][0:NSAMP, 0:DV]).then_inc(os_done, 1)

        @block.gpsimd
        def _(pool):
            pool.wait_ge(gs_exp, 1)
            for kind, h, c in order:
                par = h % 2
                if kind == "prep":
                    pool.wait_ge(exp_done, h + 1)
                    pool.wait_ge(proj_evac, h * NP + 2)
                    if h >= 2:
                        pool.wait_ge(os_done, h - 1)
                    nc.gpsimd.tensor_tensor(qa[:, par, :, 0:4:3, :], qT[:, par, :].rearrange("p (c a t) -> p c a t", c=TILES, a=2),
                                            ep[:, :].rearrange("p (c a t) -> p c a t", c=TILES, a=2), ALU.mult).then_inc(qa_done, 1)
                    nc.gpsimd.tensor_tensor(kd[:, :], kT[:, par, :], kd[:, :], ALU.mult).then_inc(kd_done, 1)
                elif kind == "fold":
                    pool.wait_ge(gs_here, 16 * (h + 1))
                    for b in range(NSAMP):
                        nc.gpsimd.tensor_scalar(gs[:, b, :], gs[:, b, :], gks[:, h, b:b + 1], None, ALU.mult).then_inc(sdec_done, 1)


def stage_gate(nc, k):
    TOKENS = TILES + 1
    z_items = [("z", g, c) for g in range(GROUPS) for c in range(TOKENS)]
    g_items = [("g", i, c) for i in range(2) for c in range(TOKENS)]
    y_turns = [(c, g) for c in range(TOKENS) for g in range(GROUPS)]
    o_turns = [(c, i) for c in range(TOKENS) for i in range(2)]
    NZ, NG = len(z_items), len(g_items)
    rows = [P] * TILES + [NSAMP]
    cols = lambda c: tile_cols(c) if c < TILES else slice(0, NSAMP)
    out_cols = lambda c: slice(c * P, c * P + rows[c])
    BANKS, BUFS = 4, 3
    with ExitStack() as ctx:
        sb = lambda n, s, d=F32: ctx.enter_context(nc.sbuf_tensor("t_" + n, s, d, side="right"))
        sem = lambda n: k.sem("t_" + n)
        gate = sb("gate", [P, BUFS, 512])
        ssy = sb("ssy", [P, TOKENS, GROUPS])
        sso = sb("sso", [P, TOKENS, GH])
        wy = sb("wy", [P, GROUPS * 4])
        wo = sb("wo", [P, KD])
        ins_here, item_ready, item_gated, mul_done, sq_done, zero_done = map(sem, ("ins_here", "item_ready", "item_gated", "mul_done", "sq_done", "zero_done"))
        osq_done, mean_done, root_done, ynorm_done, turn_ready, turn_done = map(
            sem, ("osq_done", "mean_done", "root_done", "ynorm_done", "turn_ready", "turn_done"))
        k.block_used.update({FIRST["z"] + g: (item_ready, TOKENS * (g + 1)) for g in range(GROUPS)})
        k.block_used.update({FIRST["g"] + i: (item_ready, NZ + TOKENS * (i + 1)) for i in range(2)})
        ps = k.ps
        y_of = lambda c, g: (k.y[:, c, g * GW:(g + 1) * GW] if c < TILES else k.ys[:, g * GW:(g + 1) * GW])
        o_of = lambda c, h: (k.o[:, c, h * DV:(h + 1) * DV] if c < TILES else k.os[:, h * DV:(h + 1) * DV])
        turns = [("y", c, g) for c, g in y_turns] + [("o", c, i) for c, i in o_turns]
        block = ctx.enter_context(nc.Block())

        @block.sync
        def _(sp):
            for dst, src in ((wy[:, :], k.dram["ssd_norm"]), (wo[:, :], k.dram["gla_norm"])):
                sp.dma_start(dst, src).then_inc(ins_here, 16)
            for b in range(FIRST["z"], FIRST["merge"]):
                load_block(sp, k, b + 2)

        @block.tensor
        def _(pe):
            def project(n, kind, i, c):
                b = FIRST[kind] + i
                if c == 0:
                    wait_block(pe, k, b)
                if n >= BANKS:
                    pe.wait_ge(item_gated, n - BANKS + 1)
                w = k.ring[b % 2][:, 0:KD * 512].rearrange("p (k c) -> p k c", k=KD)
                for kt in range(KD):
                    last = nc.tensor.matmul(ps[n % BANKS][0:rows[c], :], k.xnT[:, kt, cols(c)], w[:, kt, :], start=kt == 0, stop=kt == KD - 1)
                last.then_inc(item_ready, 1)

            def turn(m):
                kind, c, i = turns[m]
                if kind == "y":
                    pe.wait_ge(ynorm_done, m + 1)
                elif i == 0 and c == 0:
                    pe.wait_ge(mul_done, NZ + NG)
                if m >= 2:
                    pe.wait_ge(turn_done, m - 1)
                for a in range(4):
                    src = y_of(c, i)[:, a * P:(a + 1) * P] if kind == "y" else o_of(c, 2 * i + a // 2)[:, (a % 2) * P:(a % 2 + 1) * P]
                    last = nc.tensor.transpose(ps[BANKS + m % 2][:, a * P:a * P + rows[c]], src, k.ident[0:rows[c], 0:rows[c]])
                last.then_inc(turn_ready, 1)

            for n, item in enumerate(z_items):
                project(n, *item)
            for j, item in enumerate(g_items):
                project(NZ + j, *item)
                turn(2 * j)
                turn(2 * j + 1)
            for m in range(2 * NG, len(turns)):
                turn(m)

        @block.scalar
        def _(act):
            act.wait_ge(zero_done, 1)
            for c in range(TOKENS):
                for h in range(GH):
                    at = (c * GH + h) * DV
                    last = nc.scalar.activation(k.yT[0:rows[c], :, :].rearrange("p a b -> p (a b)")[:, at:at + DV], o_of(c, h),
                                                ACT.Square, accum_out=sso[0:rows[c], c, h:h + 1])
            last.then_inc(osq_done, 1)

            def square(n):
                _, g, c = z_items[n]
                act.wait_ge(mul_done, n + 1)
                nc.scalar.activation(gate[0:rows[c], n % BUFS, :], y_of(c, g), ACT.Square, accum_out=ssy[0:rows[c], c, g:g + 1]).then_inc(sq_done, 1)

            for n, (kind, g, c) in enumerate(z_items + g_items):
                act.wait_ge(item_ready, n + 1)
                if n >= BUFS:
                    act.wait_ge(mul_done, n - BUFS + 1)
                    act.wait_ge(sq_done, min(n - BUFS + 1, NZ))
                nc.scalar.activation(gate[0:rows[c], n % BUFS, :], ps[n % BANKS][0:rows[c], :], ACT.Silu).then_inc(item_gated, 1)
                if 1 <= n < NZ:
                    square(n - 1)
                if n == NZ - 1:
                    square(n)
                    act.wait_ge(mean_done, 1)
                    nc.scalar.activation(ssy[:, :, :], ssy[:, :, :], ACT.Sqrt)
                    nc.scalar.activation(sso[:, :, :], sso[:, :, :], ACT.Sqrt).then_inc(root_done, 1)

        @block.vector
        def _(dve):
            nc.vector.memset(ssy[:, :, :], 1.0)
            nc.vector.memset(sso[:, :, :], 1.0).then_inc(zero_done, 1)
            dve.wait_ge(ins_here, 32)
            for n, (_, g, c) in enumerate(z_items):
                dve.wait_ge(item_gated, n + 1)
                nc.vector.tensor_tensor(y_of(c, g), y_of(c, g), gate[0:rows[c], n % BUFS, :], ALU.mult).then_inc(mul_done, 1)
            dve.wait_ge(sq_done, NZ)
            dve.wait_ge(osq_done, 1)
            nc.vector.tensor_scalar(ssy[:, :, :], ssy[:, :, :], 1.0 / GW, EPS, ALU.mult, ALU.add)
            nc.vector.tensor_scalar(sso[:, :, :], sso[:, :, :], 1.0 / DV, EPS, ALU.mult, ALU.add).then_inc(mean_done, 1)
            dve.wait_ge(root_done, 1)
            nc.vector.reciprocal(ssy[:, :, :], ssy[:, :, :])
            k.vlink(dve, nc.vector.reciprocal(sso[:, :, :], sso[:, :, :]))
            for c, g in y_turns:
                nc.vector.tensor_scalar(y_of(c, g), y_of(c, g), ssy[0:rows[c], c, g:g + 1], None, ALU.mult).then_inc(ynorm_done, 1)

            def turn(m):
                kind, c, i = turns[m]
                dve.wait_ge(turn_ready, m + 1)
                w, dst = (wy, k.yT) if kind == "y" else (wo, k.oT)
                nc.vector.tensor_tensor(dst[:, 4 * i:4 * i + 4, out_cols(c)],
                                        ps[BANKS + m % 2][:, :].rearrange("p (a t) -> p a t", a=4)[:, :, 0:rows[c]],
                                        w[:, 4 * i:4 * i + 4].unsqueeze(2).to_broadcast([P, 4, rows[c]]), ALU.mult).then_inc(turn_done, 1)

            for j, (_, i, c) in enumerate(g_items):
                n = NZ + j
                dve.wait_ge(item_gated, n + 1)
                for a in range(2):
                    h = 2 * i + a
                    last = nc.vector.scalar_tensor_tensor(o_of(c, h), o_of(c, h), sso[0:rows[c], c, h:h + 1],
                                                          gate[0:rows[c], n % BUFS, a * DV:(a + 1) * DV], ALU.mult, ALU.mult)
                last.then_inc(mul_done, 1)
                turn(2 * j)
                turn(2 * j + 1)
            for m in range(2 * NG, len(turns)):
                turn(m)


TOK = SEQ + NSAMP


def stage_merge(nc, k):
    KY = GROUPS * GW // P
    MAINS = 6
    with ExitStack() as ctx:
        sb = lambda n, s, d=F32: ctx.enter_context(nc.sbuf_tensor("m_" + n, s, d, side="right"))
        sem = lambda n: k.sem("m_" + n)
        sig = sb("sig", [P, 2, 2, TOK])
        term = sb("term", [P, 2, TOK])
        main_ready, small_ready, sig_done, ssig_done, out_done, sout_done = map(
            sem, ("main_ready", "small_ready", "sig_done", "ssig_done", "out_done", "sout_done"))
        k.block_used.update({FIRST["merge"] + j: (small_ready, j + 1) for j in range(KD)})
        ps = k.ps
        block = ctx.enter_context(nc.Block())

        @block.sync
        def _(sp):
            for b in range(FIRST["merge"], FIRST["out"]):
                load_block(sp, k, b + 2)

        @block.tensor
        def _(pe):
            for j in range(KD):
                b = FIRST["merge"] + j
                wait_block(pe, k, b)
                w = k.ring[b % 2][:, 0:(3 * KD + KY) * P].rearrange("p (k c) -> p k c", c=P)
                parts = [(0, KD, k.xnT, SM, 0), (KD, KD, k.xnT, SM, 0), (2 * KD, KY, k.yT, 0, SEQ), (2 * KD + KY, KD, k.oT, 0, SEQ)]
                for i, (k0, n_k, src, at, _) in enumerate(parts):
                    n = 4 * j + i
                    if n >= MAINS:
                        if i < 2:
                            pe.wait_ge(out_done, 2 * (j - 2) + i + 1)
                        else:
                            pe.wait_ge(sig_done, 2 * (j - 1) + i - 1)
                    for kt in range(n_k):
                        last = nc.tensor.matmul(ps[n % MAINS][:, :], w[:, k0 + kt, :], src[:, kt, at:at + SEQ], start=kt == 0, stop=kt == n_k - 1)
                    last.then_inc(main_ready, 1)
                if j >= 2:
                    pe.wait_ge(sout_done, j - 1)
                for i, (k0, n_k, src, _, at) in enumerate(parts):
                    for kt in range(n_k):
                        last = nc.tensor.matmul(ps[MAINS + j % 2][:, i * NSAMP:(i + 1) * NSAMP], w[:, k0 + kt, :], src[:, kt, at:at + NSAMP],
                                                start=kt == 0, stop=kt == n_k - 1)
                last.then_inc(small_ready, 1)

        @block.scalar
        def _(act):
            for j in range(KD):
                for i in range(2):
                    n = 4 * j + i
                    act.wait_ge(main_ready, n + 1)
                    if j >= 2:
                        act.wait_ge(sout_done, j - 1)
                    nc.scalar.activation(sig[:, j % 2, i, 0:SEQ], ps[n % MAINS][:, :], ACT.Sigmoid).then_inc(sig_done, 1)
                act.wait_ge(small_ready, j + 1)
                nc.scalar.activation(sig[:, j % 2, :, SEQ:TOK], ps[MAINS + j % 2][:, 0:2 * NSAMP].rearrange("p (i b) -> p i b", i=2),
                                     ACT.Sigmoid).then_inc(ssig_done, 1)

        @block.vector
        def _(dve):
            for j in range(KD):
                for i in range(2):
                    n = 4 * j + 2 + i
                    dve.wait_ge(main_ready, n + 1)
                    dve.wait_ge(sig_done, 2 * j + i + 1)
                    dst = k.mixT[:, j, 0:SEQ] if i == 0 else term[:, j % 2, 0:SEQ]
                    nc.vector.tensor_tensor(dst, ps[n % MAINS][:, :], sig[:, j % 2, i, 0:SEQ], ALU.mult).then_inc(out_done, 1)
                dve.wait_ge(ssig_done, j + 1)
                small = ps[MAINS + j % 2]
                nc.vector.tensor_tensor(k.mixT[:, j, SEQ:TOK], small[:, 2 * NSAMP:3 * NSAMP], sig[:, j % 2, 0, SEQ:TOK], ALU.mult)
                k.vlink(dve, nc.vector.tensor_tensor(term[:, j % 2, SEQ:TOK], small[:, 3 * NSAMP:4 * NSAMP], sig[:, j % 2, 1, SEQ:TOK], ALU.mult))
                dve.wait_ge(out_done, 2 * j + 2)
                nc.vector.tensor_tensor(k.mixT[:, j, :], k.mixT[:, j, :], term[:, j % 2, :], ALU.add).then_inc(sout_done, 1)


def stage_out(nc, k):
    TOKENS = TILES + 1
    rows = [P] * TILES + [NSAMP]
    mix_cols = lambda c: slice(c * P, c * P + rows[c])
    BANKS = 4
    with ExitStack() as ctx:
        sb = lambda n, s, d=F32: ctx.enter_context(nc.sbuf_tensor("q_" + n, s, d, side="right"))
        sem = lambda n: k.sem("q_" + n)
        prompt_x1 = sb("x1", [P, TILES, D])
        prompt_hn = sb("hn", [P, TILES, D])
        ss = sb("ss", [P, TOKENS])
        x1_of = lambda c: prompt_x1[:, c, :] if c < TILES else k.x1s[:, :]
        hn_of = lambda c: prompt_hn[:, c, :] if c < TILES else k.hns[:, :]
        ins_here, out_ready, x1_done, sq_done, mean_done, root_done = map(
            sem, ("ins_here", "out_ready", "x1_done", "sq_done", "mean_done", "root_done"))
        hn_done, turn_ready, turn_done, stored = map(sem, ("hn_done", "turn_ready", "turn_done", "stored"))
        k.block_used.update({FIRST["out"] + i: (out_ready, TOKENS * (i + 1)) for i in range(2)})
        ps = k.ps
        block = ctx.enter_context(nc.Block())

        @block.sync
        def _(sp):
            for c in range(TOKENS):
                lo = SM + c * P if c < TILES else 0
                sp.dma_start(x1_of(c), k.dram["x_all"][lo:lo + rows[c], :]).then_inc(ins_here, 16)
            sp.dma_start(k.w2[:, :], k.dram["norm2"]).then_inc(ins_here, 16)
            for h in range(2):
                sp.dma_start(k.qw[:, h, :], k.dram["w"]["query"][h]).then_inc(k.qw_here[h], 16)
            sp.dma_start(k.keys[:, :, :], k.dram["keys"]).then_inc(ins_here, 16)
            for c in range(TILES):
                sp.wait_ge(x1_done, TOKENS + c + 1)
                sp.dma_start(k.x1_dram[c * P:(c + 1) * P, :], x1_of(c)).then_inc(stored, 16)
            sp.wait_ge(stored, 16 * TILES)

        @block.tensor
        def _(pe):
            def turn(c):
                pe.wait_ge(hn_done, c + 1)
                for half in range(2):
                    m = 2 * c + half
                    if m >= 2:
                        pe.wait_ge(turn_done, m - 1)
                    for a in range(4):
                        kt = 4 * half + a
                        last = nc.tensor.transpose(ps[4 + m % 2][:, a * P:a * P + rows[c]], hn_of(c)[:, kt * P:(kt + 1) * P],
                                                   k.ident[0:rows[c], 0:rows[c]])
                    last.then_inc(turn_ready, 1)

            for i in range(2):
                b = FIRST["out"] + i
                wait_block(pe, k, b)
                w = k.ring[b % 2][:, 0:KD * 512].rearrange("p (k c) -> p k c", k=KD)
                for c in range(TOKENS):
                    n = i * TOKENS + c
                    if n >= BANKS:
                        pe.wait_ge(x1_done, n - BANKS + 1)
                    for kt in range(KD):
                        last = nc.tensor.matmul(ps[n % BANKS][0:rows[c], :], k.mixT[:, kt, mix_cols(c)], w[:, kt, :], start=kt == 0, stop=kt == KD - 1)
                    last.then_inc(out_ready, 1)
                    if i == 1 and c >= 1:
                        turn(c - 1)
            turn(TILES)

        @block.vector
        def _(dve):
            dve.wait_ge(ins_here, 16 * (TOKENS + 2))
            for i in range(2):
                for c in range(TOKENS):
                    n = i * TOKENS + c
                    dve.wait_ge(out_ready, n + 1)
                    v = x1_of(c)[:, i * 512:(i + 1) * 512]
                    nc.vector.tensor_tensor(v, v, ps[n % BANKS][0:rows[c], :], ALU.add).then_inc(x1_done, 1)
                    if i == 0:
                        continue
                    dve.wait_ge(sq_done, c + 1)
                    nc.vector.tensor_scalar(ss[0:rows[c], c:c + 1], ss[0:rows[c], c:c + 1], 1.0 / D, EPS, ALU.mult, ALU.add).then_inc(mean_done, 1)
                    dve.wait_ge(root_done, c + 1)
                    k.vlink(dve, nc.vector.reciprocal(k.rs2[0:rows[c], c:c + 1], ss[0:rows[c], c:c + 1]))
                    nc.vector.scalar_tensor_tensor(hn_of(c), x1_of(c), k.rs2[0:rows[c], c:c + 1], k.w2[0:rows[c], :], ALU.mult, ALU.mult).then_inc(hn_done, 1)

        @block.scalar
        def _(act):
            def copies(c):
                for half in range(2):
                    act.wait_ge(turn_ready, 2 * c + half + 1)
                    nc.scalar.copy(k.hnT[:, 4 * half:4 * half + 4, mix_cols(c)],
                                   ps[4 + half][:, :].rearrange("p (a t) -> p a t", a=4)[:, :, 0:rows[c]]).then_inc(turn_done, 1)

            for c in range(TOKENS):
                act.wait_ge(x1_done, TOKENS + c + 1)
                nc.scalar.activation(hn_of(c), x1_of(c), ACT.Square, accum_out=ss[0:rows[c], c:c + 1]).then_inc(sq_done, 1)
                act.wait_ge(mean_done, c + 1)
                nc.scalar.activation(ss[0:rows[c], c:c + 1], ss[0:rows[c], c:c + 1], ACT.Sqrt).then_inc(root_done, 1)
                if c >= 1:
                    copies(c - 1)
            copies(TILES)


def stage_peer(nc, k):
    UNITS = TILES * EH
    RING = 8
    LOT = 8
    PAIR = 2
    DIAGS = 4
    PARTS_AFTER = (1, 3, 5, 6)
    AHEAD = 3
    SROWS = NSAMP * EH
    SLOTS = TOPK
    QUERY_SLOTS, SCORE_SLOT, QUERY_COPIES = (0, 6), 12, (2, 5)
    LOW = -3.4e38
    with ExitStack() as ctx:
        sb = lambda n, s, d=F32, side="left": ctx.enter_context(nc.sbuf_tensor("p_" + n, s, d, side=side))
        sem = lambda n: k.sem("p_" + n)
        rows = sb("rows", [P, RING, ROW])
        wf = sb("wf", [P, D])
        hn_cur = sb("hn_cur", [P, D])
        idx = sb("idx", [P, (UNITS + 2) * SLOTS], U32)
        gates = sb("gates", [P, (UNITS + 2) * SLOTS])
        sidx = sb("sidx", [SROWS, SLOTS], U32)
        sgates = sb("sgates", [SROWS, SLOTS])
        sc = sb("sc", [P, UNITS + 2, 2 * NKEYS])
        ssc = sb("ssc", [SROWS, 2 * NKEYS])
        ssc_head = sb("ssc_head", [NSAMP, 2, 2 * NKEYS])
        q = sb("q", [P, 2, TOK])
        x1_in = sb("x1_in", [P, D])
        ssel = sb("ssel", [SROWS, NSAMP])
        ssel_t = sb("ssel_t", [NSAMP, SROWS])
        lot = sb("lot", [P, 2, LOT], U32)
        hid = sb("hid", [P, SLOTS])
        gel = sb("gel", [P, SLOTS])
        diag = sb("diag", [P, DIAGS, P])
        zeros = sb("zeros", [P, 512])
        fin = sb("fin", [P, D])
        sfin = k.x1s
        squares = sb("squares", [P, D])
        fss = sb("fss", [P, 2])
        tv = sb("tv", [P, 2, TOPK])
        ti = sb("ti", [P, 2, TOPK], U32)
        tif = sb("tif", [P, 2, TOPK])
        rest = sb("rest", [P, 2, NKEYS])
        cand = sb("cand", [P, TOPK, TOPK])
        crest = sb("crest", [P, TOPK, TOPK])
        bv = sb("bv", [P, TOPK])
        bp = sb("bp", [P, TOPK], U32)
        ab = sb("ab", [P, 2, TOPK], U32)
        abf = sb("abf", [P, 2, TOPK])
        hot = sb("hot", [P, 2, TOPK, TOPK])
        pick = sb("pick", [P, 2, TOPK])
        pickf = sb("pickf", [P, TOPK])
        iota = sb("iota", [P, TOPK])
        scu = sb("scu", [P, 2 * NKEYS])
        nmax = sb("nmax", [P, 1])
        ex = sb("ex", [P, TOPK])
        esum = sb("esum", [P, 1])
        ins_here, lot_here, dot_done, gelu_done, diag_done, used = map(
            sem, ("ins_here", "lot_here", "dot_done", "gelu_done", "diag_done", "used"))
        row_here = [sem(f"row_here{j}") for j in range(RING)]
        choice, best_done, exp_done, cleared, hn_rep, hn_cur_done = map(
            sem, ("choice", "best_done", "exp_done", "cleared", "hn_rep", "hn_cur_done"))
        acc_closed, fin_done, fsq_done, fmean, froot, out_ready, out_done, turn = map(
            sem, ("acc_closed", "fin_done", "fsq_done", "fmean", "froot", "out_ready", "out_done", "turn"))
        x1_here, opened, computed, copied, ssc_here = map(sem, ("x1_here", "opened", "computed", "copied", "ssc_here"))
        ps = k.ps
        ACC, SACC, REP = (0, 1), (2, 3), (4, 5)
        Q, SQ, SC, SSC = (2, 3), (4, 5), (6, 7), 4
        INS = 5
        CHOICE_STEPS = 21
        block = ctx.enter_context(nc.Block())

        @block.sync
        def _(sp):
            def load_x1(tile):
                sp.dma_start(x1_in[:, :], k.x1_dram[bass.ds(tile * P, P), :]).then_inc(x1_here, 16)

            load_x1(0)
            for dst, src in ((wf[:, :], k.dram["norm_f"]), (iota[:, :], k.dram["c_iota"]), (ssel[:, :], k.dram["c_ssel"]), (ssel_t[:, :], k.dram["c_ssel_t"]),
                             (zeros[:, :], k.dram["c_zeros"])):
                sp.dma_start(dst, src).then_inc(ins_here, 16)
            for h in range(EH):
                if h + 2 < EH:
                    sp.wait_ge(computed, 3 * h + 2)
                    sp.dma_start(k.qw[:, h % 2, :], k.dram["w"]["query"][h + 2]).then_inc(k.qw_here[h % 2], 16)
                sp.wait_ge(copied, 5 * h + 5)
                if h >= 1:
                    sp.wait_ge(ssc_here, 16 * h)
                sp.dma_start(ssc[h * NSAMP:(h + 1) * NSAMP, :], ssc_head[:, h % 2, :]).then_inc(ssc_here, 16)
            sp.wait_ge(opened, 1)
            sp.wait_ge(hn_cur_done, 1)
            load_x1(1)
            sp.wait_ge(out_ready, 1)
            sp.dma_start(k.dram["o_prompt"][0:P, :], fin[:, :]).then_inc(out_done, 16)
            sp.wait_ge(out_ready, 2)
            sp.dma_start(k.dram["o_sample"], sfin[:, :]).then_inc(out_done, 16)
            with sp.Fori(1, TILES - 1) as c:
                sp.wait_ge(opened, c + 1)
                sp.sem_inc(turn, 1)
                sp.wait_ge(hn_cur_done, c + 2)
                sp.sem_inc(turn, 1)
                load_x1(c + 1)
                sp.wait_ge(out_ready, c + 2)
                sp.sem_inc(turn, 1)
                sp.dma_start(k.dram["o_prompt"][bass.ds(c * P, P), :], fin[:, :]).then_inc(out_done, 16)
            sp.wait_ge(out_ready, TILES + 1)
            sp.dma_start(k.dram["o_prompt"][SEQ - P:SEQ, :], fin[:, :]).then_inc(out_done, 16)
            sp.wait_ge(out_done, 16 * (TILES + 1))

        @block.gpsimd
        def _(pool):
            def gathers(m, unit):
                for s in range(SLOTS):
                    if s % LOT == 0:
                        pool.wait_ge(lot_here, unit * 2 + s // LOT + 1)
                        pool.sem_inc(turn, 1)
                    pool.wait_ge(used, unit * SLOTS + s + 1)
                    pool.sem_inc(turn, 1)
                    nc.gpsimd.indirect_dma_start(rows[0:m, s % RING, :], None, k.dram["experts"],
                                                 bass.IndirectOffsetOnAxis(lot[0:m, s // LOT, s % LOT:s % LOT + 1], 0)).then_inc(row_here[s % RING], 16)

            with pool.Fori(0, EH) as i:
                gathers(P, i)
            gathers(SROWS, EH)
            with pool.Fori(EH, UNITS) as i:
                gathers(P, i + 1)

        @block.vector
        def _(dve):
            def choice_parts(m, scores, idx_out, gates_out, turn_no, wait=lambda: None):
                count = [0]

                def link(ins):
                    count[0] += 1
                    ins.then_inc(choice, 1)
                    dve.wait_ge(choice, turn_no * CHOICE_STEPS + count[0])
                    dve.sem_inc(turn, 1)

                def best16(values, rest_, top, where):
                    link(nc.vector.max(top[:, 0:8], values))
                    nc.vector.max_index(where[:, 0:8], top[:, 0:8], values)
                    link(nc.vector.match_replace(rest_, top[:, 0:8], values, LOW))
                    link(nc.vector.max(top[:, 8:16], rest_))
                    nc.vector.max_index(where[:, 8:16], top[:, 8:16], rest_)

                flat = lambda t: t[0:m, :, :].rearrange("p a b -> p (a b)")
                grid = [m, TOPK, TOPK]

                def keys(s):
                    best16(scu[0:m, s * NKEYS:(s + 1) * NKEYS], rest[0:m, s, :], tv[0:m, s, :], ti[0:m, s, :])

                def part0():
                    wait()
                    link(nc.vector.tensor_copy(scu[0:m, :], scores))
                    keys(0)

                def part1():
                    keys(1)

                def part2():
                    link(nc.vector.tensor_tensor(cand[0:m], tv[0:m, 0, :].unsqueeze(2).to_broadcast(grid), tv[0:m, 1, :].unsqueeze(1).to_broadcast(grid), ALU.add))
                    nc.vector.tensor_copy(tif[0:m], ti[0:m])
                    link(nc.vector.max(bv[0:m, 0:8], flat(cand)))
                    nc.vector.max_index(bp[0:m, 0:8], bv[0:m, 0:8], flat(cand))
                    link(nc.vector.match_replace(flat(crest), bv[0:m, 0:8], flat(cand), LOW))
                    link(nc.vector.max(bv[0:m, 8:16], flat(crest)))
                    nc.vector.tensor_scalar(nmax[0:m], bv[0:m, 0:1], -1.0, None, ALU.mult).then_inc(best_done, 1)
                    link(nc.vector.max_index(bp[0:m, 8:16], bv[0:m, 8:16], flat(crest)))

                def part3():
                    nc.vector.tensor_scalar(ab[0:m, 0, :], bp[0:m], 4, None, ALU.logical_shift_right)
                    link(nc.vector.tensor_scalar(ab[0:m, 1, :], bp[0:m], 15, None, ALU.bitwise_and))
                    link(nc.vector.tensor_copy(abf[0:m], ab[0:m]))
                    for s in range(2):
                        last = nc.vector.tensor_tensor(hot[0:m, s], abf[0:m, s, :].unsqueeze(2).to_broadcast(grid),
                                                       iota[0:m, :].unsqueeze(1).to_broadcast(grid), ALU.is_equal)
                    link(last)
                    for s in range(2):
                        last = nc.vector.tensor_tensor(hot[0:m, s], hot[0:m, s], tif[0:m, s, :].unsqueeze(1).to_broadcast(grid), ALU.mult)
                    link(last)
                    link(nc.vector.tensor_reduce(pick[0:m], hot[0:m], AX.X, ALU.add))
                    link(nc.vector.scalar_tensor_tensor(pickf[0:m], pick[0:m, 0, :], float(NKEYS), pick[0:m, 1, :], ALU.mult, ALU.add))
                    link(nc.vector.tensor_copy(idx_out, pickf[0:m]))
                    dve.wait_ge(exp_done, turn_no + 1)
                    link(nc.vector.reciprocal(esum[0:m], esum[0:m]))
                    link(nc.vector.tensor_scalar(gates_out, ex[0:m], esum[0:m], None, ALU.mult))
                    assert count[0] == CHOICE_STEPS, count[0]

                return part0, part1, part2, part3

            def choose(*of):
                for part in choice_parts(*of):
                    part()

            def stage_lot(m, src, half):
                nc.vector.tensor_copy(lot[0:m, half, :], src).then_inc(lot_here, 1)

            def diags(m, width, ident, unit, pair, gate):
                dve.wait_ge(gelu_done, unit * (SLOTS // PAIR) + pair + 1)
                for s in range(PAIR * pair, PAIR * pair + PAIR):
                    dve.wait_ge(used, RING + unit * SLOTS + s - DIAGS + 1)
                    nc.vector.tensor_scalar(diag[0:m, s % DIAGS, 0:width], ident, gel[0:m, s:s + 1], gate(s), ALU.mult, ALU.mult).then_inc(diag_done, 1)

            def unit_slots(m, width, ident, hn, unit, gate, next_lots, parts, next_m=P):
                for pair in range(SLOTS // PAIR):
                    for s in range(PAIR * pair, PAIR * pair + PAIR):
                        dve.wait_ge(row_here[s % RING], unit * 16 * (SLOTS // RING) + 16 * (s // RING + 1))
                        u = rows[0:m, s % RING, 0:D]
                        nc.vector.tensor_tensor_reduce(out=u, in0=u, in1=hn, scale=1.0, scalar=0.0, op0=ALU.mult, op1=ALU.add,
                                                       accum_out=hid[0:m, s:s + 1]).then_inc(dot_done, 1)
                    if (pair * PAIR + PAIR) % LOT == 0:
                        half = pair * PAIR // LOT
                        stage_lot(next_m, next_lots(half), half)
                    if pair >= 1:
                        diags(m, width, ident, unit, pair - 1, gate)
                    if pair in PARTS_AFTER:
                        parts[PARTS_AFTER.index(pair)]()
                diags(m, width, ident, unit, SLOTS // PAIR - 1, gate)

            def read_sum(m, bank, out, n):
                dve.wait_ge(acc_closed, n + 1)
                for half in range(2):
                    last = nc.vector.tensor_copy(out[:, half * 512:half * 512 + 512], ps[bank[half]][0:m, :])
                last.then_inc(fin_done, 1)

            def last_norm(m, out, j, n):
                dve.wait_ge(fsq_done, n + 1)
                nc.vector.tensor_scalar(fss[0:m, j:j + 1], fss[0:m, j:j + 1], 1.0 / D, EPS, ALU.mult, ALU.add).then_inc(fmean, 1)
                dve.wait_ge(froot, n + 1)
                nc.vector.reciprocal(fss[0:m, j:j + 1], fss[0:m, j:j + 1]).then_inc(cleared, 1)
                dve.wait_ge(cleared, n + 1)
                nc.vector.scalar_tensor_tensor(out, out, fss[0:m, j:j + 1], wf[0:m, :], ALU.mult, ALU.mult).then_inc(out_ready, 1)

            unit_of = lambda t, i: t[:, bass.ds(i * SLOTS, SLOTS)]
            sc_flat = sc[:, :, :].rearrange("p u n -> p (u n)")
            gate_of = lambda i: lambda s: gates[:, bass.ds(i * SLOTS + s, 1)]
            lots_of = lambda i: lambda half: idx[:, bass.ds(i * SLOTS + half * LOT, LOT)]
            choice_of = lambda i, turn_no, wait=lambda: None: choice_parts(
                P, sc_flat[:, bass.ds(i * 2 * NKEYS, 2 * NKEYS)], unit_of(idx, i), unit_of(gates, i), turn_no, wait)
            head_scored = lambda h: lambda: dve.wait_ge(copied, 5 * h + 5)

            def tile_hn(c):
                return nc.vector.scalar_tensor_tensor(hn_cur[:, :], x1_in[:, :], k.rs2[:, bass.ds(c, 1)], k.w2[:, :], ALU.mult, ALU.mult)

            k.vlink(dve, nc.vector.memset(sc[:, UNITS:UNITS + 2, :], 0.0))
            dve.wait_ge(ins_here, 16 * INS)
            dve.wait_ge(x1_here, 16)
            tile_hn(0).then_inc(hn_cur_done, 1)
            for part in choice_of(0, 0, head_scored(0)):
                part()
            for half in range(2):
                stage_lot(P, lots_of(0)(half), half)
            for part in choice_of(1, 1, head_scored(1)):
                part()
            dve.wait_ge(hn_cur_done, 1)
            with dve.Fori(0, EH - 2) as i:
                unit_slots(P, P, k.ident[:, :], hn_cur[:, :], i, gate_of(i), lots_of(i + 1), choice_of(i + 2, i + 2, head_scored(i + 2)))
            unit_slots(P, P, k.ident[:, :], hn_cur[:, :], EH - 2, gate_of(EH - 2), lots_of(EH - 1),
                       choice_parts(SROWS, ssc[:, :], sidx[:, :], sgates[:, :], EH, lambda: dve.wait_ge(ssc_here, 16 * EH)))
            unit_slots(P, P, k.ident[:, :], hn_cur[:, :], EH - 1, gate_of(EH - 1), lambda half: sidx[:, half * LOT:(half + 1) * LOT],
                       choice_of(EH, EH + 1), next_m=SROWS)
            dve.wait_ge(dot_done, EH * SLOTS)
            dve.wait_ge(hn_rep, 1)
            for half in range(2):
                last = nc.vector.tensor_copy(hn_cur[0:SROWS, half * 512:half * 512 + 512], ps[REP[half]][0:SROWS, :])
            last.then_inc(hn_cur_done, 1)
            dve.wait_ge(hn_cur_done, 2)
            unit_slots(SROWS, NSAMP, ssel[:, :], hn_cur[0:SROWS, :], EH, lambda s: sgates[:, s:s + 1], lots_of(EH), choice_of(EH + 1, EH + 2))
            read_sum(P, ACC, fin[:, :], 0)
            read_sum(NSAMP, SACC, sfin[:, :], 1)
            last_norm(P, fin[:, :], 1, 0)
            last_norm(NSAMP, sfin[:, :], 0, 1)
            with dve.Fori(1, TILES) as c:
                dve.wait_ge(dot_done, (c * EH + 1) * SLOTS)
                dve.wait_ge(x1_here, c * 16 + 16)
                tile_hn(c).then_inc(hn_cur_done, 1)
                dve.wait_ge(hn_cur_done, c + 2)
                dve.sem_inc(turn, 1)
                with dve.Fori(0, EH) as h:
                    i = c * EH + h
                    unit_slots(P, P, k.ident[:, :], hn_cur[:, :], i + 1, gate_of(i), lots_of(i + 1), choice_of(i + 2, i + 3))
                dve.wait_ge(out_done, c * 16 + 16)
                read_sum(P, ACC, fin[:, :], c + 1)
                last_norm(P, fin[:, :], 1, c + 1)

        @block.scalar
        def _(act):
            def softmax(m, turn_no):
                act.wait_ge(best_done, turn_no + 1)
                nc.scalar.activation(ex[0:m], bv[0:m], ACT.Exp, bias=nmax[0:m], accum_out=esum[0:m]).then_inc(exp_done, 1)

            def copy_query(h, s):
                act.wait_ge(computed, 3 * h + s + 1)
                nc.scalar.copy(q[:, s, 0:SEQ], ps[Q[s]][:, :])
                nc.scalar.copy(q[:, s, SEQ:TOK], ps[SQ[s]][:, 0:NSAMP]).then_inc(copied, 1)

            def copy_scores(h):
                act.wait_ge(computed, 3 * h + 3)
                for i, bank in enumerate(SC):
                    nc.scalar.copy(sc[:, 0:UNITS, :].rearrange("p (c h) n -> p c h n", h=EH)[:, 2 * i:2 * i + 2, h, :],
                                   ps[bank][:, :].rearrange("p (c n) -> p c n", c=2)).then_inc(copied, 1)
                if h >= 2:
                    act.wait_ge(ssc_here, 16 * (h - 1))
                nc.scalar.copy(ssc_head[:, h % 2, :], ps[SSC][0:NSAMP, 0:2 * NKEYS]).then_inc(copied, 1)

            def copy_head(h):
                copy_query(h, 0)
                copy_query(h, 1)
                copy_scores(h)

            def unit_gelus(m, unit, middle, head=None):
                for pair in range(SLOTS // PAIR):
                    if head is not None and pair in QUERY_COPIES:
                        copy_query(head, QUERY_COPIES.index(pair))
                    act.wait_ge(dot_done, unit * SLOTS + PAIR * pair + PAIR)
                    s = slice(PAIR * pair, PAIR * pair + PAIR)
                    nc.scalar.activation(gel[0:m, s], hid[0:m, s], ACT.Gelu).then_inc(gelu_done, 1)
                    if pair == PARTS_AFTER[2]:
                        middle()
                if head is not None:
                    copy_scores(head)

            def last_norm(m, out, j, n, first=False):
                act.wait_ge(fin_done, n + 1)
                if not first:
                    act.wait_ge(froot, n)
                nc.scalar.activation(squares[0:m, :], out, ACT.Square, accum_out=fss[0:m, j:j + 1]).then_inc(fsq_done, 1)
                act.wait_ge(fmean, n + 1)
                nc.scalar.activation(fss[0:m, j:j + 1], fss[0:m, j:j + 1], ACT.Sqrt).then_inc(froot, 1)

            copy_head(0)
            softmax(P, 0)
            copy_head(1)
            softmax(P, 1)
            copy_head(2)
            for i in range(EH):
                unit_gelus(P, i, lambda: softmax(SROWS if i == EH - 2 else P, i + 2), i + AHEAD if i + AHEAD < EH else None)
            unit_gelus(SROWS, EH, lambda: softmax(P, EH + 2))
            last_norm(P, fin[:, :], 1, 0, first=True)
            last_norm(NSAMP, sfin[:, :], 0, 1)
            with act.Fori(1, TILES) as c:
                with act.Fori(0, EH) as h:
                    i = c * EH + h
                    unit_gelus(P, i + 1, lambda: softmax(P, i + 3))
                last_norm(P, fin[:, :], 1, c + 1)

        @block.tensor
        def _(pe):
            def open_sum(banks, m, x1):
                return [nc.tensor.matmul(ps[b][0:m, :], k.ident[0:m, 0:m], x1[:, half * 512:half * 512 + 512], start=True, stop=False)
                        for half, b in enumerate(banks)]

            def close_sum(banks, m):
                for b in banks:
                    last = nc.tensor.matmul(ps[b][0:m, :], k.ident[:, 0:m], zeros[:, :], start=False, stop=True)
                last.then_inc(acc_closed, 1)

            def queries(h, s):
                if s == 0:
                    pe.wait_ge(k.qw_here[h % 2], 16 * (h // 2 + 1))
                if h >= 1:
                    pe.wait_ge(copied, 5 * h)
                w = k.qw[:, h % 2, :].rearrange("p (k c) -> p k c", k=KD)
                for bank, cols in ((Q[s], slice(0, SEQ)), (SQ[s], slice(SEQ, TOK))):
                    for kt in range(KD):
                        last = nc.tensor.matmul(ps[bank][:, 0:cols.stop - cols.start], w[:, kt, s * P:(s + 1) * P], k.hnT[:, kt, cols],
                                                start=kt == 0, stop=kt == KD - 1)
                last.then_inc(computed, 1)

            def scores(h):
                pe.wait_ge(copied, 5 * h + 2)
                for c in range(TILES + 1):
                    m, bank, at = (P, SC[c // 2], c % 2 * 2 * NKEYS) if c < TILES else (NSAMP, SSC, 0)
                    for s in range(2):
                        last = nc.tensor.matmul(ps[bank][0:m, at + s * NKEYS:at + (s + 1) * NKEYS], q[:, s, c * P:c * P + m], k.keys[:, 2 * h + s, :],
                                                start=True, stop=True)
                last.then_inc(computed, 1)

            def unit_sums(m, width, banks, unit, head=None):
                for s in range(SLOTS):
                    if head is not None and s in QUERY_SLOTS:
                        queries(head, QUERY_SLOTS.index(s))
                    if head is not None and s == SCORE_SLOT:
                        scores(head)
                    pe.wait_ge(diag_done, unit * SLOTS + s + 1)
                    for half, b in enumerate(banks):
                        last = nc.tensor.matmul(ps[b][0:width, :], diag[0:m, s % DIAGS, 0:width],
                                                rows[0:m, s % RING, D + half * 512:D + half * 512 + 512], start=False, stop=False)
                    last.then_inc(used, 1)

            for h in range(AHEAD):
                if h == 1:
                    pe.wait_ge(x1_here, 16)
                    first, second = open_sum(ACC, P, x1_in)
                    first.then_inc(used, RING)
                    second.then_inc(opened, 1)
                queries(h, 0)
                queries(h, 1)
                scores(h)
            pe.wait_ge(ins_here, 16 * INS)
            for h in range(EH):
                if h == EH - 2:
                    pe.wait_ge(copied, 5 * EH)
                    for half, b in enumerate(REP):
                        last = nc.tensor.matmul(ps[b][0:SROWS, :], ssel_t[:, :], k.hns[:, half * 512:half * 512 + 512], start=True, stop=True)
                    last.then_inc(hn_rep, 1)
                    open_sum(SACC, NSAMP, k.x1s)
                unit_sums(P, P, ACC, h, h + AHEAD if h + AHEAD < EH else None)
            close_sum(ACC, P)
            unit_sums(SROWS, NSAMP, SACC, EH)
            close_sum(SACC, NSAMP)
            with pe.Fori(1, TILES) as c:
                pe.wait_ge(fin_done, c + 1)
                pe.wait_ge(x1_here, c * 16 + 16)
                open_sum(ACC, P, x1_in)[1].then_inc(opened, 1)
                with pe.Fori(0, EH) as h:
                    unit_sums(P, P, ACC, c * EH + h + 1)
                close_sum(ACC, P)


def build(nc, ins, outs):
    with ExitStack() as ctx:
        k = Shared({**ins, **outs})
        k.sem = lambda n: ctx.enter_context(nc.semaphore(n))
        sb = lambda n, s, d=F32, side="left": ctx.enter_context(nc.sbuf_tensor(n, s, d, side=side))
        k.ps = [ctx.enter_context(nc.psum_tensor(f"bank{i}", [P, 512], F32)) for i in range(8)]
        k.vlink, k.alink, k.plink = Link(k.sem("vector_step")), Link(k.sem("scalar_step")), Link(k.sem("pool_step"))
        k.consts_here, k.block_used = k.sem("consts_here"), {}
        k.block_here = [k.sem("block_here0"), k.sem("block_here1")]
        k.ident = sb("ident", [P, P])
        early = ExitStack()
        sb = lambda n, s, d=F32: early.enter_context(nc.sbuf_tensor(n, s, d, side="left"))
        k.tri = sb("tri", [P, P])
        k.tri64 = sb("tri64", [P, P])
        k.ones = sb("ones", [P, P])
        k.identb = sb("identb", [P, P], BF16)
        k.future = sb("future", [P, 4 * P], BF16)
        k.att_mask = sb("att_mask", [P, P], I32)
        k.sel8 = sb("sel8", [NSAMP, NSAMP, P])
        k.diag8 = sb("diag8", [NSAMP, NSAMP])
        k.eye8 = sb("eye8", [P, NSAMP, NSAMP])
        k.const_loads = [(k.ident[:, :], k.dram["c_ident"]), (k.tri[:, :], k.dram["c_tri"]), (k.tri64[:, :], k.dram["c_tri64"]), (k.ones[:, :], k.dram["c_ones"]),
                         (k.identb[:, :], k.dram["c_identb"]), (k.future[:, :], k.dram["c_future"]), (k.att_mask[:, :], k.dram["c_att_mask"]),
                         (k.sel8[:, :, :], k.dram["c_sel8"]), (k.diag8[:, :], k.dram["c_diag8"]), (k.eye8[:, :, :], k.dram["c_eye8"])]
        k.dt = sb("dt", [P, 6, HEADS])
        k.da = sb("da", [P, 6, HEADS])
        k.dte = sb("dte", [P, 5, HEADS])
        k.eac = sb("eac", [P, TILES, HEADS])
        k.cdec = sb("cdec", [P, TILES, HEADS])
        k.nac = sb("nac", [P, TILES, HEADS])
        k.decs = sb("decs", [NSAMP, HEADS])
        k.decb = sb("decb", [P, NSAMP, HEADS])
        base = ExitStack()
        ring = [base.enter_context(nc.sbuf_tensor(f"ring{i}", [P, KD * CT * P], F32, side="left")) for i in range(2)]
        k.ring = ring
        k.xnT = base.enter_context(nc.sbuf_tensor("xnT", [P, KD, COLS], F32, side="left"))
        stage_norm(nc, k)
        top = ExitStack()
        k.y = top.enter_context(nc.sbuf_tensor("y", [P, TILES, GROUPS * GW], F32, side="left"))
        k.ys = top.enter_context(nc.sbuf_tensor("ys", [NSAMP, GROUPS * GW], F32, side="left"))
        stage_ssd(nc, k)
        top2 = ExitStack()
        k.o = top2.enter_context(nc.sbuf_tensor("o", [P, TILES, GH * DV], F32, side="left"))
        k.os = top2.enter_context(nc.sbuf_tensor("os", [NSAMP, GH * DV], F32, side="left"))
        stage_gla(nc, k)
        mid = ExitStack()
        k.yT = mid.enter_context(nc.sbuf_tensor("yT", [P, GROUPS * GW // P, TOK], F32, side="right"))
        k.oT = mid.enter_context(nc.sbuf_tensor("oT", [P, KD, TOK], F32, side="right"))
        stage_gate(nc, k)
        top2.close()
        top.close()
        k.mixT = base.enter_context(nc.sbuf_tensor("mixT", [P, KD, TOK], F32, side="left"))
        stage_merge(nc, k)
        mid.close()
        late = ExitStack()
        sb = lambda n, s, d=F32: late.enter_context(nc.sbuf_tensor(n, s, d, side="right"))
        k.hnT = sb("hnT", [P, KD, TOK])
        k.qw = sb("query_w", [P, 2, KD * 2 * P])
        k.keys = sb("sub_keys", [P, 2 * EH, NKEYS])
        k.w2 = sb("w2", [P, D])
        k.rs2 = sb("rs2", [P, TILES + 1])
        k.x1s = sb("x1s", [NSAMP, D])
        k.hns = sb("hns", [NSAMP, D])
        k.qw_here = [k.sem("qw_here0"), k.sem("qw_here1")]
        k.x1_dram = nc.dram_tensor("x1_kept", [SEQ, D], F32).ap()
        stage_out(nc, k)
        base.close()
        early.close()
        stage_peer(nc, k)
        late.close()



def _weight_tiles(w, width):
    n_k = w.shape[0] // P
    return np.ascontiguousarray(w.reshape(n_k, P, -1, width).transpose(2, 1, 0, 3).reshape(-1, P, n_k * width))


def _every_partition(row):
    return np.ascontiguousarray(np.broadcast_to(row, (P, row.shape[-1])))


def _channels():
    x, b = np.arange(GW), np.arange(P)
    return np.concatenate([np.concatenate([g * GW + x, GROUPS * GW + g * P + b, GROUPS * (GW + P) + g * P + b]) for g in range(GROUPS)])


def _constants():
    i = np.arange(P)
    upto = (i[:, None] <= i[None, :]).astype(np.float32)
    chunk = i[:, None] // GCH == i[None, :] // GCH
    b = np.arange(NSAMP)
    sel8 = np.zeros((NSAMP, NSAMP, P), np.float32)
    sel8[b, b, :] = 1
    ssel = (np.arange(NSAMP * EH)[:, None] % NSAMP == b[None, :]).astype(np.float32)
    low = np.dtype("bfloat16")
    return dict(
        c_ident=np.eye(P, dtype=np.float32), c_tri=upto, c_tri64=(upto * chunk / 16).astype(np.float32), c_ones=np.ones((P, P), np.float32),
        c_identb=np.eye(P).astype(low), c_future=np.ascontiguousarray(np.tile(np.where(upto > 0, 0.0, -1e30).astype(low), (1, 4))),
        c_att_mask=(upto * chunk).astype(np.int32), c_sel8=sel8, c_diag8=np.eye(NSAMP, dtype=np.float32),
        c_eye8=np.ascontiguousarray(np.broadcast_to(np.eye(NSAMP, dtype=np.float32), (P, NSAMP, NSAMP))),
        c_zeros=np.zeros((P, 512), np.float32), c_iota=_every_partition(np.arange(TOPK, dtype=np.float32)), c_ssel=ssel, c_ssel_t=np.ascontiguousarray(ssel.T))


def _inputs(a):
    d_inner, gn = GROUPS * GW, GROUPS * P
    sizes = (d_inner, d_inner + 2 * gn, HEADS, GH * DK, GH * DK, GH * DV, GH * DV, RANK, 2 * D)
    z, xbc, dt, q, key, v, g, glr, merge = np.split(a["w_in"][0], np.cumsum(sizes)[:-1], axis=1)
    ch = _channels()
    conv = np.concatenate([a["conv_w"][0], a["conv_b"]], 0)[:, ch]
    hist = np.zeros((P, GROUPS, CT, CONV, NSAMP), np.float32)
    hist[:, :, :, :HIST] = a["state_conv"][0][:, :, ch].reshape(NSAMP, HIST, GROUPS, CT, P).transpose(4, 2, 3, 1, 0)
    w_gla = [np.concatenate([q[:, h * DK:(h + 1) * DK], key[:, h * DK:(h + 1) * DK], v[:, h * DV:(h + 1) * DV]], 1) for h in range(GH)]
    w = dict(
        ssd=_weight_tiles(xbc[:, ch], CT * P), gla=np.concatenate([_weight_tiles(x, 2 * DK + DV) for x in w_gla]),
        z=_weight_tiles(z, 512), g=_weight_tiles(g, 512), out=_weight_tiles(a["w_out"][0], 512), query=_weight_tiles(a["peer_w_q"][0], 2 * P),
        merge=np.concatenate([_weight_tiles(x, P) for x in (merge[:, :D], merge[:, D:], a["w_ssd_out"][0], a["w_gla_out"][0])], 2))
    x = dict(
        x_all=np.concatenate([a["x_sample"][:, 0], np.zeros((META0 - NSAMP, D), np.float32), a["meta_tokens"], a["x_prompt"][0]]),
        norm1=np.ascontiguousarray(a["norm1_w"][0].reshape(KD, P).T), wdt=_weight_tiles(dt, HEADS)[0].reshape(P, KD, HEADS),
        dt_bias=_every_partition(a["dt_bias"][0]), a_log=_every_partition(a["a_log"][0]), d_skip=_every_partition(a["d_skip"][0]),
        conv_w=np.ascontiguousarray(conv.reshape(CONV + 1, GROUPS, CT, P).transpose(3, 1, 2, 0)), state_conv=hist,
        state_ssd=np.ascontiguousarray(a["state_ssd"][0].reshape(NSAMP, GROUPS, GW, P).transpose(1, 3, 0, 2)),
        wglr=_weight_tiles(glr, RANK)[0].reshape(P, KD, RANK), gate_up=np.concatenate([a["gla_gate_up"][0], a["gla_gate_b"]], 0),
        state_gla=np.ascontiguousarray(a["state_gla"][0].transpose(1, 2, 0, 3)),
        ssd_norm=np.ascontiguousarray(a["ssd_norm_w"][0].reshape(-1, P).T),
        gla_norm=np.ascontiguousarray(np.tile(a["gla_norm_w"][0].reshape(DV // P, P), (GH, 1)).T),
        norm2=_every_partition(a["norm2_w"][0]), norm_f=_every_partition(a["final_norm_w"]),
        keys=np.ascontiguousarray(a["peer_sub_keys"][0].transpose(3, 1, 0, 2).reshape(P, 2 * EH, NKEYS)),
        experts=np.concatenate([a["peer_u"][0], a["peer_v"][0]], 1))
    return {**x, **{"w_" + n: t for n, t in w.items()}, **_constants()}


_OUTS = dict(o_prompt=(SEQ, D), o_sample=(NSAMP, D), o_pssd=(GROUPS, P, GW), o_pconv=(P, GROUPS, CT, HIST), o_pgla=(GH, DK, DV),
             o_sssd=(GROUPS, P, NSAMP, GW), o_sconv=(P, GROUPS, CT, HIST, NSAMP), o_sgla=(GH, DK, NSAMP, DV))


def kernel(**inputs):
    import concourse.bacc as _bacc
    from concourse.bass_utils import run_bass_kernel_spmd as _run

    nc = _bacc.Bacc("TRN2", target_bir_lowering=False, num_devices=1)
    arrays = {f"in_{n}": x for n, x in _inputs({n: np.asarray(x) for n, x in inputs.items()}).items()}
    ins = {n[3:]: nc.dram_tensor(n, x.shape, mybir.dt.from_np(x.dtype), kind="ExternalInput").ap() for n, x in arrays.items()}
    ins["w"] = {n[2:]: ins.pop(n) for n in [n for n in ins if n.startswith("w_")]}
    outs = {n: nc.dram_tensor(n, shape, F32, kind="ExternalOutput").ap() for n, shape in _OUTS.items()}
    build(nc, ins, outs)
    got = _run(nc, [arrays], core_ids=[0]).results[0]
    back = np.argsort(_channels())
    return (
        got["o_prompt"][None], got["o_sample"][:, None],
        got["o_pssd"].transpose(0, 2, 1).reshape(1, 1, HEADS, HEAD, P),
        got["o_pconv"].transpose(3, 1, 2, 0).reshape(HIST, -1)[:, back][None, None],
        got["o_pgla"][None, None],
        got["o_sssd"].transpose(2, 0, 3, 1).reshape(1, NSAMP, HEADS, HEAD, P),
        got["o_sconv"].transpose(4, 3, 1, 2, 0).reshape(NSAMP, HIST, -1)[:, :, back][None],
        got["o_sgla"].transpose(2, 0, 1, 3)[None])
```

```python
import concourse.bass as bass
from concourse import mybir
from concourse.alu_op_type import AluOpType as ALU
from contextlib import ExitStack
import numpy as np

ACT = mybir.ActivationFunctionType
AX = mybir.AxisListType
F32 = mybir.dt.float32
F32R = mybir.dt.float32r
BF16 = mybir.dt.bfloat16
I32 = mybir.dt.int32
U32 = mybir.dt.uint32

P = 128
D = 1024
KD = D // P
SEQ, NMETA, NSAMP = 512, 16, 8
TILES = SEQ // P
META0 = 32
SM = META0 + NMETA
S0 = NMETA + SEQ
COLS = S0 + NSAMP
HALF = COLS // 2
TOK = SEQ + NSAMP
TOK_HALVES = (slice(0, TOK // 2), slice(TOK // 2, TOK))
HALVES = (slice(0, HALF), slice(HALF, COLS))
EPS = 1e-6
GROUPS, HPG, HEAD = 4, 8, 64
HEADS = GROUPS * HPG
GW = HPG * HEAD
CT = GW // P + 2
B_TILE, C_TILE = CT - 2, CT - 1
CONV = 4
HIST = CONV - 1
RAW = HIST + NMETA + SEQ
CONVD = NMETA + SEQ
GH, DK, DV = 4, 128, 256
GCH = 64
RANK = 16
EH, NKEYS, TOPK = 8, 128, 16
ROW = 2 * D


def tile_cols(c):
    return slice(NMETA + c * P, NMETA + (c + 1) * P)


BLOCKS = ([("ssd", g) for g in range(GROUPS)] + [("gla", h) for h in range(GH)]
          + [("z", g) for g in range(GROUPS)] + [("g", i) for i in range(2)]
          + [("merge", j) for j in range(KD)] + [("out", i) for i in range(2)])
FIRST = {kind: next(i for i, x in enumerate(BLOCKS) if x[0] == kind)
         for kind in ("ssd", "gla", "z", "g", "merge", "out")}


SPLIT = 96


def split_rows(dve, nc, link, dst, src, rem, mid):
    link(dve, nc.vector.tensor_copy(dst[0:NSAMP], src))
    link(dve, nc.vector.tensor_tensor(rem, src, dst[0:NSAMP], ALU.subtract))
    link(dve, nc.vector.tensor_copy(mid, rem))
    nc.vector.tensor_copy(dst[32:32 + NSAMP], mid)
    link(dve, nc.vector.tensor_tensor(rem, rem, mid, ALU.subtract))
    return nc.vector.tensor_copy(dst[64:64 + NSAMP], rem)


class Shared:

    def __init__(self, dram):
        self.dram = dram


class Link:

    def __init__(self, sem):
        self.sem, self.count = sem, 0

    def __call__(self, eng, ins):
        self.count += 1
        ins.then_inc(self.sem, 1)
        eng.wait_ge(self.sem, self.count)


def load_block(sp, k, b):
    if b >= len(BLOCKS):
        return
    kind, i = BLOCKS[b]
    if b >= 2:
        sp.wait_ge(*k.block_used[b - 2])
    src = k.dram["w"][kind][i]
    sp.dma_start(k.ring[b % 2][:, 0:src.shape[1]], src).then_inc(k.block_here[b % 2], 16)


def wait_block(pe, k, b):
    pe.wait_ge(k.block_here[b % 2], 16 * (b // 2 + 1))


def stage_norm(nc, k):
    NT = TILES + 1
    with ExitStack() as ctx:
        sb = lambda n, s, d=F32: ctx.enter_context(nc.sbuf_tensor(n, s, d, side="right"))
        sem = lambda n: k.sem("n_" + n)
        x = sb("n_x", [P, NT, D])
        xn = sb("n_xn", [P, NT, D])
        ss = sb("n_ss", [P, NT])
        rs = sb("n_rs", [P, NT])
        w1 = sb("n_w1", [P, KD])
        wdt = sb("n_wdt", [P, KD, HEADS])
        dtb = sb("n_dtb", [P, HEADS])
        ea = sb("n_ea", [P, HEADS])
        u = sb("n_u", [P, 6, HEADS])
        e = sb("n_e", [P, 6, HEADS])
        lu = sb("n_lu", [P, 6, HEADS])
        w = sb("n_w", [P, 6, HEADS])
        ac = sb("n_ac", [P, 5, HEADS])
        al = sb("n_al", [P, 5, HEADS])
        decd = sb("n_decd", [NSAMP, NSAMP, HEADS])
        x_here, sq_done, ms_done, rt_done, xn_done = map(sem, ("x_here", "sq_done", "ms_done", "rt_done", "xn_done"))
        tr_done, ev_done, dt_raw, dt_lin = map(sem, ("tr_done", "ev_done", "dt_raw", "dt_lin"))
        exps_done, da_done, cum_done, cum_copied = map(sem, ("exps_done", "da_done", "cum_done", "cum_copied"))
        decd_done, decb_done, small_here = map(sem, ("decd_done", "decb_done", "small_here"))
        rows = [P] * TILES + [SM]
        ps = k.ps
        TURN = (0, 1, 3, 4)
        block = ctx.enter_context(nc.Block())

        @block.sync
        def _(sp):
            for i in range(NT):
                lo = SM + i * P if i < TILES else 0
                sp.dma_start(x[0:rows[i], i, :], k.dram["x_all"][lo:lo + rows[i], :]).then_inc(x_here, 16)
            for dst, src in ((w1[:, :], k.dram["norm1"]), (wdt[:, :, :], k.dram["wdt"]), (dtb[:, :], k.dram["dt_bias"]), (ea[:, :], k.dram["a_log"])):
                sp.dma_start(dst, src).then_inc(small_here, 16)
            for dst, src in k.const_loads:
                sp.dma_start(dst, src).then_inc(k.consts_here, 16)
            load_block(sp, k, 0)
            load_block(sp, k, 1)

        @block.scalar
        def _(act):
            act.wait_ge(x_here, 16 * NT)
            for i in range(NT):
                last = nc.scalar.activation(xn[0:rows[i], i, :], x[0:rows[i], i, :], ACT.Square,
                                            accum_out=ss[0:rows[i], i:i + 1])
                last.then_inc(sq_done, 1)
            act.wait_ge(ms_done, 1)
            nc.scalar.activation(rs[:, 0:TILES], rs[:, 0:TILES], ACT.Sqrt)
            nc.scalar.activation(rs[0:SM, TILES:NT], rs[0:SM, TILES:NT], ACT.Sqrt).then_inc(rt_done, 1)
            act.wait_ge(small_here, 64)
            nc.scalar.activation(ea[:, :], ea[:, :], ACT.Exp).then_inc(exps_done, 1)
            act.wait_ge(dt_lin, 1)
            k.alink(act, nc.scalar.activation(e[:, :, :], u[:, :, :], ACT.Abs))
            k.alink(act, nc.scalar.activation(e[:, :, :], e[:, :, :], ACT.Exp, scale=-1.0))
            nc.scalar.activation(lu[:, :, :], e[:, :, :], ACT.Ln, bias=1.0).then_inc(exps_done, 1)
            act.wait_ge(cum_copied, 1)
            nc.scalar.activation(k.eac[:, :, :], ac[:, 0:TILES, :], ACT.Exp)
            nc.scalar.activation(k.cdec[:, :, :], al[:, 0:TILES, :], ACT.Exp)
            nc.scalar.activation(k.decs[:, :], k.da[0:NSAMP, 5, :], ACT.Exp)
            nc.scalar.activation(k.dte[:, :, :], w[:, 0:5, :], ACT.Exp).then_inc(exps_done, 1)

        @block.vector
        def _(dve):
            dve.wait_ge(sq_done, NT)
            nc.vector.tensor_scalar(rs[:, 0:TILES], ss[:, 0:TILES], 1.0 / D, EPS, ALU.mult, ALU.add)
            nc.vector.tensor_scalar(rs[0:SM, TILES:NT], ss[0:SM, TILES:NT], 1.0 / D, EPS, ALU.mult, ALU.add).then_inc(ms_done, 1)
            dve.wait_ge(rt_done, 1)
            nc.vector.reciprocal(rs[:, 0:TILES], rs[:, 0:TILES])
            k.vlink(dve, nc.vector.reciprocal(rs[0:SM, TILES:NT], rs[0:SM, TILES:NT]))
            dve.wait_ge(x_here, 16 * NT)

            def normed(i):
                nc.vector.tensor_scalar(xn[0:rows[i], i, :], x[0:rows[i], i, :], rs[0:rows[i], i:i + 1], None, ALU.mult).then_inc(xn_done, 1)

            normed(0)
            normed(1)
            dve.wait_ge(small_here, 64)
            for i in range(NT):
                if i + 2 < NT:
                    normed(i + 2)
                spans = [(tile_cols(i), slice(0, P))] if i < TILES else [(slice(0, NMETA), slice(META0, SM)), (slice(S0, COLS), slice(0, NSAMP))]
                for half in range(2):
                    n = 2 * i + half
                    dve.wait_ge(tr_done, n + 1)
                    for dst, at in spans:
                        m = at.stop - at.start
                        last = nc.vector.tensor_tensor(k.xnT[:, 4 * half:4 * half + 4, dst], ps[TURN[n % 4]][:, :].rearrange("p (a t) -> p a t", a=4)[:, :, at],
                                                       w1[:, 4 * half:4 * half + 4].unsqueeze(2).to_broadcast([P, 4, m]), ALU.mult)
                    if i == TILES:
                        last = nc.vector.tensor_tensor(k.xsm[:, 4 * half:4 * half + 4, :], ps[TURN[n % 4]][:, :].rearrange("p (a t) -> p a t", a=4)[:, :, 0:SM],
                                                       w1[:, 4 * half:4 * half + 4].unsqueeze(2).to_broadcast([P, 4, SM]), ALU.mult)
                    last.then_inc(ev_done, 1)
            k.vlink(dve, nc.vector.memset(u[:, :, :], 0.0))
            dve.wait_ge(dt_raw, 1)
            raw = ps[6][:, 0:6 * HEADS].rearrange("p (a h) -> p a h", a=6)
            nc.vector.tensor_tensor(u[:, 0:TILES, :], raw[:, 0:TILES, :], dtb[:, :].unsqueeze(1).to_broadcast([P, TILES, HEADS]), ALU.add)
            nc.vector.tensor_tensor(u[0:NMETA, 4, :], raw[0:NMETA, 4, :], dtb[0:NMETA, :], ALU.add)
            nc.vector.tensor_tensor(u[0:NSAMP, 5, :], raw[0:NSAMP, 5, :], dtb[0:NSAMP, :], ALU.add).then_inc(dt_lin, 1)
            dve.wait_ge(exps_done, 2)
            TINY = 1e-30
            k.vlink(dve, nc.vector.tensor_scalar(w[:, :, :], e[:, :, :], 1.0, None, ALU.add))
            k.vlink(dve, nc.vector.tensor_scalar(w[:, :, :], w[:, :, :], -1.0, TINY, ALU.add, ALU.add))
            k.vlink(dve, nc.vector.reciprocal(w[:, :, :], w[:, :, :]))
            k.vlink(dve, nc.vector.scalar_tensor_tensor(lu[:, :, :], lu[:, :, :], TINY, w[:, :, :], ALU.add, ALU.mult))
            k.vlink(dve, nc.vector.tensor_tensor(lu[:, :, :], lu[:, :, :], e[:, :, :], ALU.mult))
            k.vlink(dve, nc.vector.scalar_tensor_tensor(k.dt[:, :, :], u[:, :, :], 0.0, lu[:, :, :], ALU.max, ALU.add))
            dve.wait_ge(exps_done, 1)
            nc.vector.scalar_tensor_tensor(k.da[:, :, :], k.dt[:, :, :], -1.0, ea[:, :].unsqueeze(1).to_broadcast([P, 6, HEADS]), ALU.mult, ALU.mult).then_inc(da_done, 1)
            k.vlink(dve, nc.vector.memset(ac[:, :, :], 0.0))
            dve.wait_ge(cum_done, 1)
            cum = ps[3][:, 0:5 * HEADS].rearrange("p (a h) -> p a h", a=5)
            tot = ps[4][:, 0:5 * HEADS].rearrange("p (a h) -> p a h", a=5)
            nc.vector.tensor_copy(ac[:, 0:TILES, :], cum[:, 0:TILES, :])
            nc.vector.tensor_copy(al[:, :, :], tot)
            k.vlink(dve, nc.vector.tensor_copy(ac[0:NMETA, 4, :], cum[0:NMETA, 4, :]))
            nc.vector.tensor_scalar(k.nac[:, :, :], ac[:, 0:TILES, :], -1.0, None, ALU.mult)
            nc.vector.tensor_tensor(w[:, 0:5, :], al[:, :, :], ac[:, :, :], ALU.subtract).then_inc(cum_copied, 1)
            dve.wait_ge(exps_done, 3)
            dve.wait_ge(k.consts_here, 16 * len(k.const_loads))
            nc.vector.tensor_tensor(k.dte[:, :, :], k.dte[:, :, :], k.dt[:, 0:5, :], ALU.mult)
            nc.vector.tensor_tensor(decd[:, :, :], k.decs[:, :].unsqueeze(1).to_broadcast([NSAMP, NSAMP, HEADS]),
                                    k.diag8[:, :].unsqueeze(2).to_broadcast([NSAMP, NSAMP, HEADS]),
                                    ALU.mult).then_inc(decd_done, 1)
            dve.wait_ge(decb_done, 1)
            k.vlink(dve, nc.vector.tensor_copy(k.decb[:, :, :], ps[5][:, 0:NSAMP * HEADS].rearrange("p (b h) -> p b h", b=NSAMP)))

        @block.tensor
        def _(pe):
            pe.wait_ge(k.consts_here, 16 * len(k.const_loads))
            for i in range(NT):
                pe.wait_ge(xn_done, i + 1)
                for half in range(2):
                    n = 2 * i + half
                    if n >= 4:
                        pe.wait_ge(ev_done, n - 3)
                    for a in range(4):
                        kt = 4 * half + a
                        last = nc.tensor.transpose(ps[TURN[n % 4]][:, a * P:a * P + rows[i]], xn[0:rows[i], i, kt * P:(kt + 1) * P],
                                                   k.ident[0:rows[i], 0:rows[i]])
                    last.then_inc(tr_done, 1)
            pe.wait_ge(ev_done, 2 * NT)
            pe.wait_ge(small_here, 64)
            spans = [(tile_cols(c), P) for c in range(TILES)] + [(slice(0, NMETA), NMETA), (slice(S0, COLS), NSAMP)]
            for a, (cols, m) in enumerate(spans):
                for kt in range(KD):
                    last = nc.tensor.matmul(ps[6][0:m, a * HEADS:(a + 1) * HEADS], k.xnT[:, kt, cols], wdt[:, kt, :],
                                            start=kt == 0, stop=kt == KD - 1)
            last.then_inc(dt_raw, 1)
            wait_block(pe, k, FIRST["ssd"])
            w = k.ring[0][:, 0:KD * CT * P].rearrange("p (k c) -> p k c", k=KD)
            for bank, half in ((0, HALVES[0]), (2, HALVES[1])):
                for kt in range(KD):
                    last = nc.tensor.matmul(ps[bank][:, 0:HALF], w[:, kt, 0:P], k.xnT[:, kt, half], start=kt == 0, stop=kt == KD - 1)
            last.then_inc(k.tile_ready, 1)
            pe.wait_ge(da_done, 1)
            daf = k.da[:, :, :].rearrange("p a h -> p (a h)")
            m0 = TILES * HEADS
            nc.tensor.matmul(ps[3][:, 0:m0], k.tri[:, :], daf[:, 0:m0], start=True, stop=True)
            nc.tensor.matmul(ps[3][0:NMETA, m0:m0 + HEADS], k.tri[0:NMETA, 0:NMETA], daf[0:NMETA, m0:m0 + HEADS], start=True, stop=True)
            nc.tensor.matmul(ps[4][:, 0:m0], k.ones[:, :], daf[:, 0:m0], start=True, stop=True)
            nc.tensor.matmul(ps[4][:, m0:m0 + HEADS], k.ones[0:NMETA, :], daf[0:NMETA, m0:m0 + HEADS], start=True, stop=True).then_inc(cum_done, 1)
            pe.wait_ge(decd_done, 1)
            nc.tensor.matmul(ps[5][:, 0:NSAMP * HEADS], k.ones[0:NSAMP, :], decd[:, :, :].rearrange("p b h -> p (b h)"), start=True, stop=True).then_inc(decb_done, 1)


STEPS = 1 + TILES


def ssd_order():
    order = [("tile", 0, j) for j in range(CT)]
    for g in range(GROUPS):
        tiles = [("tile", g + 1, j) for j in range(CT)] if g + 1 < GROUPS else []
        order += [("front", g, 0)] + tiles[0:1]
        for i in range(1, STEPS):
            order += [("off", g, i - 1), ("front", g, i), ("back", g, i - 1), ("late", g, i)]
            order += tiles[i:i + 1] if i < STEPS - 1 else [("sprep", g, 0)] + tiles[i:]
        order += [("off", g, STEPS - 1), ("back", g, STEPS - 1), ("sample", g, 0)]
    return order


SSD_ORDER = ssd_order()


def stage_ssd(nc, k):
    with ExitStack() as ctx:
        sb = lambda n, s, d=F32: ctx.enter_context(nc.sbuf_tensor("s_" + n, s, d, side="right"))
        sem = lambda n: k.sem("s_" + n)
        raw = sb("raw", [P, 3, RAW])
        cv = sb("cv", [P, 3, CONVD])
        xc = sb("xc", [P, 2, CT, CONVD])
        hist = sb("hist", [P, GROUPS, CT, CONV, NSAMP])
        cw = sb("cw", [P, GROUPS, CT, CONV + 1])
        last3 = sb("last3", [P, GROUPS, CT, HIST])
        sconv = sb("sconv", [P, CT, NSAMP])
        sterm = sb("sterm", [P, CT, NSAMP])
        sxc = sb("sxc", [P, 2, CT, NSAMP])
        cmask = sb("cmask", [P, NSAMP, NSAMP])
        xdt = sb("xdt", [P, 2, GW])
        xdec = sb("xdec", [P, 2, GW])
        bcb = sb("bcb", [P, 2, 2, P])
        mix = sb("mix", [P, 2, 2, 4, P])
        yoff = sb("yoff", [P, GW])
        state = sb("state", [P, 2, GW])
        sxdt = sb("sxdt", [NSAMP, GW])
        sxdt3 = sb("sxdt3", [SPLIT, GW], BF16)
        srem = sb("srem", [NSAMP, GW])
        smid = sb("smid", [NSAMP, GW], BF16)
        sst = sb("sst", [P, NSAMP, GW])
        dsk = sb("dsk", [P, HEADS])
        ins_here, tile_evac, conv_first, conv_done, xc_ready = map(sem, ("ins_here", "tile_evac", "conv_first", "conv_done", "xc_ready"))
        tile_ready = k.tile_ready
        xt_ready, bc_ready, xt_used, bc_copied, yoff_done = map(sem, ("xt_ready", "bc_ready", "xt_used", "bc_copied", "yoff_done"))
        seg_ready, exp_done, mix_done, yd_ready, yo_ready = map(sem, ("seg_ready", "exp_done", "mix_done", "yd_ready", "yo_ready"))
        cs_ready, y_done, state_done, xdt_done, xdec_done, zeroed = map(
            sem, ("cs_ready", "y_done", "state_done", "xdt_done", "xdec_done", "zeroed"))
        sconv_done, sxc_ready, sxt_ready, sxdt_done, cmask_done = map(sem, ("sconv_done", "sxc_ready", "sxt_ready", "sxdt_done", "cmask_done"))
        sst_here, sdec_done, sx_ready, sst_done, sy_ready, sy_done = map(sem, ("sst_here", "sdec_done", "sx_ready", "sst_done", "sy_ready", "sy_done"))
        sst_out, pst_out, conv_out, pst_final = map(sem, ("sst_out", "pst_out", "conv_out", "pst_final"))
        k.block_used.update({FIRST["ssd"] + g: (tile_ready, CT * (g + 1)) for g in range(GROUPS)})
        ps = k.ps
        MAIN, REST, XT, BC, SEG, YD, YO = (0, 1), 2, 3, 4, 5, 6, 7
        CS = YO
        block = ctx.enter_context(nc.Block())

        def chunk_cols(i):
            return slice(0, NMETA) if i == 0 else slice(NMETA + (i - 1) * P, NMETA + i * P)

        def chunks_before(s):
            return s // STEPS * TILES + max(0, s % STEPS - 1)

        @block.sync
        def _(sp):
            for dst, src in ((hist[:, :, :, :, :], k.dram["state_conv"]), (cw[:, :, :, :], k.dram["conv_w"]), (dsk[:, :], k.dram["d_skip"])):
                sp.dma_start(dst, src).then_inc(ins_here, 16)
            for g in range(GROUPS):
                if g >= 1:
                    sp.wait_ge(sst_out, 16 * NSAMP // 2 * g)
                    sp.wait_ge(sy_ready, g)
                sp.dma_start(sst[:, :, :], k.dram["state_ssd"][g]).then_inc(sst_here, 16)
                load_block(sp, k, FIRST["ssd"] + g + 2)
                for b in range(0, NSAMP, 2):
                    sp.wait_ge(sst_done, NSAMP * g + b + 2)
                    sp.dma_start(k.dram["o_sssd"][g, :, b:b + 2, :], sst[:, b:b + 2, :]).then_inc(sst_out, 16)
                sp.wait_ge(state_done, STEPS * (g + 1))
                sp.dma_start(k.dram["o_pssd"][g], state[:, g % 2, :]).then_inc(pst_out, 16)
            sp.wait_ge(tile_evac, GROUPS * CT)
            sp.dma_start(k.dram["o_sconv"], hist[:, :, :, 1:CONV, :]).then_inc(conv_out, 16)
            sp.dma_start(k.dram["o_pconv"], last3[:, :, :, :]).then_inc(conv_out, 16)
            sp.wait_ge(conv_out, 32)
            sp.wait_ge(sst_out, 16 * NSAMP // 2 * GROUPS)
            sp.wait_ge(pst_out, 16 * GROUPS)

        @block.tensor
        def _(pe):
            def decays(g, i, half):
                q = 2 * (g * TILES + i - 1) + half
                if q >= 1:
                    pe.wait_ge(exp_done, q)
                nc.tensor.matmul(ps[SEG][:, :], k.identb[:, :], k.future[:, :], start=True, stop=False)
                for h in range(4):
                    hh = g * HPG + half * 4 + h
                    last = nc.tensor.matmul(ps[SEG][:, h * P:(h + 1) * P], k.da[:, i - 1, hh:hh + 1].to_broadcast([P, P]),
                                            k.tri[:, :], start=False, stop=h == 3)
                last.then_inc(seg_ready, 1)

            for kind, g, i in SSD_ORDER:
                if kind == "tile":
                    n, b = g * CT + i, FIRST["ssd"] + g
                    if n == 0:
                        continue
                    if i == 0:
                        wait_block(pe, k, b)
                    if n >= 2:
                        pe.wait_ge(tile_evac, n - 1)
                    w = k.ring[b % 2][:, 0:KD * CT * P].rearrange("p (k c) -> p k c", k=KD)
                    for kt in range(KD):
                        wt = w[:, kt, i * P:(i + 1) * P]
                        nc.tensor.matmul(ps[MAIN[n % 2]][:, 0:HALF], wt, k.xnT[:, kt, HALVES[0]], start=kt == 0, stop=kt == KD - 1)
                    if n >= 1:
                        pe.wait_ge(tile_evac, n)
                    for kt in range(KD):
                        wt = w[:, kt, i * P:(i + 1) * P]
                        last = nc.tensor.matmul(ps[REST][:, 0:HALF], wt, k.xnT[:, kt, HALVES[1]], start=kt == 0, stop=kt == KD - 1)
                    last.then_inc(tile_ready, 1)
                elif kind == "front":
                    s = g * STEPS + i
                    cols, m = chunk_cols(i), (NMETA if i == 0 else P)
                    x = xc[:, g % 2]
                    if i > 0:
                        decays(g, i, 0)
                    if i == 0:
                        pe.wait_ge(xc_ready, CT * (g + 1))
                        if g >= 1:
                            pe.wait_ge(sst_done, NSAMP * g)
                            pe.wait_ge(sy_done, g)
                    if i == 1:
                        pe.wait_ge(xdec_done, s)
                    elif s >= 1:
                        pe.wait_ge(xt_used, chunks_before(s))
                    for a in range(CT - 2):
                        last = nc.tensor.transpose(ps[XT][0:m, a * P:(a + 1) * P], x[:, a, cols], k.ident[:, :])
                    last.then_inc(xt_ready, 1)
                    if s >= 1:
                        pe.wait_ge(bc_copied, s)
                    last = nc.tensor.transpose(ps[BC][0:m, 0:P], x[:, B_TILE, cols], k.ident[:, :])
                    if i > 0:
                        last = nc.tensor.matmul(ps[BC][:, P:2 * P], x[:, B_TILE, cols], x[:, C_TILE, cols], start=True, stop=True)
                    last.then_inc(bc_ready, 1)
                elif kind == "late":
                    decays(g, i, 1)
                elif kind == "off" and i > 0:
                    pe.wait_ge(state_done, g * STEPS + i)
                    nc.tensor.matmul(ps[YO][:, :], xc[:, g % 2, C_TILE, chunk_cols(i)], state[:, g % 2, :], start=True, stop=True).then_inc(yo_ready, 1)
                elif kind == "back":
                    s, d = g * STEPS + i, g * TILES + i - 1
                    m, par = (NMETA if i == 0 else P), s % 2
                    if i == 0 and s >= 1:
                        pe.wait_ge(state_done, s)
                    if i > 0:
                        if d >= 1:
                            pe.wait_ge(y_done, d)
                        pe.wait_ge(xdt_done, d + 1)
                        pe.wait_ge(mix_done, 2 * d + 2)
                        for h in range(HPG):
                            last = nc.tensor.matmul(ps[YD][:, h * HEAD:(h + 1) * HEAD], mix[:, d % 2, h // 4, h % 4, :],
                                                    xdt[:, par, h * HEAD:(h + 1) * HEAD], start=True, stop=True)
                        last.then_inc(yd_ready, 1)
                        pe.wait_ge(yoff_done, d + 1)
                    pe.wait_ge(xdec_done, s + 1)
                    pe.wait_ge(bc_copied, s + 1)
                    nc.tensor.matmul(ps[CS][:, :], bcb[0:m, par, 0, :], xdec[0:m, par, :], start=True, stop=True).then_inc(cs_ready, 1)
                elif kind == "sprep":
                    pe.wait_ge(sxc_ready, g + 1)
                    pe.wait_ge(xt_used, TILES * (g + 1))
                    for a in range(CT - 2):
                        last = nc.tensor.transpose(ps[XT][0:NSAMP, a * P:(a + 1) * P], sxc[:, g % 2, a, :], k.ident[:, :])
                    last.then_inc(sxt_ready, 1)
                elif kind == "sample":
                    pe.wait_ge(sxdt_done, g + 1)
                    pe.wait_ge(cmask_done, g + 1)

                    def spread(b):
                        q = g * NSAMP + b
                        if q >= 2:
                            pe.wait_ge(sst_done, q - 1)
                        nc.tensor.matmul(ps[(XT, CS)[b % 2]][:, :], k.sel3[:, b, :], sxdt3[:, :], start=True, stop=True).then_inc(sx_ready, 1)

                    spread(0)
                    pe.wait_ge(state_done, STEPS * (g + 1))
                    for b in range(NSAMP):
                        if b + 1 < NSAMP:
                            spread(b + 1)
                        if b == 0:
                            pe.wait_ge(y_done, TILES * (g + 1))
                        pe.wait_ge(sst_done, g * NSAMP + b + 1)
                        last = nc.tensor.matmul(ps[YD][0:NSAMP, :], cmask[:, b, :], sst[:, b, :], start=b == 0, stop=b == NSAMP - 1)
                    last.then_inc(sy_ready, 1)

        @block.scalar
        def _(act):
            act.wait_ge(ins_here, 48)
            act.wait_ge(zeroed, 1)

            def silu(n):
                g, j = divmod(n, CT)
                act.wait_ge(conv_done, n + 1)
                if j == 0 and g >= 2:
                    act.wait_ge(cs_ready, STEPS * (g - 1))
                nc.scalar.activation(xc[:, g % 2, j, :], cv[:, n % 3, :], ACT.Silu).then_inc(xc_ready, 1)

            def decays(g, i, half):
                d = g * TILES + i - 1
                act.wait_ge(seg_ready, 2 * d + half + 1)
                if d >= 2:
                    act.wait_ge(yd_ready, d - 1)
                for h in range(4):
                    hh = g * HPG + half * 4 + h
                    last = nc.scalar.activation(mix[:, d % 2, half, h, :], ps[SEG][:, h * P:(h + 1) * P], ACT.Exp,
                                                bias=k.nac[:, i - 1, hh:hh + 1])
                last.then_inc(exp_done, 1)

            for kind, g, i in SSD_ORDER:
                if kind == "tile":
                    n = g * CT + i
                    act.wait_ge(tile_ready, n + 1)
                    if n >= 3:
                        act.wait_ge(conv_done, n - 2)
                    end = S0 - HALF
                    nc.scalar.copy(raw[:, n % 3, HIST:HIST + HALF], ps[MAIN[n % 2]][:, 0:HALF])
                    nc.scalar.copy(raw[:, n % 3, HIST + HALF:RAW], ps[REST][:, 0:end])
                    nc.scalar.copy(hist[:, g, i, CONV - 1, :], ps[REST][:, end:HALF])
                    nc.scalar.copy(last3[:, g, i, :], ps[REST][:, end - HIST:end]).then_inc(tile_evac, 1)
                    act.wait_ge(tile_evac, n + 1)
                    if n >= 3:
                        act.wait_ge(xc_ready, n - 2)
                    nc.scalar.activation(cv[:, n % 3, :], raw[:, n % 3, 0:CONVD], ACT.Identity,
                                         bias=cw[:, g, i, CONV:CONV + 1], scale=cw[:, g, i, 0:1]).then_inc(conv_first, 1)
                    if n % CT >= 1:
                        silu(n - 1)
                    if n % CT == CT - 1:
                        silu(n)
                        act.wait_ge(sconv_done, g + 1)
                        if g >= 2:
                            act.wait_ge(sst_done, NSAMP * (g - 1))
                        nc.scalar.activation(sxc[:, g % 2, :, :], sconv[:, :, :], ACT.Silu).then_inc(sxc_ready, 1)
                elif kind == "front":
                    s = g * STEPS + i
                    m, par = (NMETA if i == 0 else P), s % 2
                    if i > 0:
                        decays(g, i, 0)
                    act.wait_ge(bc_ready, s + 1)
                    if s >= 2:
                        act.wait_ge(cs_ready, s - 1)
                        if chunks_before(s - 1):
                            act.wait_ge(mix_done, 2 * chunks_before(s - 1))
                    w = P if i == 0 else 2 * P
                    nc.scalar.copy(bcb[0:m, par, :, :].rearrange("p a b -> p (a b)")[:, 0:w], ps[BC][0:m, 0:w]).then_inc(bc_copied, 1)
                elif kind == "late":
                    decays(g, i, 1)

        @block.vector
        def _(dve):
            dve.wait_ge(ins_here, 48)
            nc.vector.memset(raw[:, :, 0:HIST], 0.0).then_inc(zeroed, 1)
            k.vlink(dve, nc.vector.memset(sxdt3[:, :], 0.0))
            heads = lambda ap: ap.rearrange("p (h c) -> p h c", c=HEAD)

            def mix_half(s, d, half):
                dve.wait_ge(bc_copied, s + 1)
                dve.wait_ge(exp_done, 2 * d + half + 1)
                nc.vector.tensor_tensor(mix[:, d % 2, half, :, :], mix[:, d % 2, half, :, :],
                                        bcb[:, s % 2, 1, :].unsqueeze(1).to_broadcast([P, 4, P]), ALU.mult).then_inc(mix_done, 1)

            for kind, g, i in SSD_ORDER:
                hs = slice(g * HPG, (g + 1) * HPG)
                gc = slice(g * GW, (g + 1) * GW)
                wide = lambda ap, m=P: ap.unsqueeze(2).to_broadcast([m, HPG, HEAD])
                if kind == "tile":
                    n = g * CT + i
                    dve.wait_ge(conv_first, n + 1)
                    for j in range(1, CONV):
                        ins = nc.vector.scalar_tensor_tensor(cv[:, n % 3, :], raw[:, n % 3, j:j + CONVD], cw[:, g, i, j:j + 1],
                                                             cv[:, n % 3, :], ALU.mult, ALU.add)
                        if j < CONV - 1:
                            k.vlink(dve, ins)
                    ins.then_inc(conv_done, 1)
                elif kind == "front":
                    s, d = g * STEPS + i, g * TILES + i - 1
                    m, par = (NMETA if i == 0 else P), s % 2
                    c = TILES if i == 0 else i - 1
                    dve.wait_ge(xt_ready, s + 1)
                    if s >= 2:
                        dve.wait_ge(cs_ready, s - 1)
                        if chunks_before(s - 1):
                            dve.wait_ge(yd_ready, chunks_before(s - 1))
                    xt = heads(ps[XT][0:m, :])
                    nc.vector.tensor_tensor(heads(xdec[0:m, par, :]), xt, wide(k.dte[0:m, c, hs], m), ALU.mult).then_inc(xdec_done, 1)
                    if i > 0:
                        nc.vector.tensor_tensor(heads(xdt[:, par, :]), xt, wide(k.dt[:, c, hs]), ALU.mult).then_inc(xdt_done, 1)
                        nc.vector.tensor_tensor(heads(k.y[:, c, gc]), xt, wide(dsk[:, hs]), ALU.mult).then_inc(xt_used, 1)
                        mix_half(s, d, 0)
                elif kind == "late":
                    mix_half(g * STEPS + i, g * TILES + i - 1, 1)
                elif kind == "off" and i > 0:
                    d, c = g * TILES + i - 1, i - 1
                    dve.wait_ge(yo_ready, d + 1)
                    nc.vector.tensor_tensor(heads(yoff[:, :]), heads(ps[YO][:, :]), wide(k.eac[:, c, hs]), ALU.mult).then_inc(yoff_done, 1)
                    k.vlink(dve, nc.vector.tensor_tensor(heads(state[:, g % 2, :]), heads(state[:, g % 2, :]), wide(k.cdec[:, c, hs]), ALU.mult))
                    dve.wait_ge(xt_used, d + 1)
                    nc.vector.tensor_tensor(k.y[:, c, gc], k.y[:, c, gc], yoff[:, :], ALU.add)
                elif kind == "back":
                    s, d, c = g * STEPS + i, g * TILES + i - 1, i - 1
                    if i > 0:
                        dve.wait_ge(cs_ready, s + 1)
                        nc.vector.tensor_tensor(state[:, g % 2, :], state[:, g % 2, :], ps[CS][:, :], ALU.add).then_inc(state_done, 1)
                        dve.wait_ge(yd_ready, d + 1)
                        dve.wait_ge(state_done, s + 1)
                        nc.vector.tensor_tensor(k.y[:, c, gc], k.y[:, c, gc], ps[YD][:, :], ALU.add).then_inc(y_done, 1)
                    else:
                        if g >= 2:
                            dve.wait_ge(pst_out, 16 * (g - 1))
                        dve.wait_ge(cs_ready, s + 1)
                        nc.vector.tensor_copy(state[:, g % 2, :], ps[CS][:, :]).then_inc(state_done, 1)
                elif kind == "sprep":
                    dve.wait_ge(sxc_ready, g + 1)
                    if g >= 1:
                        dve.wait_ge(sy_ready, g)
                    nc.vector.tensor_tensor(cmask[:, :, :], k.eye8[:, :, :], sxc[:, g % 2, C_TILE, :].unsqueeze(1).to_broadcast([P, NSAMP, NSAMP]),
                                            ALU.mult).then_inc(cmask_done, 1)
                    dve.wait_ge(sxt_ready, g + 1)
                    xt = heads(ps[XT][0:NSAMP, :])
                    nc.vector.tensor_tensor(heads(sxdt[:, :]), xt, wide(k.dt[0:NSAMP, 5, hs], NSAMP), ALU.mult)
                    k.vlink(dve, nc.vector.tensor_tensor(heads(k.ys[:, gc]), xt, wide(dsk[0:NSAMP, hs], NSAMP), ALU.mult))
                    split_rows(dve, nc, k.vlink, sxdt3, sxdt[:, :], srem[:, :], smid[:, :]).then_inc(sxdt_done, 1)
                elif kind == "sample":
                    for b in range(NSAMP):
                        q = g * NSAMP + b
                        dve.wait_ge(sdec_done, q + 1)
                        dve.wait_ge(sx_ready, q + 1)
                        nc.vector.scalar_tensor_tensor(sst[:, b, :], ps[(XT, CS)[b % 2]][:, :], sxc[:, g % 2, B_TILE, b:b + 1],
                                                       sst[:, b, :], ALU.mult, ALU.add).then_inc(sst_done, 1)
                    dve.wait_ge(sy_ready, g + 1)
                    dve.wait_ge(sxdt_done, g + 1)
                    nc.vector.tensor_tensor(k.ys[:, gc], k.ys[:, gc], ps[YD][0:NSAMP, :], ALU.add).then_inc(sy_done, 1)

        @block.gpsimd
        def _(pool):
            pool.wait_ge(ins_here, 48)
            for kind, g, i in SSD_ORDER:
                if kind == "tile" and i == CT - 1:
                    pool.wait_ge(tile_evac, CT * (g + 1))
                    if g >= 1:
                        pool.wait_ge(sxc_ready, g)
                    tap = lambda j: cw[:, g, :, j:j + 1].to_broadcast([P, CT, NSAMP])
                    k.plink(pool, nc.gpsimd.tensor_tensor(sconv[:, :, :], hist[:, g, :, 0, :], tap(0), ALU.mult))
                    for j in range(1, CONV):
                        k.plink(pool, nc.gpsimd.tensor_tensor(sterm[:, :, :], hist[:, g, :, j, :], tap(j), ALU.mult))
                        k.plink(pool, nc.gpsimd.tensor_tensor(sconv[:, :, :], sconv[:, :, :], sterm[:, :, :], ALU.add))
                    nc.gpsimd.tensor_tensor(sconv[:, :, :], sconv[:, :, :], tap(CONV), ALU.add).then_inc(sconv_done, 1)
                elif kind == "front" and i == 1:
                    pool.wait_ge(sst_here, 16 * (g + 1))
                    for b in range(NSAMP):
                        v = sst[:, b, :].rearrange("p (h c) -> p h c", c=HEAD)
                        nc.gpsimd.tensor_tensor(v, v, k.decb[:, b, g * HPG:(g + 1) * HPG].unsqueeze(2).to_broadcast([P, HPG, HEAD]),
                                                ALU.mult).then_inc(sdec_done, 1)


def gla_order():
    proj = lambda h: [("q", h, 0), ("k", h, 0)] + [("v", h, c) for c in range(TILES)] + [("vsmall", h, 0)]
    order = proj(0)
    for h in range(GH):
        steps = [("prep", h, 0), ("fold", h, 0)] + [("chunk", h, c) for c in range(TILES)] + [("sample", h, 0)]
        nxt = proj(h + 1) if h + 1 < GH else [None] * len(steps)
        for a, b in zip(steps, nxt):
            order += [a] + ([b] if b else [])
    return order


def stage_gla(nc, k):
    order = gla_order()
    NCH = SEQ // GCH
    NP = 2 + TILES
    QSCALE = DK ** -0.5
    with ExitStack() as ctx:
        sb = lambda n, s, d=F32: ctx.enter_context(nc.sbuf_tensor("g_" + n, s, d, side="right"))
        sem = lambda n: k.sem("g_" + n)
        glrT = sb("glrT", [RANK + 1, COLS])
        gk = sb("gk", [P, TILES, GH * DK])
        gkm = sb("gkm", [NMETA, GH * DK])
        gks = sb("gks", [P, GH, NSAMP])
        qT = sb("qT", [P, 2, SEQ])
        qs = sb("qs", [P, 2, NSAMP])
        kT = sb("kT", [P, 2, NMETA + SEQ])
        ks = sb("ks", [P, 2, NSAMP])
        vt = sb("vt", [P, 2, TILES, DV])
        vm = sb("vm", [NMETA, 2, DV])
        vs = sb("vs", [NSAMP, 2, DV])
        vs3 = sb("vs3", [SPLIT, 2, DV], BF16)
        vrem = sb("vrem", [NSAMP, DV])
        vmid = sb("vmid", [NSAMP, DV], BF16)
        bend = sb("bend", [P, NCH + 1])
        cdg = sb("cdg", [P, 2, NCH])
        ep = sb("ep", [P, SEQ])
        qa = sb("qa", [P, 2, TILES, 4, GCH])
        ke = sb("ke", [P, SEQ])
        kd = sb("kd", [P, NMETA + SEQ])
        kt_ = sb("kt", [P, TILES, DK])
        ktm = sb("ktm", [NMETA, DK])
        att = sb("att", [P, TILES, P])
        st = sb("st", [P, 2, 2, DV])
        gs = sb("gs", [P, NSAMP, DV])
        qmask = sb("qmask", [P, NSAMP, NSAMP])
        ones_set, glr_ready, glr_copied, gk_ready, gk_ln, gk_done, gs_exp = map(
            sem, ("ones_set", "glr_ready", "glr_copied", "gk_ready", "gk_ln", "gk_done", "gs_exp"))
        proj_ready, proj_evac, vs_ready, vs_evac, vs3_done = map(sem, ("proj_ready", "proj_evac", "vs_ready", "vs_evac", "vs3_done"))
        cum_ready, bend_done, exp_done, qa_done, ke_done, kd_done = map(sem, ("cum_ready", "bend_done", "exp_done", "qa_done", "ke_done", "kd_done"))
        kt_ready, kt_copied, att_ready, att_done = map(sem, ("kt_ready", "kt_copied", "att_ready", "att_done"))
        cs_ready, st_done, o_ready, o_copied, st_out = map(sem, ("cs_ready", "st_done", "o_ready", "o_copied", "st_out"))
        gs_here, sdec_done, sv_ready, gs_done, os_ready, os_done, gs_out, qm_done = map(
            sem, ("gs_here", "sdec_done", "sv_ready", "gs_done", "os_ready", "os_done", "gs_out", "qm_done"))
        k.block_used.update({FIRST["gla"] + h: (vs_ready, h + 1) for h in range(GH)})
        ps = k.ps
        SMALL, CUM, ATT, O, CS, MISC = 2, 3, 4, 5, 6, 7
        block = ctx.enter_context(nc.Block())

        @block.sync
        def _(sp):
            for h in range(GH):
                if h >= 1:
                    sp.wait_ge(gs_out, 32 * h)
                    sp.wait_ge(os_ready, h)
                sp.dma_start(gs[:, :, :], k.dram["state_gla"][h]).then_inc(gs_here, 16)
                load_block(sp, k, FIRST["gla"] + h + 2)
                sp.wait_ge(st_done, (NCH + 1) * (h + 1))
                sp.dma_start(k.dram["o_pgla"][h], st[:, h % 2, 0, :]).then_inc(st_out, 16)
                for b in range(0, NSAMP, 4):
                    sp.wait_ge(gs_done, NSAMP * h + b + 4)
                    sp.dma_start(k.dram["o_sgla"][h, :, b:b + 4, :], gs[:, b:b + 4, :]).then_inc(gs_out, 16)
            sp.wait_ge(st_out, 16 * GH)
            sp.wait_ge(gs_out, 32 * GH)

        @block.tensor
        def _(pe):
            for kt in range(KD):
                nc.tensor.matmul(ps[0][0:RANK, 0:HALF], k.wglr[:, kt, :], k.xnT[:, kt, HALVES[0]], start=kt == 0, stop=kt == KD - 1)
            for kt in range(KD):
                last = nc.tensor.matmul(ps[SMALL][0:RANK, 0:HALF], k.wglr[:, kt, :], k.xnT[:, kt, HALVES[1]], start=kt == 0, stop=kt == KD - 1)
            last.then_inc(glr_ready, 1)
            pe.wait_ge(glr_copied, 1)
            for c in range(TILES):
                nc.tensor.matmul(ps[CUM + c][:, :], glrT[:, tile_cols(c)], k.up[:, :], start=True, stop=True)
            nc.tensor.matmul(ps[MISC][0:NMETA, :], glrT[:, 0:NMETA], k.up[:, :], start=True, stop=True)
            for h in range(GH):
                last = nc.tensor.matmul(ps[1][:, h * NSAMP:(h + 1) * NSAMP], k.up[:, h * DK:(h + 1) * DK], glrT[:, S0:COLS], start=True, stop=True)
            last.then_inc(gk_ready, 1)
            for kind, h, c in order:
                par, b = h % 2, FIRST["gla"] + h
                w = k.ring[b % 2][:, 0:KD * (2 * DK + DV)].rearrange("p (k c) -> p k c", k=KD)
                if kind in ("q", "k"):
                    n = h * NP + (kind == "k")
                    if kind == "q":
                        wait_block(pe, k, b)
                    if n == 1:
                        pe.wait_ge(gk_done, 1)
                    if n >= 2:
                        pe.wait_ge(proj_evac, n - 1)
                    off = DK * (kind == "k")
                    for kt in range(KD):
                        nc.tensor.matmul(ps[n % 2][:, 0:HALF], w[:, kt, off:off + DK], k.xnT[:, kt, HALVES[0]], start=kt == 0, stop=kt == KD - 1)
                    if kind == "k":
                        pe.wait_ge(proj_evac, n)
                    elif h >= 1:
                        pe.wait_ge(vs_evac, h)
                    for kt in range(KD):
                        last = nc.tensor.matmul(ps[SMALL][:, 0:HALF], w[:, kt, off:off + DK], k.xnT[:, kt, HALVES[1]], start=kt == 0, stop=kt == KD - 1)
                    last.then_inc(proj_ready, 1)
                elif kind == "v":
                    n = h * NP + 2 + c
                    pe.wait_ge(proj_evac, n - 1)
                    for kt in range(KD):
                        last = nc.tensor.matmul(ps[n % 2][:, 0:DV], k.xnT[:, kt, tile_cols(c)], w[:, kt, 2 * DK:2 * DK + DV],
                                                start=kt == 0, stop=kt == KD - 1)
                    last.then_inc(proj_ready, 1)
                elif kind == "vsmall":
                    pe.wait_ge(proj_evac, h * NP + 2)
                    for kt in range(KD):
                        last = nc.tensor.matmul(ps[SMALL][0:SM, 0:DV], k.xsm[:, kt, :], w[:, kt, 2 * DK:2 * DK + DV], start=kt == 0, stop=kt == KD - 1)
                    last.then_inc(vs_ready, 1)
                elif kind == "prep":
                    if h >= 1:
                        pe.wait_ge(gs_done, NSAMP * h)
                        pe.wait_ge(os_done, h)
                    for c_ in range(TILES):
                        nc.tensor.matmul(ps[CUM][:, c_ * P:(c_ + 1) * P], gk[:, c_, h * DK:(h + 1) * DK], k.tri64[:, :], start=True, stop=True)
                    nc.tensor.matmul(ps[MISC][:, 0:NMETA], gkm[:, h * DK:(h + 1) * DK], k.tri64[0:NMETA, 0:NMETA], start=True, stop=True).then_inc(cum_ready, 1)
                elif kind == "fold":
                    pe.wait_ge(kd_done, h + 1)
                    pe.wait_ge(exp_done, h + 1)
                    for c_ in range(TILES):
                        nc.tensor.transpose(ps[CUM][:, c_ * P:(c_ + 1) * P], kd[:, NMETA + c_ * P:NMETA + (c_ + 1) * P], k.ident[:, :])
                    nc.tensor.transpose(ps[MISC][0:NMETA, 0:DK], kd[:, 0:NMETA], k.ident[:, :]).then_inc(kt_ready, 1)
                    pe.wait_ge(ke_done, h + 1)
                    pe.wait_ge(qa_done, h + 1)
                    for c_ in range(TILES):
                        last = nc.tensor.matmul(ps[ATT][:, c_ * P:(c_ + 1) * P], ke[:, c_ * P:(c_ + 1) * P], qa[:, par, c_, 0:4:3, :], start=True, stop=True)
                    last.then_inc(att_ready, 1)
                    pe.wait_ge(kt_copied, h + 1)
                    pe.wait_ge(vs_evac, h + 1)
                    if h >= 1:
                        pe.wait_ge(st_done, (NCH + 1) * h)
                    nc.tensor.matmul(ps[CS][:, 0:DV], ktm[:, :], vm[:, par, :], start=True, stop=True).then_inc(cs_ready, 1)
                elif kind == "chunk":
                    t = h * TILES + c
                    if c == 0:
                        pe.wait_ge(att_done, h + 1)
                    if t >= 1:
                        pe.wait_ge(o_copied, t)
                    nc.tensor.matmul(ps[O][:, 0:DV], att[:, c, :], vt[:, par, c, :], start=True, stop=False)
                    for half in range(2):
                        j = 2 * c + half
                        pe.wait_ge(st_done, (NCH + 1) * h + j + 1)
                        rows = slice(half * GCH, (half + 1) * GCH)
                        last = nc.tensor.matmul(ps[O][:, 0:DV], qa[:, par, c, 2 * half:2 * half + 2, :], st[:, par, j % 2, :], start=False, stop=half == 1)
                        if half == 1:
                            last.then_inc(o_ready, 1)
                        nc.tensor.matmul(ps[CS][:, 0:DV], kt_[rows, c, :], vt[rows, par, c, :], start=True, stop=True).then_inc(cs_ready, 1)
                else:
                    pe.wait_ge(qm_done, h + 1)
                    pe.wait_ge(vs3_done, h + 1)
                    pe.wait_ge(kt_copied, h + 1)
                    pe.wait_ge(att_done, h + 1)

                    def spread(b_):
                        q = h * NSAMP + b_
                        if q >= 2:
                            pe.wait_ge(gs_done, q - 1)
                        nc.tensor.matmul(ps[(CUM, ATT)[b_ % 2]][:, 0:DV], k.sel3[:, b_, :], vs3[:, par, :], start=True, stop=True).then_inc(sv_ready, 1)

                    spread(0)
                    for b_ in range(NSAMP):
                        if b_ + 1 < NSAMP:
                            spread(b_ + 1)
                        pe.wait_ge(gs_done, h * NSAMP + b_ + 1)
                        last = nc.tensor.matmul(ps[MISC][0:NSAMP, 0:DV], qmask[:, b_, :], gs[:, b_, :], start=b_ == 0, stop=b_ == NSAMP - 1)
                    last.then_inc(os_ready, 1)

        @block.scalar
        def _(act):
            act.wait_ge(ones_set, 1)
            act.wait_ge(glr_ready, 1)
            nc.scalar.copy(glrT[0:RANK, HALVES[0]], ps[0][0:RANK, 0:HALF])
            nc.scalar.copy(glrT[0:RANK, HALVES[1]], ps[SMALL][0:RANK, 0:HALF]).then_inc(glr_copied, 1)
            act.wait_ge(gk_ready, 1)
            parts = [(gk[:, c, :], ps[CUM + c][:, :]) for c in range(TILES)]
            parts += [(gkm[:, :], ps[MISC][0:NMETA, :]), (gks[:, :, :].rearrange("p h b -> p (h b)"), ps[1][:, 0:GH * NSAMP])]
            for dst, src in parts:
                last = nc.scalar.activation(dst, src, ACT.Abs)
            k.alink(act, last)
            for dst, src in parts:
                last = nc.scalar.activation(dst, dst, ACT.Exp, scale=-1.0)
            k.alink(act, last)
            for dst, src in parts:
                last = nc.scalar.activation(dst, dst, ACT.Ln, bias=1.0)
            last.then_inc(gk_ln, 1)
            act.wait_ge(gk_done, 1)
            nc.scalar.activation(gks[:, :, :], gks[:, :, :], ACT.Exp, scale=1.0 / 16.0).then_inc(gs_exp, 1)
            for kind, h, c in order:
                par = h % 2
                if kind in ("q", "k"):
                    n = h * NP + (kind == "k")
                    act.wait_ge(proj_ready, n + 1)
                    if kind == "q" and h >= 2:
                        act.wait_ge(os_done, h - 1)
                    if kind == "q":
                        nc.scalar.mul(qT[:, par, 0:HALF - NMETA], ps[n % 2][:, NMETA:HALF], QSCALE)
                        nc.scalar.mul(qT[:, par, HALF - NMETA:SEQ], ps[SMALL][:, 0:S0 - HALF], QSCALE)
                        nc.scalar.mul(qs[:, par, :], ps[SMALL][:, S0 - HALF:HALF], QSCALE).then_inc(proj_evac, 1)
                    else:
                        nc.scalar.copy(kT[:, par, 0:HALF], ps[n % 2][:, 0:HALF])
                        nc.scalar.copy(kT[:, par, HALF:S0], ps[SMALL][:, 0:S0 - HALF])
                        nc.scalar.copy(ks[:, par, :], ps[SMALL][:, S0 - HALF:HALF]).then_inc(proj_evac, 1)
                elif kind == "v":
                    n = h * NP + 2 + c
                    act.wait_ge(proj_ready, n + 1)
                    nc.scalar.copy(vt[:, par, c, :], ps[n % 2][:, 0:DV]).then_inc(proj_evac, 1)
                elif kind == "vsmall":
                    act.wait_ge(vs_ready, h + 1)
                    nc.scalar.copy(vm[:, par, :], ps[SMALL][META0:SM, 0:DV])
                    nc.scalar.copy(vs[:, par, :], ps[SMALL][0:NSAMP, 0:DV]).then_inc(vs_evac, 1)
                elif kind == "prep":
                    act.wait_ge(bend_done, h + 1)
                    if h >= 1:
                        act.wait_ge(qa_done, h)
                        act.wait_ge(att_ready, h)
                        act.wait_ge(kt_ready, h)
                    nc.scalar.activation(ep[:, :], ps[CUM][:, :], ACT.Exp)
                    nc.scalar.activation(ke[:, :], ps[CUM][:, :], ACT.Exp, scale=-1.0)
                    for j in range(NCH):
                        nc.scalar.activation(kd[:, NMETA + j * GCH:NMETA + (j + 1) * GCH], ps[CUM][:, j * GCH:(j + 1) * GCH], ACT.Exp,
                                             scale=-1.0, bias=bend[:, j:j + 1])
                    nc.scalar.activation(kd[:, 0:NMETA], ps[MISC][:, 0:NMETA], ACT.Exp, scale=-1.0, bias=bend[:, NCH:NCH + 1])
                    nc.scalar.activation(cdg[:, par, :], bend[:, 0:NCH], ACT.Exp).then_inc(exp_done, 1)
                elif kind == "fold":
                    act.wait_ge(kt_ready, h + 1)
                    if h >= 1:
                        act.wait_ge(cs_ready, (NCH + 1) * h)
                    nc.scalar.copy(kt_[:, :, :].rearrange("p c d -> p (c d)"), ps[CUM][:, :])
                    nc.scalar.copy(ktm[:, :], ps[MISC][0:NMETA, 0:DK]).then_inc(kt_copied, 1)
                elif kind == "chunk":
                    t = h * TILES + c
                    act.wait_ge(o_ready, t + 1)
                    nc.scalar.copy(k.o[:, c, h * DV:(h + 1) * DV], ps[O][:, 0:DV]).then_inc(o_copied, 1)

        @block.vector
        def _(dve):
            nc.vector.memset(glrT[:, :], 1.0).then_inc(ones_set, 1)
            nc.vector.memset(att[:, :, :], 0.0)
            nc.vector.memset(vs3[:, :, :], 0.0)
            k.vlink(dve, nc.vector.memset(qa[:, :, :, :, :], 0.0))
            dve.wait_ge(gk_ln, 1)
            parts = [(gk[:, c, :], ps[CUM + c][:, :]) for c in range(TILES)]
            parts += [(gkm[:, :], ps[MISC][0:NMETA, :]), (gks[:, :, :].rearrange("p h b -> p (h b)"), ps[1][:, 0:GH * NSAMP])]
            for dst, src in parts:
                last = nc.vector.scalar_tensor_tensor(dst, src, 0.0, dst, ALU.min, ALU.subtract)
            last.then_inc(gk_done, 1)
            for kind, h, c in order:
                par = h % 2
                if kind == "prep":
                    dve.wait_ge(cum_ready, h + 1)
                    if h >= 1:
                        dve.wait_ge(exp_done, h)
                    nc.vector.tensor_copy(bend[:, 0:NCH], ps[CUM][:, GCH - 1:SEQ:GCH])
                    nc.vector.tensor_copy(bend[:, NCH:NCH + 1], ps[MISC][:, NMETA - 1:NMETA]).then_inc(bend_done, 1)
                    dve.wait_ge(exp_done, h + 1)
                    dve.wait_ge(proj_evac, h * NP + 2)
                    nc.vector.tensor_tensor(ke[:, :], kT[:, par, NMETA:NMETA + SEQ], ke[:, :], ALU.mult).then_inc(ke_done, 1)
                    dve.wait_ge(vs_evac, h + 1)
                    split_rows(dve, nc, k.vlink, vs3[:, par, :], vs[:, par, :], vrem[:, :], vmid[:, :]).then_inc(vs3_done, 1)
                elif kind == "fold":
                    dve.wait_ge(att_ready, h + 1)
                    if h >= 1:
                        dve.wait_ge(o_ready, TILES * h)
                    nc.vector.copy_predicated(att[:, :, :], k.att_mask[:, :].unsqueeze(1).to_broadcast([P, TILES, P]),
                                              ps[ATT][:, :].rearrange("p (c t) -> p c t", c=TILES)).then_inc(att_done, 1)
                    dve.wait_ge(cs_ready, (NCH + 1) * h + 1)
                    if h >= 2:
                        dve.wait_ge(st_out, 16 * (h - 1))
                    nc.vector.tensor_copy(st[:, par, 0, :], ps[CS][:, 0:DV]).then_inc(st_done, 1)
                elif kind == "chunk":
                    for half in range(2):
                        j = 2 * c + half
                        dve.wait_ge(cs_ready, (NCH + 1) * h + j + 2)
                        dve.wait_ge(st_done, (NCH + 1) * h + j + 1)
                        nc.vector.scalar_tensor_tensor(st[:, par, (j + 1) % 2, :], st[:, par, j % 2, :], cdg[:, par, j:j + 1],
                                                       ps[CS][:, 0:DV], ALU.mult, ALU.add).then_inc(st_done, 1)
                elif kind == "sample":
                    dve.wait_ge(proj_evac, h * NP + 2)
                    if h >= 1:
                        dve.wait_ge(os_ready, h)
                    nc.vector.tensor_tensor(qmask[:, :, :], k.eye8[:, :, :], qs[:, par, :].unsqueeze(1).to_broadcast([P, NSAMP, NSAMP]),
                                            ALU.mult).then_inc(qm_done, 1)
                    for b in range(NSAMP):
                        q = h * NSAMP + b
                        dve.wait_ge(sdec_done, q + 1)
                        dve.wait_ge(sv_ready, q + 1)
                        nc.vector.scalar_tensor_tensor(gs[:, b, :], ps[(CUM, ATT)[b % 2]][:, 0:DV], ks[:, par, b:b + 1],
                                                       gs[:, b, :], ALU.mult, ALU.add).then_inc(gs_done, 1)
                    dve.wait_ge(os_ready, h + 1)
                    nc.vector.tensor_copy(k.os[:, h * DV:(h + 1) * DV], ps[MISC][0:NSAMP, 0:DV]).then_inc(os_done, 1)

        @block.gpsimd
        def _(pool):
            pool.wait_ge(gs_exp, 1)
            for kind, h, c in order:
                par = h % 2
                if kind == "prep":
                    pool.wait_ge(exp_done, h + 1)
                    pool.wait_ge(proj_evac, h * NP + 2)
                    if h >= 2:
                        pool.wait_ge(os_done, h - 1)
                    nc.gpsimd.tensor_tensor(qa[:, par, :, 0:4:3, :], qT[:, par, :].rearrange("p (c a t) -> p c a t", c=TILES, a=2),
                                            ep[:, :].rearrange("p (c a t) -> p c a t", c=TILES, a=2), ALU.mult).then_inc(qa_done, 1)
                    nc.gpsimd.tensor_tensor(kd[:, :], kT[:, par, :], kd[:, :], ALU.mult).then_inc(kd_done, 1)
                elif kind == "fold":
                    pool.wait_ge(gs_here, 16 * (h + 1))
                    for b in range(NSAMP):
                        nc.gpsimd.tensor_scalar(gs[:, b, :], gs[:, b, :], gks[:, h, b:b + 1], None, ALU.mult).then_inc(sdec_done, 1)


def stage_gate(nc, k):
    TOKENS = TILES + 1
    z_items = [("z", g, c) for g in range(GROUPS) for c in range(TOKENS)]
    g_items = [("g", i, c) for i in range(2) for c in range(TOKENS)]
    y_turns = [(c, g) for c in range(TOKENS) for g in range(GROUPS)]
    o_turns = [(c, i) for c in range(TOKENS) for i in range(2)]
    NZ, NG = len(z_items), len(g_items)
    rows = [P] * TILES + [NSAMP]
    cols = lambda c: tile_cols(c) if c < TILES else slice(S0, COLS)
    out_cols = lambda c: slice(c * P, c * P + rows[c])
    BANKS, BUFS = 4, 3
    with ExitStack() as ctx:
        sb = lambda n, s, d=F32: ctx.enter_context(nc.sbuf_tensor("t_" + n, s, d, side="right"))
        sem = lambda n: k.sem("t_" + n)
        gate = sb("gate", [P, BUFS, 512])
        ssy = sb("ssy", [P, TOKENS, GROUPS])
        sso = sb("sso", [P, TOKENS, GH])
        wy = sb("wy", [P, GROUPS * 4])
        wo = sb("wo", [P, KD])
        ins_here, item_ready, item_gated, mul_done, sq_done, zero_done = map(sem, ("ins_here", "item_ready", "item_gated", "mul_done", "sq_done", "zero_done"))
        osq_done, mean_done, root_done, ynorm_done, turn_ready, turn_done = map(
            sem, ("osq_done", "mean_done", "root_done", "ynorm_done", "turn_ready", "turn_done"))
        k.block_used.update({FIRST["z"] + g: (item_ready, TOKENS * (g + 1)) for g in range(GROUPS)})
        k.block_used.update({FIRST["g"] + i: (item_ready, NZ + TOKENS * (i + 1)) for i in range(2)})
        ps = k.ps
        y_of = lambda c, g: (k.y[:, c, g * GW:(g + 1) * GW] if c < TILES else k.ys[:, g * GW:(g + 1) * GW])
        o_of = lambda c, h: (k.o[:, c, h * DV:(h + 1) * DV] if c < TILES else k.os[:, h * DV:(h + 1) * DV])
        turns = [("y", c, g) for c, g in y_turns] + [("o", c, i) for c, i in o_turns]
        block = ctx.enter_context(nc.Block())

        @block.sync
        def _(sp):
            for dst, src in ((wy[:, :], k.dram["ssd_norm"]), (wo[:, :], k.dram["gla_norm"])):
                sp.dma_start(dst, src).then_inc(ins_here, 16)
            for b in range(FIRST["z"], FIRST["merge"]):
                load_block(sp, k, b + 2)

        @block.tensor
        def _(pe):
            def project(n, kind, i, c):
                b = FIRST[kind] + i
                if c == 0:
                    wait_block(pe, k, b)
                if n >= BANKS:
                    pe.wait_ge(item_gated, n - BANKS + 1)
                w = k.ring[b % 2][:, 0:KD * 512].rearrange("p (k c) -> p k c", k=KD)
                for kt in range(KD):
                    last = nc.tensor.matmul(ps[n % BANKS][0:rows[c], :], k.xnT[:, kt, cols(c)], w[:, kt, :], start=kt == 0, stop=kt == KD - 1)
                last.then_inc(item_ready, 1)

            def turn(m):
                kind, c, i = turns[m]
                if kind == "y":
                    pe.wait_ge(ynorm_done, m + 1)
                elif i == 0 and c == 0:
                    pe.wait_ge(mul_done, NZ + NG)
                if m >= 2:
                    pe.wait_ge(turn_done, m - 1)
                for a in range(4):
                    src = y_of(c, i)[:, a * P:(a + 1) * P] if kind == "y" else o_of(c, 2 * i + a // 2)[:, (a % 2) * P:(a % 2 + 1) * P]
                    last = nc.tensor.transpose(ps[BANKS + m % 2][:, a * P:a * P + rows[c]], src, k.ident[0:rows[c], 0:rows[c]])
                last.then_inc(turn_ready, 1)

            for n, item in enumerate(z_items):
                project(n, *item)
            for j, item in enumerate(g_items):
                project(NZ + j, *item)
                turn(2 * j)
                turn(2 * j + 1)
            for m in range(2 * NG, len(turns)):
                turn(m)

        @block.scalar
        def _(act):
            act.wait_ge(zero_done, 1)

            def square_o(n):
                c, h = divmod(n, GH)
                nc.scalar.activation(k.yT[0:rows[c], :, :].rearrange("p a b -> p (a b)")[:, n * DV:(n + 1) * DV], o_of(c, h),
                                     ACT.Square, accum_out=sso[0:rows[c], c, h:h + 1]).then_inc(osq_done, 1)

            def square(n):
                _, g, c = z_items[n]
                act.wait_ge(mul_done, n + 1)
                nc.scalar.activation(gate[0:rows[c], n % BUFS, :], y_of(c, g), ACT.Square, accum_out=ssy[0:rows[c], c, g:g + 1]).then_inc(sq_done, 1)

            for n, (kind, g, c) in enumerate(z_items + g_items):
                act.wait_ge(item_ready, n + 1)
                if n >= BUFS:
                    act.wait_ge(mul_done, n - BUFS + 1)
                    act.wait_ge(sq_done, min(n - BUFS + 1, NZ))
                nc.scalar.activation(gate[0:rows[c], n % BUFS, :], ps[n % BANKS][0:rows[c], :], ACT.Silu).then_inc(item_gated, 1)
                if n < TOKENS * GH:
                    square_o(n)
                if 1 <= n < NZ:
                    square(n - 1)
                if n == NZ - 1:
                    square(n)
                    act.wait_ge(mean_done, 1)
                    nc.scalar.activation(ssy[:, :, :], ssy[:, :, :], ACT.Sqrt)
                    nc.scalar.activation(sso[:, :, :], sso[:, :, :], ACT.Sqrt).then_inc(root_done, 1)

        @block.vector
        def _(dve):
            nc.vector.memset(ssy[:, :, :], 1.0)
            nc.vector.memset(sso[:, :, :], 1.0).then_inc(zero_done, 1)
            dve.wait_ge(ins_here, 32)
            for n, (_, g, c) in enumerate(z_items):
                dve.wait_ge(item_gated, n + 1)
                nc.vector.tensor_tensor(y_of(c, g), y_of(c, g), gate[0:rows[c], n % BUFS, :], ALU.mult).then_inc(mul_done, 1)
            dve.wait_ge(sq_done, NZ)
            dve.wait_ge(osq_done, TOKENS * GH)
            nc.vector.tensor_scalar(ssy[:, :, :], ssy[:, :, :], 1.0 / GW, EPS, ALU.mult, ALU.add)
            nc.vector.tensor_scalar(sso[:, :, :], sso[:, :, :], 1.0 / DV, EPS, ALU.mult, ALU.add).then_inc(mean_done, 1)
            dve.wait_ge(root_done, 1)
            nc.vector.reciprocal(ssy[:, :, :], ssy[:, :, :])
            k.vlink(dve, nc.vector.reciprocal(sso[:, :, :], sso[:, :, :]))
            for c, g in y_turns:
                nc.vector.tensor_scalar(y_of(c, g), y_of(c, g), ssy[0:rows[c], c, g:g + 1], None, ALU.mult).then_inc(ynorm_done, 1)

            def turn(m):
                kind, c, i = turns[m]
                dve.wait_ge(turn_ready, m + 1)
                w, dst = (wy, k.yT) if kind == "y" else (wo, k.oT)
                nc.vector.tensor_tensor(dst[:, 4 * i:4 * i + 4, out_cols(c)],
                                        ps[BANKS + m % 2][:, :].rearrange("p (a t) -> p a t", a=4)[:, :, 0:rows[c]],
                                        w[:, 4 * i:4 * i + 4].unsqueeze(2).to_broadcast([P, 4, rows[c]]), ALU.mult).then_inc(turn_done, 1)

            for j, (_, i, c) in enumerate(g_items):
                n = NZ + j
                dve.wait_ge(item_gated, n + 1)
                for a in range(2):
                    h = 2 * i + a
                    last = nc.vector.scalar_tensor_tensor(o_of(c, h), o_of(c, h), sso[0:rows[c], c, h:h + 1],
                                                          gate[0:rows[c], n % BUFS, a * DV:(a + 1) * DV], ALU.mult, ALU.mult)
                last.then_inc(mul_done, 1)
                turn(2 * j)
                turn(2 * j + 1)
            for m in range(2 * NG, len(turns)):
                turn(m)




def stage_merge(nc, k):
    KY = GROUPS * GW // P
    PARTS = [(2, 2 * KD, KY, k.yT, 0), (3, 2 * KD + KY, KD, k.oT, 0), (0, 0, KD, None, 0), (1, KD, KD, None, 0)]
    with ExitStack() as ctx:
        sb = lambda n, s, d=F32: ctx.enter_context(nc.sbuf_tensor("m_" + n, s, d, side="right"))
        sem = lambda n: k.sem("m_" + n)
        sig = sb("sig", [P, 2, TOK])
        term = sb("term", [P, TOK])
        x_hi, x_lo = sb("x_hi", [P, KD, TOK], F32R), sb("x_lo", [P, KD, TOK], F32R)
        w_hi, w_lo = sb("w_hi", [P, 2, KD * P], F32R), sb("w_lo", [P, 2, KD * P], F32R)
        ready, sig_done, out_done, x_split, w_split = map(sem, ("ready", "sig_done", "out_done", "x_split", "w_split"))
        k.block_used.update({FIRST["merge"] + j: (ready, 8 * (j + 1)) for j in range(KD)})
        ps = k.ps
        block = ctx.enter_context(nc.Block())

        @block.sync
        def _(sp):
            for b in range(FIRST["merge"], FIRST["out"]):
                load_block(sp, k, b + 2)

        @block.tensor
        def _(pe):
            for j in range(KD):
                b = FIRST["merge"] + j
                wait_block(pe, k, b)
                w = k.ring[b % 2][:, 0:(3 * KD + KY) * P].rearrange("p (k c) -> p k c", c=P)
                for i, k0, n_k, src, at in PARTS:
                    for half, cols in enumerate(TOK_HALVES):
                        out = ps[2 * i + half][:, 0:TOK // 2]
                        if j >= 1:
                            pe.wait_ge(sig_done if i < 2 else out_done, 4 * (j - 1) + 2 * (i % 2) + half + 1)
                        if src is not None:
                            for kt in range(n_k):
                                last = nc.tensor.matmul(out, w[:, k0 + kt, :], src[:, kt, at + cols.start:at + cols.stop],
                                                        start=kt == 0, stop=kt == n_k - 1)
                        else:
                            pe.wait_ge(x_split, KD)
                            pe.wait_ge(w_split, 2 * j + i + 1)
                            for kt in range(n_k):
                                at_w = slice(kt * P, (kt + 1) * P)
                                nc.tensor.matmul(out, w_hi[:, i, at_w], x_hi[:, kt, cols], start=kt == 0, stop=False)
                                nc.tensor.matmul(out, w_lo[:, i, at_w], x_hi[:, kt, cols], start=False, stop=False)
                                last = nc.tensor.matmul(out, w_hi[:, i, at_w], x_lo[:, kt, cols], start=False, stop=kt == n_k - 1)
                        last.then_inc(ready, 1)

        @block.scalar
        def _(act):
            for j in range(KD):
                for i in range(2):
                    for half, cols in enumerate(TOK_HALVES):
                        act.wait_ge(ready, 8 * j + 4 + 2 * i + half + 1)
                        if j >= 1:
                            act.wait_ge(out_done, 4 * (j - 1) + 2 * i + half + 1)
                        nc.scalar.activation(sig[:, i, cols], ps[2 * i + half][:, 0:TOK // 2], ACT.Sigmoid).then_inc(sig_done, 1)

        @block.vector
        def _(dve):
            def split_weights(j):
                b = FIRST["merge"] + j
                wait_block(dve, k, b)
                for i in range(2):
                    src = k.ring[b % 2][:, i * KD * P:(i + 1) * KD * P]
                    if j >= 1:
                        dve.wait_ge(ready, 8 * (j - 1) + 4 + 2 * i + 2)
                    k.vlink(dve, nc.vector.tensor_copy(w_hi[:, i, :], src))
                    nc.vector.tensor_tensor(w_lo[:, i, :], src, w_hi[:, i, :], ALU.subtract).then_inc(w_split, 1)

            split_weights(0)
            for kt in range(KD):
                src = k.xnT[:, kt, NMETA:COLS]
                k.vlink(dve, nc.vector.tensor_copy(x_hi[:, kt, :], src))
                nc.vector.tensor_tensor(x_lo[:, kt, :], src, x_hi[:, kt, :], ALU.subtract).then_inc(x_split, 1)
            for j in range(KD):
                for i in range(2):
                    for half, cols in enumerate(TOK_HALVES):
                        dve.wait_ge(ready, 8 * j + 2 * i + half + 1)
                        dve.wait_ge(sig_done, 4 * j + 2 * i + half + 1)
                        dst = k.mixT[:, j, cols] if i == 0 else term[:, cols]
                        nc.vector.tensor_tensor(dst, ps[4 + 2 * i + half][:, 0:TOK // 2], sig[:, i, cols], ALU.mult).then_inc(out_done, 1)
                dve.wait_ge(out_done, 4 * j + 4)
                nc.vector.tensor_tensor(k.mixT[:, j, :], k.mixT[:, j, :], term[:, :], ALU.add)
                if j + 1 < KD:
                    split_weights(j + 1)


def stage_out(nc, k):
    TOKENS = TILES + 1
    rows = [P] * TILES + [NSAMP]
    mix_cols = lambda c: slice(c * P, c * P + rows[c])
    BANKS = 4
    with ExitStack() as ctx:
        sb = lambda n, s, d=F32: ctx.enter_context(nc.sbuf_tensor("q_" + n, s, d, side="right"))
        sem = lambda n: k.sem("q_" + n)
        prompt_x1 = sb("x1", [P, TILES, D])
        prompt_hn = sb("hn", [P, TILES, D])
        ss = sb("ss", [P, TOKENS])
        x1_of = lambda c: prompt_x1[:, c, :] if c < TILES else k.x1s[:, :]
        hn_of = lambda c: prompt_hn[:, c, :] if c < TILES else k.hns[:, :]
        ins_here, out_ready, x1_done, sq_done, mean_done, root_done = map(
            sem, ("ins_here", "out_ready", "x1_done", "sq_done", "mean_done", "root_done"))
        hn_done, turn_ready, turn_done, stored = map(sem, ("hn_done", "turn_ready", "turn_done", "stored"))
        k.block_used.update({FIRST["out"] + i: (out_ready, TOKENS * (i + 1)) for i in range(2)})
        ps = k.ps
        block = ctx.enter_context(nc.Block())

        @block.sync
        def _(sp):
            for c in range(TOKENS):
                lo = SM + c * P if c < TILES else 0
                sp.dma_start(x1_of(c), k.dram["x_all"][lo:lo + rows[c], :]).then_inc(ins_here, 16)
            sp.dma_start(k.w2[:, :], k.dram["norm2"]).then_inc(ins_here, 16)
            for h in range(2):
                sp.dma_start(k.qw[:, h, :], k.dram["w"]["query"][h]).then_inc(k.qw_here[h], 16)
            sp.dma_start(k.keys[:, :, :], k.dram["keys"]).then_inc(ins_here, 16)
            for c in range(TILES):
                sp.wait_ge(x1_done, TOKENS + c + 1)
                sp.dma_start(k.x1_dram[c * P:(c + 1) * P, :], x1_of(c)).then_inc(stored, 16)
            sp.wait_ge(stored, 16 * TILES)

        @block.tensor
        def _(pe):
            def turn(c):
                pe.wait_ge(hn_done, c + 1)
                for half in range(2):
                    m = 2 * c + half
                    if m >= 2:
                        pe.wait_ge(turn_done, m - 1)
                    for a in range(4):
                        kt = 4 * half + a
                        last = nc.tensor.transpose(ps[4 + m % 2][:, a * P:a * P + rows[c]], hn_of(c)[:, kt * P:(kt + 1) * P],
                                                   k.ident[0:rows[c], 0:rows[c]])
                    last.then_inc(turn_ready, 1)

            for i in range(2):
                b = FIRST["out"] + i
                wait_block(pe, k, b)
                w = k.ring[b % 2][:, 0:KD * 512].rearrange("p (k c) -> p k c", k=KD)
                for c in range(TOKENS):
                    n = i * TOKENS + c
                    if n >= BANKS:
                        pe.wait_ge(x1_done, n - BANKS + 1)
                    for kt in range(KD):
                        last = nc.tensor.matmul(ps[n % BANKS][0:rows[c], :], k.mixT[:, kt, mix_cols(c)], w[:, kt, :], start=kt == 0, stop=kt == KD - 1)
                    last.then_inc(out_ready, 1)
                    if i == 1 and c >= 1:
                        turn(c - 1)
            turn(TILES)

        @block.vector
        def _(dve):
            dve.wait_ge(ins_here, 16 * (TOKENS + 2))
            for i in range(2):
                for c in range(TOKENS):
                    n = i * TOKENS + c
                    dve.wait_ge(out_ready, n + 1)
                    v = x1_of(c)[:, i * 512:(i + 1) * 512]
                    nc.vector.tensor_tensor(v, v, ps[n % BANKS][0:rows[c], :], ALU.add).then_inc(x1_done, 1)
                    if i == 0:
                        continue
                    dve.wait_ge(sq_done, c + 1)
                    nc.vector.tensor_scalar(ss[0:rows[c], c:c + 1], ss[0:rows[c], c:c + 1], 1.0 / D, EPS, ALU.mult, ALU.add).then_inc(mean_done, 1)
                    dve.wait_ge(root_done, c + 1)
                    k.vlink(dve, nc.vector.reciprocal(k.rs2[0:rows[c], c:c + 1], ss[0:rows[c], c:c + 1]))
                    nc.vector.scalar_tensor_tensor(hn_of(c), x1_of(c), k.rs2[0:rows[c], c:c + 1], k.w2[0:rows[c], :], ALU.mult, ALU.mult).then_inc(hn_done, 1)

        @block.scalar
        def _(act):
            def copies(c):
                for half in range(2):
                    act.wait_ge(turn_ready, 2 * c + half + 1)
                    nc.scalar.copy(k.hnT[:, 4 * half:4 * half + 4, mix_cols(c)],
                                   ps[4 + half][:, :].rearrange("p (a t) -> p a t", a=4)[:, :, 0:rows[c]]).then_inc(turn_done, 1)

            for c in range(TOKENS):
                act.wait_ge(x1_done, TOKENS + c + 1)
                nc.scalar.activation(hn_of(c), x1_of(c), ACT.Square, accum_out=ss[0:rows[c], c:c + 1]).then_inc(sq_done, 1)
                act.wait_ge(mean_done, c + 1)
                nc.scalar.activation(ss[0:rows[c], c:c + 1], ss[0:rows[c], c:c + 1], ACT.Sqrt).then_inc(root_done, 1)
                if c >= 1:
                    copies(c - 1)
            copies(TILES)


def stage_peer(nc, k):
    UNITS = TILES * EH
    RING = 8
    LOT = 8
    PAIR = 2
    DIAGS = 4
    PARTS_AFTER = (1, 3, 5, 6)
    AHEAD = 3
    SIX_AFTER, TWO_AFTER = (0, 1, 3, 4, 5, 6), (2, 4)
    SROWS = NSAMP * EH
    SLOTS = TOPK
    QUERY_SLOTS, SCORE_SLOT, QUERY_COPIES = (2, 8), 13, (3, 6)
    LOW = -3.4e38
    with ExitStack() as ctx:
        sb = lambda n, s, d=F32, side="left": ctx.enter_context(nc.sbuf_tensor("p_" + n, s, d, side=side))
        sem = lambda n: k.sem("p_" + n)
        rows = sb("rows", [P, RING, ROW])
        wf = sb("wf", [P, D])
        hn_cur = sb("hn_cur", [P, D])
        idx = sb("idx", [P, (UNITS + 2) * SLOTS], U32)
        gates = sb("gates", [P, (UNITS + 2) * SLOTS])
        sidx = sb("sidx", [SROWS, SLOTS], U32)
        sgates = sb("sgates", [SROWS, SLOTS])
        sc = sb("sc", [P, UNITS + 2, 2 * NKEYS])
        ssc = sb("ssc", [SROWS, 2 * NKEYS])
        ssc_head = sb("ssc_head", [NSAMP, 2, 2 * NKEYS])
        q = sb("q", [P, 2, TOK])
        x1_in = sb("x1_in", [P, D])
        ssel = sb("ssel", [SROWS, NSAMP])
        ssel_t = sb("ssel_t", [NSAMP, SROWS])
        lot = sb("lot", [P, 2, LOT], U32)
        hid = sb("hid", [P, SLOTS])
        gel = sb("gel", [P, SLOTS])
        diag = sb("diag", [P, DIAGS, P])
        zeros = sb("zeros", [P, 512], BF16)
        fin = sb("fin", [P, D])
        sfin = k.x1s
        squares = sb("squares", [P, D])
        fss = sb("fss", [P, 2])
        tv = sb("tv", [P, 2, TOPK])
        ti = sb("ti", [P, 2, TOPK], U32)
        tif = sb("tif", [P, 2, TOPK])
        rest = sb("rest", [P, 2, NKEYS])
        cand = sb("cand", [P, TOPK, TOPK])
        crest = sb("crest", [P, TOPK, TOPK])
        bv = sb("bv", [P, TOPK])
        bp = sb("bp", [P, TOPK], U32)
        ab = sb("ab", [P, 2, TOPK], U32)
        abf = sb("abf", [P, 2, TOPK])
        hot = sb("hot", [P, 2, TOPK, TOPK])
        pick = sb("pick", [P, 2, TOPK])
        pickf = sb("pickf", [P, TOPK])
        iota = sb("iota", [P, TOPK])
        scu = sb("scu", [P, 2 * NKEYS])
        nmax = sb("nmax", [P, 1])
        ex = sb("ex", [P, TOPK])
        esum = sb("esum", [P, 1])
        ins_here, lot_here, dot_done, gelu_done, diag_done, used = map(
            sem, ("ins_here", "lot_here", "dot_done", "gelu_done", "diag_done", "used"))
        row_here = [sem(f"row_here{j}") for j in range(RING)]
        choice, best_done, exp_done, cleared, hn_rep, hn_cur_done = map(
            sem, ("choice", "best_done", "exp_done", "cleared", "hn_rep", "hn_cur_done"))
        acc_closed, fin_done, fsq_done, fmean, froot, out_ready, out_done, turn = map(
            sem, ("acc_closed", "fin_done", "fsq_done", "fmean", "froot", "out_ready", "out_done", "turn"))
        x1_here, opened, computed, copied, ssc_here = map(sem, ("x1_here", "opened", "computed", "copied", "ssc_here"))
        ps = k.ps
        ACC, SACC, REP = (0, 1), (2, 3), (4, 5)
        Q, QREST, SC, SSC = (2, 3), (4, 5), (6, 7), 4
        INS = 5
        CHOICE_STEPS = 21
        block = ctx.enter_context(nc.Block())

        @block.sync
        def _(sp):
            def load_x1(tile):
                sp.dma_start(x1_in[:, :], k.x1_dram[bass.ds(tile * P, P), :]).then_inc(x1_here, 16)

            load_x1(0)
            for dst, src in ((wf[:, :], k.dram["norm_f"]), (iota[:, :], k.dram["c_iota"]), (ssel[:, :], k.dram["c_ssel"]), (ssel_t[:, :], k.dram["c_ssel_t"]),
                             (zeros[:, :], k.dram["c_zeros"])):
                sp.dma_start(dst, src).then_inc(ins_here, 16)
            for h in range(EH):
                if h + 2 < EH:
                    sp.wait_ge(computed, 3 * h + 2)
                    sp.dma_start(k.qw[:, h % 2, :], k.dram["w"]["query"][h + 2]).then_inc(k.qw_here[h % 2], 16)
                sp.wait_ge(copied, 5 * h + 5)
                if h >= 1:
                    sp.wait_ge(ssc_here, 16 * h)
                sp.dma_start(ssc[h * NSAMP:(h + 1) * NSAMP, :], ssc_head[:, h % 2, :]).then_inc(ssc_here, 16)
            sp.wait_ge(opened, 1)
            sp.wait_ge(hn_cur_done, 1)
            load_x1(1)
            sp.wait_ge(out_ready, 1)
            sp.dma_start(k.dram["o_sample"], sfin[:, :]).then_inc(out_done, 16)

            def store(tile):
                sp.wait_ge(out_ready, tile + 2)
                sp.sem_inc(turn, 1)
                sp.dma_start(k.dram["o_prompt"][bass.ds(tile * P, P), :], fin[:, :]).then_inc(out_done, 16)

            with sp.Fori(1, TILES - 1) as c:
                sp.wait_ge(opened, c + 1)
                sp.sem_inc(turn, 1)
                sp.wait_ge(hn_cur_done, c + 2)
                sp.sem_inc(turn, 1)
                load_x1(c + 1)
                store(c - 1)
            store(TILES - 2)
            store(TILES - 1)
            sp.wait_ge(out_done, 16 * (TILES + 1))

        @block.gpsimd
        def _(pool):
            def gathers(m, unit):
                for s in range(SLOTS):
                    if s % LOT == 0:
                        pool.wait_ge(lot_here, unit * 2 + s // LOT + 1)
                        pool.sem_inc(turn, 1)
                    pool.wait_ge(used, unit * SLOTS + s + 1)
                    pool.sem_inc(turn, 1)
                    nc.gpsimd.indirect_dma_start(rows[0:m, s % RING, :], None, k.dram["experts"],
                                                 bass.IndirectOffsetOnAxis(lot[0:m, s // LOT, s % LOT:s % LOT + 1], 0)).then_inc(row_here[s % RING], 16)

            with pool.Fori(0, EH) as i:
                gathers(P, i)
            gathers(SROWS, EH)
            with pool.Fori(EH, UNITS) as i:
                gathers(P, i + 1)

        @block.vector
        def _(dve):
            def choice_parts(m, scores, idx_out, gates_out, turn_no, wait=lambda: None):
                count = [0]

                def link(ins):
                    count[0] += 1
                    ins.then_inc(choice, 1)
                    dve.wait_ge(choice, turn_no * CHOICE_STEPS + count[0])
                    dve.sem_inc(turn, 1)

                def best16(values, rest_, top, where):
                    link(nc.vector.max(top[:, 0:8], values))
                    nc.vector.max_index(where[:, 0:8], top[:, 0:8], values)
                    link(nc.vector.match_replace(rest_, top[:, 0:8], values, LOW))
                    link(nc.vector.max(top[:, 8:16], rest_))
                    nc.vector.max_index(where[:, 8:16], top[:, 8:16], rest_)

                flat = lambda t: t[0:m, :, :].rearrange("p a b -> p (a b)")
                grid = [m, TOPK, TOPK]

                def keys(s):
                    best16(scu[0:m, s * NKEYS:(s + 1) * NKEYS], rest[0:m, s, :], tv[0:m, s, :], ti[0:m, s, :])

                def part0():
                    wait()
                    link(nc.vector.tensor_copy(scu[0:m, :], scores))
                    keys(0)

                def part1():
                    keys(1)

                def part2():
                    link(nc.vector.tensor_tensor(cand[0:m], tv[0:m, 0, :].unsqueeze(2).to_broadcast(grid), tv[0:m, 1, :].unsqueeze(1).to_broadcast(grid), ALU.add))
                    nc.vector.tensor_copy(tif[0:m], ti[0:m])
                    link(nc.vector.max(bv[0:m, 0:8], flat(cand)))
                    nc.vector.max_index(bp[0:m, 0:8], bv[0:m, 0:8], flat(cand))
                    link(nc.vector.match_replace(flat(crest), bv[0:m, 0:8], flat(cand), LOW))
                    link(nc.vector.max(bv[0:m, 8:16], flat(crest)))
                    nc.vector.tensor_scalar(nmax[0:m], bv[0:m, 0:1], -1.0, None, ALU.mult).then_inc(best_done, 1)
                    link(nc.vector.max_index(bp[0:m, 8:16], bv[0:m, 8:16], flat(crest)))

                def part3():
                    nc.vector.tensor_scalar(ab[0:m, 0, :], bp[0:m], 4, None, ALU.logical_shift_right)
                    link(nc.vector.tensor_scalar(ab[0:m, 1, :], bp[0:m], 15, None, ALU.bitwise_and))
                    link(nc.vector.tensor_copy(abf[0:m], ab[0:m]))
                    for s in range(2):
                        last = nc.vector.tensor_tensor(hot[0:m, s], abf[0:m, s, :].unsqueeze(2).to_broadcast(grid),
                                                       iota[0:m, :].unsqueeze(1).to_broadcast(grid), ALU.is_equal)
                    link(last)
                    for s in range(2):
                        last = nc.vector.tensor_tensor(hot[0:m, s], hot[0:m, s], tif[0:m, s, :].unsqueeze(1).to_broadcast(grid), ALU.mult)
                    link(last)
                    link(nc.vector.tensor_reduce(pick[0:m], hot[0:m], AX.X, ALU.add))
                    link(nc.vector.scalar_tensor_tensor(pickf[0:m], pick[0:m, 0, :], float(NKEYS), pick[0:m, 1, :], ALU.mult, ALU.add))
                    link(nc.vector.tensor_copy(idx_out, pickf[0:m]))
                    dve.wait_ge(exp_done, turn_no + 1)
                    link(nc.vector.reciprocal(esum[0:m], esum[0:m]))
                    link(nc.vector.tensor_scalar(gates_out, ex[0:m], esum[0:m], None, ALU.mult))
                    assert count[0] == CHOICE_STEPS, count[0]

                return part0, part1, part2, part3

            def choose(*of):
                for part in choice_parts(*of):
                    part()

            def stage_lot(m, src, half):
                nc.vector.tensor_copy(lot[0:m, half, :], src).then_inc(lot_here, 1)

            def diags(m, width, ident, unit, pair, gate):
                dve.wait_ge(gelu_done, unit * (SLOTS // PAIR) + pair + 1)
                for s in range(PAIR * pair, PAIR * pair + PAIR):
                    dve.wait_ge(used, RING + unit * SLOTS + s - DIAGS + 1)
                    nc.vector.tensor_scalar(diag[0:m, s % DIAGS, 0:width], ident, gel[0:m, s:s + 1], gate(s), ALU.mult, ALU.mult).then_inc(diag_done, 1)

            def unit_slots(m, width, ident, hn, unit, gate, next_lots, parts, next_m=P, after=PARTS_AFTER):
                for pair in range(SLOTS // PAIR):
                    for s in range(PAIR * pair, PAIR * pair + PAIR):
                        dve.wait_ge(row_here[s % RING], unit * 16 * (SLOTS // RING) + 16 * (s // RING + 1))
                        u = rows[0:m, s % RING, 0:D]
                        nc.vector.tensor_tensor_reduce(out=u, in0=u, in1=hn, scale=1.0, scalar=0.0, op0=ALU.mult, op1=ALU.add,
                                                       accum_out=hid[0:m, s:s + 1]).then_inc(dot_done, 1)
                    if (pair * PAIR + PAIR) % LOT == 0:
                        half = pair * PAIR // LOT
                        stage_lot(next_m, next_lots(half), half)
                    if pair >= 1:
                        diags(m, width, ident, unit, pair - 1, gate)
                    if pair in after:
                        parts[after.index(pair)]()
                diags(m, width, ident, unit, SLOTS // PAIR - 1, gate)

            def read_sum(m, bank, out, n):
                dve.wait_ge(acc_closed, n + 1)
                for half in range(2):
                    last = nc.vector.tensor_copy(out[:, half * 512:half * 512 + 512], ps[bank[half]][0:m, :])
                last.then_inc(fin_done, 1)

            def last_norm(m, out, j, n):
                dve.wait_ge(fsq_done, n + 1)
                nc.vector.tensor_scalar(fss[0:m, j:j + 1], fss[0:m, j:j + 1], 1.0 / D, EPS, ALU.mult, ALU.add).then_inc(fmean, 1)
                dve.wait_ge(froot, n + 1)
                nc.vector.reciprocal(fss[0:m, j:j + 1], fss[0:m, j:j + 1]).then_inc(cleared, 1)
                dve.wait_ge(cleared, n + 1)
                nc.vector.scalar_tensor_tensor(out, out, fss[0:m, j:j + 1], wf[0:m, :], ALU.mult, ALU.mult).then_inc(out_ready, 1)

            unit_of = lambda t, i: t[:, bass.ds(i * SLOTS, SLOTS)]
            sc_flat = sc[:, :, :].rearrange("p u n -> p (u n)")
            gate_of = lambda i: lambda s: gates[:, bass.ds(i * SLOTS + s, 1)]
            lots_of = lambda i: lambda half: idx[:, bass.ds(i * SLOTS + half * LOT, LOT)]
            choice_of = lambda i, turn_no, wait=lambda: None: choice_parts(
                P, sc_flat[:, bass.ds(i * 2 * NKEYS, 2 * NKEYS)], unit_of(idx, i), unit_of(gates, i), turn_no, wait)
            head_scored = lambda h: lambda: dve.wait_ge(copied, 5 * h + 5)

            def tile_hn(c):
                return nc.vector.scalar_tensor_tensor(hn_cur[:, :], x1_in[:, :], k.rs2[:, bass.ds(c, 1)], k.w2[:, :], ALU.mult, ALU.mult)

            k.vlink(dve, nc.vector.memset(sc[:, UNITS:UNITS + 2, :], 0.0))
            dve.wait_ge(ins_here, 16 * INS)
            dve.wait_ge(x1_here, 16)
            tile_hn(0).then_inc(hn_cur_done, 1)
            for part in choice_of(0, 0, head_scored(0)):
                part()
            for half in range(2):
                stage_lot(P, lots_of(0)(half), half)
            for part in choice_of(1, 1, head_scored(1)):
                part()
            dve.wait_ge(hn_cur_done, 1)
            with dve.Fori(0, EH - 2) as i:
                unit_slots(P, P, k.ident[:, :], hn_cur[:, :], i, gate_of(i), lots_of(i + 1), choice_of(i + 2, i + 2, head_scored(i + 2)))
            unit_slots(P, P, k.ident[:, :], hn_cur[:, :], EH - 2, gate_of(EH - 2), lots_of(EH - 1),
                       choice_parts(SROWS, ssc[:, :], sidx[:, :], sgates[:, :], EH, lambda: dve.wait_ge(ssc_here, 16 * EH)))
            second = choice_of(EH + 1, EH + 2)
            unit_slots(P, P, k.ident[:, :], hn_cur[:, :], EH - 1, gate_of(EH - 1), lambda half: sidx[:, half * LOT:(half + 1) * LOT],
                       choice_of(EH, EH + 1) + second[:2], next_m=SROWS, after=SIX_AFTER)
            dve.wait_ge(dot_done, EH * SLOTS)
            dve.wait_ge(hn_rep, 1)
            for half in range(2):
                last = nc.vector.tensor_copy(hn_cur[0:SROWS, half * 512:half * 512 + 512], ps[REP[half]][0:SROWS, :])
            last.then_inc(hn_cur_done, 1)
            dve.wait_ge(hn_cur_done, 2)
            unit_slots(SROWS, NSAMP, ssel[:, :], hn_cur[0:SROWS, :], EH, lambda s: sgates[:, s:s + 1], lots_of(EH), second[2:], after=TWO_AFTER)
            read_sum(P, ACC, fin[:, :], 0)
            read_sum(NSAMP, SACC, sfin[:, :], 1)
            last_norm(NSAMP, sfin[:, :], 0, 0)
            with dve.Fori(1, TILES) as c:
                dve.wait_ge(dot_done, (c * EH + 1) * SLOTS)
                dve.wait_ge(x1_here, c * 16 + 16)
                tile_hn(c).then_inc(hn_cur_done, 1)
                dve.wait_ge(hn_cur_done, c + 2)
                dve.sem_inc(turn, 1)
                def unit(i):
                    unit_slots(P, P, k.ident[:, :], hn_cur[:, :], i + 1, gate_of(i), lots_of(i + 1), choice_of(i + 2, i + 3))

                unit(c * EH)
                last_norm(P, fin[:, :], 1, c)
                with dve.Fori(1, EH) as h:
                    unit(c * EH + h)
                dve.wait_ge(out_done, c * 16 + 16)
                read_sum(P, ACC, fin[:, :], c + 1)
            last_norm(P, fin[:, :], 1, TILES)

        @block.scalar
        def _(act):
            def softmax(m, turn_no):
                act.wait_ge(best_done, turn_no + 1)
                nc.scalar.activation(ex[0:m], bv[0:m], ACT.Exp, bias=nmax[0:m], accum_out=esum[0:m]).then_inc(exp_done, 1)

            def copy_query(h, s):
                act.wait_ge(computed, 3 * h + s + 1)
                nc.scalar.copy(q[:, s, TOK_HALVES[0]], ps[Q[s]][:, 0:TOK // 2])
                nc.scalar.copy(q[:, s, TOK_HALVES[1]], ps[QREST[s]][:, 0:TOK // 2]).then_inc(copied, 1)

            def copy_scores(h):
                act.wait_ge(computed, 3 * h + 3)
                for i, bank in enumerate(SC):
                    nc.scalar.copy(sc[:, 0:UNITS, :].rearrange("p (c h) n -> p c h n", h=EH)[:, 2 * i:2 * i + 2, h, :],
                                   ps[bank][:, :].rearrange("p (c n) -> p c n", c=2)).then_inc(copied, 1)
                if h >= 2:
                    act.wait_ge(ssc_here, 16 * (h - 1))
                nc.scalar.copy(ssc_head[:, h % 2, :], ps[SSC][0:NSAMP, 0:2 * NKEYS]).then_inc(copied, 1)

            def copy_head(h):
                copy_query(h, 0)
                copy_query(h, 1)
                copy_scores(h)

            def unit_gelus(m, unit, softmaxes, head=None):
                for pair in range(SLOTS // PAIR):
                    if head is not None and pair in QUERY_COPIES:
                        copy_query(head, QUERY_COPIES.index(pair))
                    act.wait_ge(dot_done, unit * SLOTS + PAIR * pair + PAIR)
                    s = slice(PAIR * pair, PAIR * pair + PAIR)
                    nc.scalar.activation(gel[0:m, s], hid[0:m, s], ACT.Gelu).then_inc(gelu_done, 1)
                    if pair in softmaxes:
                        softmax(*softmaxes[pair])
                if head is not None:
                    copy_scores(head)

            def last_norm(m, out, j, n, sums):
                act.wait_ge(fin_done, sums)
                if j == 1:
                    act.wait_ge(froot, n)
                nc.scalar.activation(squares[0:m, :], out, ACT.Square, accum_out=fss[0:m, j:j + 1]).then_inc(fsq_done, 1)
                act.wait_ge(fmean, n + 1)
                nc.scalar.activation(fss[0:m, j:j + 1], fss[0:m, j:j + 1], ACT.Sqrt).then_inc(froot, 1)

            copy_head(0)
            softmax(P, 0)
            copy_head(1)
            softmax(P, 1)
            copy_head(2)
            for i in range(EH):
                softmaxes = {PARTS_AFTER[2]: (SROWS if i == EH - 2 else P, i + 2)}
                if i == EH - 1:
                    softmaxes = {SIX_AFTER[2]: (P, i + 2)}
                unit_gelus(P, i, softmaxes, i + AHEAD if i + AHEAD < EH else None)
            unit_gelus(SROWS, EH, {TWO_AFTER[0]: (P, EH + 2)})
            last_norm(NSAMP, sfin[:, :], 0, 0, 2)
            with act.Fori(1, TILES) as c:
                unit_gelus(P, c * EH + 1, {PARTS_AFTER[2]: (P, c * EH + 3)})
                last_norm(P, fin[:, :], 1, c, c + 1)
                with act.Fori(1, EH) as h:
                    i = c * EH + h
                    unit_gelus(P, i + 1, {PARTS_AFTER[2]: (P, i + 3)})
            last_norm(P, fin[:, :], 1, TILES, TILES + 1)

        @block.tensor
        def _(pe):
            def open_sum(banks, m, x1):
                return [nc.tensor.matmul(ps[b][0:m, :], k.ident[0:m, 0:m], x1[:, half * 512:half * 512 + 512], start=True, stop=False)
                        for half, b in enumerate(banks)]

            def close_sum(banks, m):
                for b in banks:
                    last = nc.tensor.matmul(ps[b][0:m, :], zeros[:, 0:m], zeros[:, :], start=False, stop=True)
                last.then_inc(acc_closed, 1)

            def queries(h, s):
                if s == 0:
                    pe.wait_ge(k.qw_here[h % 2], 16 * (h // 2 + 1))
                if h >= 1:
                    pe.wait_ge(copied, 5 * h)
                w = k.qw[:, h % 2, :].rearrange("p (k c) -> p k c", k=KD)
                for bank, cols in ((Q[s], TOK_HALVES[0]), (QREST[s], TOK_HALVES[1])):
                    for kt in range(KD):
                        last = nc.tensor.matmul(ps[bank][:, 0:cols.stop - cols.start], w[:, kt, s * P:(s + 1) * P], k.hnT[:, kt, cols],
                                                start=kt == 0, stop=kt == KD - 1)
                last.then_inc(computed, 1)

            def scores(h):
                pe.wait_ge(copied, 5 * h + 2)
                for c in range(TILES + 1):
                    m, bank, at = (P, SC[c // 2], c % 2 * 2 * NKEYS) if c < TILES else (NSAMP, SSC, 0)
                    for s in range(2):
                        last = nc.tensor.matmul(ps[bank][0:m, at + s * NKEYS:at + (s + 1) * NKEYS], q[:, s, c * P:c * P + m], k.keys[:, 2 * h + s, :],
                                                start=True, stop=True)
                last.then_inc(computed, 1)

            def unit_sums(m, width, banks, unit, head=None):
                for s in range(SLOTS):
                    if head is not None and s in QUERY_SLOTS:
                        queries(head, QUERY_SLOTS.index(s))
                    if head is not None and s == SCORE_SLOT:
                        scores(head)
                    pe.wait_ge(diag_done, unit * SLOTS + s + 1)
                    for half, b in enumerate(banks):
                        last = nc.tensor.matmul(ps[b][0:width, :], diag[0:m, s % DIAGS, 0:width],
                                                rows[0:m, s % RING, D + half * 512:D + half * 512 + 512], start=False, stop=False)
                    last.then_inc(used, 1)

            for h in range(AHEAD):
                if h == 1:
                    pe.wait_ge(x1_here, 16)
                    first, second = open_sum(ACC, P, x1_in)
                    first.then_inc(used, RING)
                    second.then_inc(opened, 1)
                queries(h, 0)
                queries(h, 1)
                scores(h)
            pe.wait_ge(ins_here, 16 * INS)
            for h in range(EH):
                if h == EH - 2:
                    pe.wait_ge(copied, 5 * EH)
                    for half, b in enumerate(REP):
                        last = nc.tensor.matmul(ps[b][0:SROWS, :], ssel_t[:, :], k.hns[:, half * 512:half * 512 + 512], start=True, stop=True)
                    last.then_inc(hn_rep, 1)
                    open_sum(SACC, NSAMP, k.x1s)
                unit_sums(P, P, ACC, h, h + AHEAD if h + AHEAD < EH else None)
            close_sum(ACC, P)
            unit_sums(SROWS, NSAMP, SACC, EH)
            close_sum(SACC, NSAMP)
            with pe.Fori(1, TILES) as c:
                pe.wait_ge(fin_done, c + 1)
                pe.wait_ge(x1_here, c * 16 + 16)
                open_sum(ACC, P, x1_in)[1].then_inc(opened, 1)
                with pe.Fori(0, EH) as h:
                    unit_sums(P, P, ACC, c * EH + h + 1)
                close_sum(ACC, P)


def build(nc, ins, outs):
    with ExitStack() as ctx:
        k = Shared({**ins, **outs})
        k.sem = lambda n: ctx.enter_context(nc.semaphore(n))
        sb = lambda n, s, d=F32, side="left": ctx.enter_context(nc.sbuf_tensor(n, s, d, side=side))
        k.ps = [ctx.enter_context(nc.psum_tensor(f"bank{i}", [P, 512], F32)) for i in range(8)]
        k.vlink, k.alink, k.plink = Link(k.sem("vector_step")), Link(k.sem("scalar_step")), Link(k.sem("pool_step"))
        k.consts_here, k.block_used = k.sem("consts_here"), {}
        k.block_here = [k.sem("block_here0"), k.sem("block_here1")]
        k.ident = sb("ident", [P, P])
        early = ExitStack()
        sb = lambda n, s, d=F32: early.enter_context(nc.sbuf_tensor(n, s, d, side="left"))
        k.tri = sb("tri", [P, P])
        k.tri64 = sb("tri64", [P, P])
        k.ones = sb("ones", [P, P])
        k.identb = sb("identb", [P, P], BF16)
        k.future = sb("future", [P, 4 * P], BF16)
        k.att_mask = sb("att_mask", [P, P], I32)
        k.sel3 = sb("sel3", [SPLIT, NSAMP, P], BF16)
        k.diag8 = sb("diag8", [NSAMP, NSAMP])
        k.eye8 = sb("eye8", [P, NSAMP, NSAMP])
        k.wglr = sb("wglr_in", [P, KD, RANK])
        k.up = sb("gate_up_in", [RANK + 1, GH * DK])
        k.const_loads = [(k.wglr[:, :, :], k.dram["wglr"]), (k.up[:, :], k.dram["gate_up"]),
                         (k.ident[:, :], k.dram["c_ident"]), (k.tri[:, :], k.dram["c_tri"]), (k.tri64[:, :], k.dram["c_tri64"]), (k.ones[:, :], k.dram["c_ones"]),
                         (k.identb[:, :], k.dram["c_identb"]), (k.future[:, :], k.dram["c_future"]), (k.att_mask[:, :], k.dram["c_att_mask"]),
                         (k.sel3[:, :, :], k.dram["c_sel3"]), (k.diag8[:, :], k.dram["c_diag8"]), (k.eye8[:, :, :], k.dram["c_eye8"])]
        k.dt = sb("dt", [P, 6, HEADS])
        k.da = sb("da", [P, 6, HEADS])
        k.dte = sb("dte", [P, 5, HEADS])
        k.eac = sb("eac", [P, TILES, HEADS])
        k.cdec = sb("cdec", [P, TILES, HEADS])
        k.nac = sb("nac", [P, TILES, HEADS])
        k.decs = sb("decs", [NSAMP, HEADS])
        k.decb = sb("decb", [P, NSAMP, HEADS])
        base = ExitStack()
        ring = [base.enter_context(nc.sbuf_tensor(f"ring{i}", [P, KD * CT * P], F32, side="left")) for i in range(2)]
        k.ring = ring
        k.xnT = base.enter_context(nc.sbuf_tensor("xnT", [P, KD, COLS], F32, side="left"))
        k.xsm = base.enter_context(nc.sbuf_tensor("xsm", [P, KD, SM], F32, side="left"))
        k.tile_ready = k.sem("tile_ready")
        stage_norm(nc, k)
        top = ExitStack()
        k.y = top.enter_context(nc.sbuf_tensor("y", [P, TILES, GROUPS * GW], F32, side="left"))
        k.ys = top.enter_context(nc.sbuf_tensor("ys", [NSAMP, GROUPS * GW], F32, side="left"))
        stage_ssd(nc, k)
        top2 = ExitStack()
        k.o = top2.enter_context(nc.sbuf_tensor("o", [P, TILES, GH * DV], F32, side="left"))
        k.os = top2.enter_context(nc.sbuf_tensor("os", [NSAMP, GH * DV], F32, side="left"))
        stage_gla(nc, k)
        mid = ExitStack()
        k.yT = mid.enter_context(nc.sbuf_tensor("yT", [P, GROUPS * GW // P, TOK], F32, side="right"))
        k.oT = mid.enter_context(nc.sbuf_tensor("oT", [P, KD, TOK], F32, side="right"))
        stage_gate(nc, k)
        top2.close()
        top.close()
        k.mixT = base.enter_context(nc.sbuf_tensor("mixT", [P, KD, TOK], F32, side="left"))
        stage_merge(nc, k)
        mid.close()
        late = ExitStack()
        sb = lambda n, s, d=F32: late.enter_context(nc.sbuf_tensor(n, s, d, side="right"))
        k.hnT = sb("hnT", [P, KD, TOK])
        k.qw = sb("query_w", [P, 2, KD * 2 * P])
        k.keys = sb("sub_keys", [P, 2 * EH, NKEYS])
        k.w2 = sb("w2", [P, D])
        k.rs2 = sb("rs2", [P, TILES + 1])
        k.x1s = sb("x1s", [NSAMP, D])
        k.hns = sb("hns", [NSAMP, D])
        k.qw_here = [k.sem("qw_here0"), k.sem("qw_here1")]
        k.x1_dram = nc.dram_tensor("x1_kept", [SEQ, D], F32).ap()
        stage_out(nc, k)
        base.close()
        early.close()
        stage_peer(nc, k)
        late.close()



def _weight_tiles(w, width):
    n_k = w.shape[0] // P
    return np.ascontiguousarray(w.reshape(n_k, P, -1, width).transpose(2, 1, 0, 3).reshape(-1, P, n_k * width))


def _every_partition(row):
    return np.ascontiguousarray(np.broadcast_to(row, (P, row.shape[-1])))


def _channels():
    x, b = np.arange(GW), np.arange(P)
    return np.concatenate([np.concatenate([g * GW + x, GROUPS * GW + g * P + b, GROUPS * (GW + P) + g * P + b]) for g in range(GROUPS)])


def _constants():
    i = np.arange(P)
    upto = (i[:, None] <= i[None, :]).astype(np.float32)
    chunk = i[:, None] // GCH == i[None, :] // GCH
    b = np.arange(NSAMP)
    ssel = (np.arange(NSAMP * EH)[:, None] % NSAMP == b[None, :]).astype(np.float32)
    low = np.dtype("bfloat16")
    sel3 = np.zeros((SPLIT, NSAMP, P), low)
    for part in range(0, SPLIT, 32):
        sel3[part + b, b, :] = 1
    return dict(
        c_ident=np.eye(P, dtype=np.float32), c_tri=upto, c_tri64=(upto * chunk / 16).astype(np.float32), c_ones=np.ones((P, P), np.float32),
        c_identb=np.eye(P).astype(low), c_future=np.ascontiguousarray(np.tile(np.where(upto > 0, 0.0, -1e30).astype(low), (1, 4))),
        c_att_mask=(upto * chunk).astype(np.int32), c_sel3=sel3, c_diag8=np.eye(NSAMP, dtype=np.float32),
        c_eye8=np.ascontiguousarray(np.broadcast_to(np.eye(NSAMP, dtype=np.float32), (P, NSAMP, NSAMP))),
        c_zeros=np.zeros((P, 512), low), c_iota=_every_partition(np.arange(TOPK, dtype=np.float32)), c_ssel=ssel, c_ssel_t=np.ascontiguousarray(ssel.T))


def _inputs(a):
    d_inner, gn = GROUPS * GW, GROUPS * P
    sizes = (d_inner, d_inner + 2 * gn, HEADS, GH * DK, GH * DK, GH * DV, GH * DV, RANK, 2 * D)
    z, xbc, dt, q, key, v, g, glr, merge = np.split(a["w_in"][0], np.cumsum(sizes)[:-1], axis=1)
    ch = _channels()
    conv = np.concatenate([a["conv_w"][0], a["conv_b"]], 0)[:, ch]
    hist = np.zeros((P, GROUPS, CT, CONV, NSAMP), np.float32)
    hist[:, :, :, :HIST] = a["state_conv"][0][:, :, ch].reshape(NSAMP, HIST, GROUPS, CT, P).transpose(4, 2, 3, 1, 0)
    w_gla = [np.concatenate([q[:, h * DK:(h + 1) * DK], key[:, h * DK:(h + 1) * DK], v[:, h * DV:(h + 1) * DV]], 1) for h in range(GH)]
    w = dict(
        ssd=_weight_tiles(xbc[:, ch], CT * P), gla=np.concatenate([_weight_tiles(x, 2 * DK + DV) for x in w_gla]),
        z=_weight_tiles(z, 512), g=_weight_tiles(g, 512), out=_weight_tiles(a["w_out"][0], 512), query=_weight_tiles(a["peer_w_q"][0], 2 * P),
        merge=np.concatenate([_weight_tiles(x, P) for x in (merge[:, :D], merge[:, D:], a["w_ssd_out"][0], a["w_gla_out"][0])], 2))
    x = dict(
        x_all=np.concatenate([a["x_sample"][:, 0], np.zeros((META0 - NSAMP, D), np.float32), a["meta_tokens"], a["x_prompt"][0]]),
        norm1=np.ascontiguousarray(a["norm1_w"][0].reshape(KD, P).T), wdt=_weight_tiles(dt, HEADS)[0].reshape(P, KD, HEADS),
        dt_bias=_every_partition(a["dt_bias"][0]), a_log=_every_partition(a["a_log"][0]), d_skip=_every_partition(a["d_skip"][0]),
        conv_w=np.ascontiguousarray(conv.reshape(CONV + 1, GROUPS, CT, P).transpose(3, 1, 2, 0)), state_conv=hist,
        state_ssd=np.ascontiguousarray(a["state_ssd"][0].reshape(NSAMP, GROUPS, GW, P).transpose(1, 3, 0, 2)),
        wglr=_weight_tiles(glr, RANK)[0].reshape(P, KD, RANK), gate_up=np.concatenate([a["gla_gate_up"][0], a["gla_gate_b"]], 0),
        state_gla=np.ascontiguousarray(a["state_gla"][0].transpose(1, 2, 0, 3)),
        ssd_norm=np.ascontiguousarray(a["ssd_norm_w"][0].reshape(-1, P).T),
        gla_norm=np.ascontiguousarray(np.tile(a["gla_norm_w"][0].reshape(DV // P, P), (GH, 1)).T),
        norm2=_every_partition(a["norm2_w"][0]), norm_f=_every_partition(a["final_norm_w"]),
        keys=np.ascontiguousarray(a["peer_sub_keys"][0].transpose(3, 1, 0, 2).reshape(P, 2 * EH, NKEYS)),
        experts=np.concatenate([a["peer_u"][0], a["peer_v"][0]], 1))
    return {**x, **{"w_" + n: t for n, t in w.items()}, **_constants()}


_OUTS = dict(o_prompt=(SEQ, D), o_sample=(NSAMP, D), o_pssd=(GROUPS, P, GW), o_pconv=(P, GROUPS, CT, HIST), o_pgla=(GH, DK, DV),
             o_sssd=(GROUPS, P, NSAMP, GW), o_sconv=(P, GROUPS, CT, HIST, NSAMP), o_sgla=(GH, DK, NSAMP, DV))


def kernel(**inputs):
    import concourse.bacc as _bacc
    from concourse.bass_utils import run_bass_kernel_spmd as _run

    nc = _bacc.Bacc("TRN2", target_bir_lowering=False, num_devices=1)
    arrays = {f"in_{n}": x for n, x in _inputs({n: np.asarray(x) for n, x in inputs.items()}).items()}
    ins = {n[3:]: nc.dram_tensor(n, x.shape, mybir.dt.from_np(x.dtype), kind="ExternalInput").ap() for n, x in arrays.items()}
    ins["w"] = {n[2:]: ins.pop(n) for n in [n for n in ins if n.startswith("w_")]}
    outs = {n: nc.dram_tensor(n, shape, F32, kind="ExternalOutput").ap() for n, shape in _OUTS.items()}
    build(nc, ins, outs)
    got = _run(nc, [arrays], core_ids=[0]).results[0]
    back = np.argsort(_channels())
    return (
        got["o_prompt"][None], got["o_sample"][:, None],
        got["o_pssd"].transpose(0, 2, 1).reshape(1, 1, HEADS, HEAD, P),
        got["o_pconv"].transpose(3, 1, 2, 0).reshape(HIST, -1)[:, back][None, None],
        got["o_pgla"][None, None],
        got["o_sssd"].transpose(2, 0, 3, 1).reshape(1, NSAMP, HEADS, HEAD, P),
        got["o_sconv"].transpose(4, 3, 1, 2, 0).reshape(NSAMP, HIST, -1)[:, :, back][None],
        got["o_sgla"].transpose(2, 0, 1, 3)[None])
```
